# Optimizing a Trainium2 kernel written in Bass

```python
import jax, jax.numpy as jnp
from jax import lax
import numpy as np
import math

D_MODEL = 1024
BATCH = 1
SEQ = 256
DEPTH = 4

N_MIXERS = 3
HEAD_DIM = 64
N_HEADS = 12
MIX_WIDTH = N_HEADS * HEAD_DIM
N_MEM = 256
N_MEM_HEADS = 4
MEM_WIDTH = N_MEM_HEADS * HEAD_DIM
ROPE_DIM = HEAD_DIM // 4
ROPE_THETA = 500000.0
POS_OFFSET_RANGE = 8192
IDX_HEADS = 8
IDX_DIM = 64
TOPK_MAX = 256
QBLOCK_A = 64
DIL_PAIRS = ((128, 1), (512, 4), (2048, 16))
B_GROUP_HEADS = 4
B_V_DIM = MIX_WIDTH // B_GROUP_HEADS
MOBA_BLOCK = 256
MOBA_TOPK = 3
QBLOCK_C = 16
D_FF = -(-8 * D_MODEL // (3 * 256)) * 256
ALPHA = (2 * DEPTH) ** 0.25
BETA = (8 * DEPTH) ** -0.25
LN_EPS = 1e-5

WIDTH_A = 3 * MIX_WIDTH + IDX_HEADS * IDX_DIM + IDX_HEADS + IDX_DIM + MEM_WIDTH
WIDTH_BC = 3 * MIX_WIDTH + MEM_WIDTH


def layer_norm(x, g, b):
    xf = x.astype(jnp.float32)
    mu = jnp.mean(xf, -1, keepdims=True)
    var = jnp.mean(jnp.square(xf - mu), -1, keepdims=True)
    return ((xf - mu) * lax.rsqrt(var + LN_EPS) * g + b).astype(x.dtype)

def split_cols(h, widths):
    cuts = [int(c) for c in np.cumsum(widths)[:-1]]
    return jnp.split(h, cuts, axis=-1)

def rope_tables(positions):
    half = ROPE_DIM // 2
    inv = ROPE_THETA ** (-jnp.arange(half, dtype=jnp.float32) / half)
    ang = positions.astype(jnp.float32)[..., None] * inv
    return jnp.cos(ang)[:, :, None, :], jnp.sin(ang)[:, :, None, :]

def apply_rope(x, cos, sin):
    half = ROPE_DIM // 2
    c, s = cos.astype(x.dtype), sin.astype(x.dtype)
    x1, x2, rest = x[..., :half], x[..., half:ROPE_DIM], x[..., ROPE_DIM:]
    return jnp.concatenate([x1 * c - x2 * s, x2 * c + x1 * s, rest], axis=-1)

def dsa_attention(q, k, v, q_idx, w_idx, k_idx):
    Bsz, S, H, dh = q.shape
    topk = min(TOPK_MAX, S // 4)
    key_pos = jnp.arange(S)
    scale = dh ** -0.5

    def block(i):
        t0 = i * QBLOCK_A
        qpos = t0 + jnp.arange(QBLOCK_A)
        qi = lax.dynamic_slice_in_dim(q_idx, t0, QBLOCK_A, axis=1)
        wi = lax.dynamic_slice_in_dim(w_idx, t0, QBLOCK_A, axis=1)
        dots = jnp.einsum('bqhd,bsd->bqhs', qi, k_idx).astype(jnp.float32)
        score = jnp.einsum('bqhs,bqh->bqs', jax.nn.relu(dots), wi.astype(jnp.float32))
        causal = key_pos[None, :] <= qpos[:, None]
        score = jnp.where(causal[None], score, -jnp.inf)
        _, sel = lax.top_k(score, topk)
        valid = sel <= qpos[None, :, None]
        ks = jax.vmap(lambda kb, ib: kb[ib])(k, sel)
        vs = jax.vmap(lambda vb, ib: vb[ib])(v, sel)
        qb = lax.dynamic_slice_in_dim(q, t0, QBLOCK_A, axis=1)
        logits = jnp.einsum('bqhd,bqkhd->bhqk', qb, ks).astype(jnp.float32) * scale
        logits = jnp.where(valid[:, None], logits, -jnp.inf)
        p = jax.nn.softmax(logits, axis=-1).astype(v.dtype)
        return jnp.einsum('bhqk,bqkhd->bqhd', p, vs)

    out = lax.map(block, jnp.arange(S // QBLOCK_A))
    return out.transpose(1, 0, 2, 3, 4).reshape(Bsz, S, H, dh)

def dilated_group(q, k, v, window, dilation):
    Bsz, S, G, dh = q.shape
    dv = v.shape[-1]
    n = window // dilation
    L = S // dilation
    nb = -(-L // n)
    Lp = nb * n

    def to_sub(a):
        a = a.reshape(Bsz, L, dilation, G, a.shape[-1]).transpose(0, 2, 1, 3, 4)
        a = jnp.pad(a, ((0, 0), (0, 0), (0, Lp - L), (0, 0), (0, 0)))
        return a.reshape(Bsz, dilation, nb, n, G, a.shape[-1])

    qs, ks, vs = to_sub(q), to_sub(k), to_sub(v)
    shift = ((0, 0), (0, 0), (1, 0), (0, 0), (0, 0), (0, 0))
    kk = jnp.concatenate([jnp.pad(ks[:, :, :-1], shift), ks], axis=3)
    vv = jnp.concatenate([jnp.pad(vs[:, :, :-1], shift), vs], axis=3)
    qi = jnp.arange(n)[:, None] + n
    ki = jnp.arange(2 * n)[None, :]
    dist = qi - ki
    ksub = jnp.arange(nb)[:, None, None] * n + ki[None] - n
    mask = ((dist >= 0) & (dist <= n))[None] & (ksub >= 0)
    logits = jnp.einsum('brnqgd,brnkgd->brngqk', qs, kk).astype(jnp.float32) * (dh ** -0.5)
    logits = jnp.where(mask[None, None, :, None], logits, -jnp.inf)
    lse = jax.nn.logsumexp(logits, axis=-1)
    p = jnp.exp(logits - lse[..., None]).astype(v.dtype)
    out = jnp.einsum('brngqk,brnkgd->brnqgd', p, vv)
    out = out.reshape(Bsz, dilation, Lp, G, dv)[:, :, :L]
    out = out.transpose(0, 2, 1, 3, 4).reshape(Bsz, S, G, dv)
    lse = lse.transpose(0, 1, 2, 4, 3).reshape(Bsz, dilation, Lp, G)[:, :, :L]
    lse = lse.transpose(0, 2, 1, 3).reshape(Bsz, S, G)
    return out, lse

def dilated_attention(q, k, v):
    outs, lses = [], []
    for g, (window, dilation) in enumerate(DIL_PAIRS):
        hs = slice(g * B_GROUP_HEADS, (g + 1) * B_GROUP_HEADS)
        o, l = dilated_group(q[:, :, hs], k[:, :, hs], v, window, dilation)
        outs.append(o)
        lses.append(l)
    wts = jax.nn.softmax(jnp.stack(lses, 0), axis=0).astype(v.dtype)
    return jnp.einsum('gbsh,gbshd->bshd', wts, jnp.stack(outs, 0))

def moba_attention(q, k, v):
    Bsz, S, H, dh = q.shape
    nblk = -(-S // MOBA_BLOCK)
    Sp = nblk * MOBA_BLOCK
    pad = lambda a: jnp.pad(a, ((0, 0), (0, Sp - S), (0, 0), (0, 0)))
    qp = pad(q)
    kbt = pad(k).reshape(Bsz, nblk, MOBA_BLOCK, H, dh).transpose(0, 3, 1, 2, 4)
    vbt = pad(v).reshape(Bsz, nblk, MOBA_BLOCK, H, dh).transpose(0, 3, 1, 2, 4)
    kmean = jnp.mean(kbt.astype(jnp.float32), axis=3)
    ksel = min(MOBA_TOPK, nblk)
    scale = dh ** -0.5
    bidx = jnp.arange(Bsz)[:, None, None, None]
    hidx = jnp.arange(H)[None, :, None, None]

    def block(i):
        t0 = i * QBLOCK_C
        own = t0 // MOBA_BLOCK
        qpos = t0 + jnp.arange(QBLOCK_C)
        qh = lax.dynamic_slice_in_dim(qp, t0, QBLOCK_C, axis=1).transpose(0, 2, 1, 3)
        gate = jnp.einsum('bhqd,bhnd->bhqn', qh.astype(jnp.float32), kmean)
        gate = jnp.where(jnp.arange(nblk) < own, gate, -jnp.inf)
        _, sel = lax.top_k(gate, ksel)
        valid = jnp.repeat(jnp.arange(ksel) < own, MOBA_BLOCK)
        kg = kbt[bidx, hidx, sel]
        vg = vbt[bidx, hidx, sel]
        ko = lax.dynamic_index_in_dim(kbt, own, axis=2, keepdims=False)
        vo = lax.dynamic_index_in_dim(vbt, own, axis=2, keepdims=False)
        kpos = own * MOBA_BLOCK + jnp.arange(MOBA_BLOCK)
        s_sel = jnp.einsum('bhqd,bhqnkd->bhqnk', qh, kg).astype(jnp.float32)
        s_sel = jnp.where(valid, s_sel.reshape(Bsz, H, QBLOCK_C, ksel * MOBA_BLOCK), -jnp.inf)
        s_own = jnp.einsum('bhqd,bhkd->bhqk', qh, ko).astype(jnp.float32)
        s_own = jnp.where(kpos[None, :] <= qpos[:, None], s_own, -jnp.inf)
        p = jax.nn.softmax(jnp.concatenate([s_sel, s_own], -1) * scale, axis=-1).astype(v.dtype)
        p_sel = p[..., :ksel * MOBA_BLOCK].reshape(Bsz, H, QBLOCK_C, ksel, MOBA_BLOCK)
        o = jnp.einsum('bhqnk,bhqnkd->bhqd', p_sel, vg) + jnp.einsum('bhqk,bhkd->bhqd', p[..., ksel * MOBA_BLOCK:], vo)
        return o.transpose(0, 2, 1, 3)

    out = lax.map(block, jnp.arange(Sp // QBLOCK_C))
    return out.transpose(1, 0, 2, 3, 4).reshape(Bsz, Sp, H, dh)[:, :S]

def memory_attention(q, mk, mv):
    logits = jnp.einsum('bshd,bnhd->bhsn', q, mk).astype(jnp.float32) * (HEAD_DIM ** -0.5)
    p = jax.nn.softmax(logits, axis=-1).astype(mv.dtype)
    return jnp.einsum('bhsn,bnhd->bshd', p, mv)

def swiglu(x, w_gate_up, w_down):
    g, u = jnp.split(x @ w_gate_up, 2, axis=-1)
    return (jax.nn.silu(g) * u) @ w_down

def first_inputs(seed: int = 0) -> dict:
    key = jax.random.key(seed)
    ks = jax.random.split(key, 18)
    n_a, n_b, n_c = (DEPTH + 2) // 3, (DEPTH + 1) // 3, DEPTH // 3
    nrm = lambda k, shape, s: jax.random.normal(k, shape, jnp.float32) * s
    gain = lambda k, shape: 1.0 + nrm(k, shape, 0.02)
    offs = jax.random.randint(ks[2], (BATCH, 1), 0, POS_OFFSET_RANGE, dtype=jnp.int32)
    positions = offs + jnp.arange(SEQ, dtype=jnp.int32)[None, :]
    return {
        'x': nrm(ks[0], (BATCH, SEQ, D_MODEL), 1.0),
        'mem': nrm(ks[1], (BATCH, N_MEM, D_MODEL), 1.0),
        'positions': positions,
        'mem_ln_g': gain(ks[3], (D_MODEL,)),
        'mem_ln_b': nrm(ks[4], (D_MODEL,), 0.02),
        'w_in_a': nrm(ks[5], (n_a, D_MODEL, WIDTH_A), D_MODEL ** -0.5),
        'idx_kn_g': gain(ks[6], (n_a, IDX_DIM)),
        'idx_kn_b': nrm(ks[7], (n_a, IDX_DIM), 0.02),
        'w_in_b': nrm(ks[8], (n_b, D_MODEL, WIDTH_BC), D_MODEL ** -0.5),
        'w_in_c': nrm(ks[9], (n_c, D_MODEL, WIDTH_BC), D_MODEL ** -0.5),
        'w_mem_kv': nrm(ks[10], (DEPTH, D_MODEL, 2 * MEM_WIDTH), D_MODEL ** -0.5),
        'w_out': nrm(ks[11], (DEPTH, MIX_WIDTH + MEM_WIDTH, D_MODEL), BETA * (MIX_WIDTH + MEM_WIDTH) ** -0.5),
        'ln1_g': gain(ks[12], (DEPTH, D_MODEL)),
        'ln1_b': nrm(ks[13], (DEPTH, D_MODEL), 0.02),
        'w_gate_up': nrm(ks[14], (DEPTH, D_MODEL, 2 * D_FF), D_MODEL ** -0.5),
        'w_down': nrm(ks[15], (DEPTH, D_FF, D_MODEL), BETA * D_FF ** -0.5),
        'ln2_g': gain(ks[16], (DEPTH, D_MODEL)),
        'ln2_b': nrm(ks[17], (DEPTH, D_MODEL), 0.02),
    }

def first_block(x, mem, positions, mem_ln_g, mem_ln_b, w_in_a, idx_kn_g, idx_kn_b, w_in_b, w_in_c,
              w_mem_kv, w_out, ln1_g, ln1_b, w_gate_up, w_down, ln2_g, ln2_b):
    Bsz, S, _ = x.shape
    cos, sin = rope_tables(positions)
    mem_n = layer_norm(mem, mem_ln_g, mem_ln_b)
    heads = lambda a, h, d: a.reshape(Bsz, S, h, d)
    for i in range(DEPTH):
        kind, j = i % N_MIXERS, i // N_MIXERS
        if kind == 0:
            q, k, v, qi, wi, ki, qm = split_cols(
                x @ w_in_a[j],
                (MIX_WIDTH, MIX_WIDTH, MIX_WIDTH, IDX_HEADS * IDX_DIM, IDX_HEADS, IDX_DIM, MEM_WIDTH))
            q = apply_rope(heads(q, N_HEADS, HEAD_DIM), cos, sin)
            k = apply_rope(heads(k, N_HEADS, HEAD_DIM), cos, sin)
            qi = apply_rope(heads(qi, IDX_HEADS, IDX_DIM), cos, sin)
            ki = apply_rope(layer_norm(ki, idx_kn_g[j], idx_kn_b[j])[:, :, None, :], cos, sin)[:, :, 0]
            wi = wi * (IDX_HEADS * IDX_DIM) ** -0.5
            mix = dsa_attention(q, k, heads(v, N_HEADS, HEAD_DIM), qi, wi, ki)
        elif kind == 1:
            q, k, v, qm = split_cols(x @ w_in_b[j], (MIX_WIDTH, MIX_WIDTH, MIX_WIDTH, MEM_WIDTH))
            q = apply_rope(heads(q, N_HEADS, HEAD_DIM), cos, sin)
            k = apply_rope(heads(k, N_HEADS, HEAD_DIM), cos, sin)
            mix = dilated_attention(q, k, heads(v, B_GROUP_HEADS, B_V_DIM))
        else:
            q, k, v, qm = split_cols(x @ w_in_c[j], (MIX_WIDTH, MIX_WIDTH, MIX_WIDTH, MEM_WIDTH))
            q = apply_rope(heads(q, N_HEADS, HEAD_DIM), cos, sin)
            k = apply_rope(heads(k, N_HEADS, HEAD_DIM), cos, sin)
            mix = moba_attention(q, k, heads(v, N_HEADS, HEAD_DIM))
        mk, mv = jnp.split(mem_n @ w_mem_kv[i], 2, axis=-1)
        mo = memory_attention(heads(qm, N_MEM_HEADS, HEAD_DIM),
                              mk.reshape(Bsz, N_MEM, N_MEM_HEADS, HEAD_DIM),
                              mv.reshape(Bsz, N_MEM, N_MEM_HEADS, HEAD_DIM))
        mixed = jnp.concatenate([mix.reshape(Bsz, S, MIX_WIDTH), mo.reshape(Bsz, S, MEM_WIDTH)], -1) @ w_out[i]
        x = layer_norm(ALPHA * x + mixed, ln1_g[i], ln1_b[i])
        x = layer_norm(ALPHA * x + swiglu(x, w_gate_up[i], w_down[i]), ln2_g[i], ln2_b[i])
    return x


DEPTH_2 = 2

PLE_DIM = 256
DA_HEADS = 4
DA_V = 2 * HEAD_DIM
DA_QK = DA_HEADS * 2 * HEAD_DIM
DA_WIDTH = DA_HEADS * DA_V
MLA_HEADS = 8
MLA_NOPE = 64
MLA_ROPE = 32
MLA_V = 64
MLA_Q_RANK = 256
MLA_KV_RANK = 128
MLA_WIDTH = MLA_HEADS * MLA_V
SW_HEADS = 8
SW_KV_HEADS = 2
SW_GROUP = SW_HEADS // SW_KV_HEADS
SW_WINDOW = 128
SW_WIDTH = SW_HEADS * HEAD_DIM
N_BRANCHES = 3
REL_BUCKETS = 32
REL_MAX_DIST = 128
BIAS_HEADS = DA_HEADS + SW_HEADS
Q_BLOCK = 128
ROPE_THETA_2 = 10000.0
EPS = 1e-6
NEG = -1e30

IN_SIZES = (DA_QK, DA_QK, DA_WIDTH, DA_WIDTH,
            MLA_Q_RANK, MLA_KV_RANK, MLA_ROPE, MLA_WIDTH,
            SW_HEADS * HEAD_DIM, SW_KV_HEADS * HEAD_DIM, SW_KV_HEADS * HEAD_DIM, SW_WIDTH,
            N_BRANCHES * D_MODEL)
IN_TOTAL = sum(IN_SIZES)


def rms_norm(x, w):
    xf = x.astype(jnp.float32)
    y = xf * lax.rsqrt(jnp.mean(xf * xf, axis=-1, keepdims=True) + EPS)
    return (y * w.astype(jnp.float32)).astype(x.dtype)

def rope(x, positions):
    half = x.shape[-1] // 2
    inv_freq = ROPE_THETA_2 ** (-jnp.arange(half, dtype=jnp.float32) / half)
    ang = positions.astype(jnp.float32)[..., None] * inv_freq
    ang = ang.reshape(ang.shape[:2] + (1,) * (x.ndim - 3) + (half,))
    cos, sin = jnp.cos(ang), jnp.sin(ang)
    xf = x.astype(jnp.float32)
    x1, x2 = xf[..., :half], xf[..., half:]
    return jnp.concatenate([x1 * cos - x2 * sin, x2 * cos + x1 * sin], axis=-1).astype(x.dtype)

def t5_bucket(rel):
    n = jnp.maximum(rel, 0)
    max_exact = REL_BUCKETS // 2
    nf = jnp.maximum(n, 1).astype(jnp.float32)
    large = max_exact + (jnp.log(nf / max_exact) / math.log(REL_MAX_DIST / max_exact)
                         * (REL_BUCKETS - max_exact)).astype(jnp.int32)
    large = jnp.minimum(large, REL_BUCKETS - 1)
    return jnp.where(n < max_exact, n, large)

def sweep_query_blocks(block_fn, n_blocks):
    out = lax.map(block_fn, jnp.arange(n_blocks))
    out = jnp.moveaxis(out, 0, 1)
    return out.reshape((out.shape[0], n_blocks * Q_BLOCK) + out.shape[3:])

def diff_attention(q, k, v, lam, rel_table):
    S = q.shape[1]
    scale = HEAD_DIM ** -0.5
    kf = k.astype(jnp.float32)
    table = rel_table.astype(jnp.float32)
    k_idx = jnp.arange(S)

    def block(i):
        q0 = i * Q_BLOCK
        qb = lax.dynamic_slice_in_dim(q, q0, Q_BLOCK, axis=1).astype(jnp.float32)
        s = jnp.einsum('bqhmd,bkhmd->bhmqk', qb, kf) * scale
        rel = (q0 + jnp.arange(Q_BLOCK))[:, None] - k_idx[None, :]
        bias = jnp.moveaxis(table[t5_bucket(rel)][..., :DA_HEADS], -1, 0)
        s = jnp.where(rel >= 0, s + bias[None, :, None], NEG)
        pm = jax.nn.softmax(s, axis=-1)
        w = pm[:, :, 0] - lam * pm[:, :, 1]
        return jnp.einsum('bhqk,bkhe->bqhe', w.astype(v.dtype), v)

    return sweep_query_blocks(block, S // Q_BLOCK)

def mla_attention(q_nope, q_rope, k_nope, k_rope, v):
    S = q_nope.shape[1]
    scale = (MLA_NOPE + MLA_ROPE) ** -0.5
    kn = k_nope.astype(jnp.float32)
    kr = k_rope.astype(jnp.float32)
    k_idx = jnp.arange(S)

    def block(i):
        q0 = i * Q_BLOCK
        qn = lax.dynamic_slice_in_dim(q_nope, q0, Q_BLOCK, axis=1).astype(jnp.float32)
        qr = lax.dynamic_slice_in_dim(q_rope, q0, Q_BLOCK, axis=1).astype(jnp.float32)
        s = (jnp.einsum('bqhd,bkhd->bhqk', qn, kn)
             + jnp.einsum('bqhr,bkr->bhqk', qr, kr)) * scale
        rel = (q0 + jnp.arange(Q_BLOCK))[:, None] - k_idx[None, :]
        s = jnp.where(rel >= 0, s, NEG)
        pm = jax.nn.softmax(s, axis=-1)
        return jnp.einsum('bhqk,bkhd->bqhd', pm.astype(v.dtype), v)

    return sweep_query_blocks(block, S // Q_BLOCK)

def sliding_window_attention(q, k, v, sinks, rel_table):
    B, S = q.shape[:2]
    nb = S // Q_BLOCK
    scale = HEAD_DIM ** -0.5
    qb = q.reshape(B, nb, Q_BLOCK, SW_KV_HEADS, SW_GROUP, HEAD_DIM).astype(jnp.float32)

    def band(t):
        tp = jnp.pad(t, ((0, 0), (Q_BLOCK, 0), (0, 0), (0, 0)))
        tp = tp.reshape(B, nb + 1, Q_BLOCK, SW_KV_HEADS, HEAD_DIM)
        return jnp.concatenate([tp[:, :-1], tp[:, 1:]], axis=2)

    kb = band(k).astype(jnp.float32)
    vb = band(v)
    s = jnp.einsum('bnqhgd,bnkhd->bnhgqk', qb, kb) * scale
    qi = jnp.arange(Q_BLOCK)
    kj = jnp.arange(2 * Q_BLOCK)
    rel = Q_BLOCK + qi[:, None] - kj[None, :]
    bias = jnp.moveaxis(rel_table.astype(jnp.float32)[t5_bucket(rel)][..., DA_HEADS:], -1, 0)
    bias = bias.reshape(SW_KV_HEADS, SW_GROUP, Q_BLOCK, 2 * Q_BLOCK)
    in_window = (rel >= 0) & (rel < SW_WINDOW)
    key_valid = (jnp.arange(nb)[:, None] * Q_BLOCK + kj[None, :] - Q_BLOCK) >= 0
    mask = in_window[None] & key_valid[:, None, :]
    s = jnp.where(mask[None, :, None, None], s + bias, NEG)
    sink = jnp.broadcast_to(sinks.astype(jnp.float32).reshape(SW_KV_HEADS, SW_GROUP, 1, 1),
                            s.shape[:-1] + (1,))
    pm = jax.nn.softmax(jnp.concatenate([s, sink], axis=-1), axis=-1)[..., :-1]
    o = jnp.einsum('bnhgqk,bnkhd->bnqhgd', pm.astype(v.dtype), vb)
    return o.reshape(B, S, SW_WIDTH)

def second_inputs(seed: int = 0) -> dict:
    key = jax.random.key(seed)
    ks = jax.random.split(key, 24)
    f32 = jnp.float32

    def nrm(k, shape, scale):
        return jax.random.normal(k, shape, f32) * scale

    def gain(k, shape):
        return 1.0 + 0.05 * jax.random.normal(k, shape, f32)

    start = jax.random.randint(ks[2], (BATCH, 1), 0, 4096, dtype=jnp.int32)
    positions = start + jnp.arange(SEQ, dtype=jnp.int32)[None, :]
    return {
        "x": nrm(ks[0], (BATCH, SEQ, D_MODEL), 1.0),
        "p": nrm(ks[1], (DEPTH_2, BATCH, SEQ, PLE_DIM), 1.0),
        "positions": positions,
        "rel_bias": nrm(ks[3], (REL_BUCKETS, BIAS_HEADS), 0.3),
        "norm_pre": gain(ks[4], (DEPTH_2, D_MODEL)),
        "norm_post": gain(ks[5], (DEPTH_2, D_MODEL)),
        "w_in": nrm(ks[6], (DEPTH_2, D_MODEL, IN_TOTAL), D_MODEL ** -0.5),
        "da_lambda": nrm(ks[7], (DEPTH_2, 4, HEAD_DIM), 0.1),
        "da_subln": gain(ks[8], (DEPTH_2, DA_V)),
        "mla_q_norm": gain(ks[9], (DEPTH_2, MLA_Q_RANK)),
        "mla_w_qb": nrm(ks[10], (DEPTH_2, MLA_Q_RANK, MLA_HEADS * (MLA_NOPE + MLA_ROPE)), MLA_Q_RANK ** -0.5),
        "mla_kv_norm": gain(ks[11], (DEPTH_2, MLA_KV_RANK)),
        "mla_w_kvb": nrm(ks[12], (DEPTH_2, MLA_KV_RANK, MLA_HEADS * (MLA_NOPE + MLA_V)), MLA_KV_RANK ** -0.5),
        "sw_sinks": nrm(ks[13], (DEPTH_2, SW_HEADS), 0.5),
        "w_br_a": nrm(ks[14], (DEPTH_2, DA_WIDTH, D_MODEL), DA_WIDTH ** -0.5),
        "w_br_b": nrm(ks[15], (DEPTH_2, MLA_WIDTH, D_MODEL), MLA_WIDTH ** -0.5),
        "w_br_c": nrm(ks[16], (DEPTH_2, SW_WIDTH, D_MODEL), SW_WIDTH ** -0.5),
        "w_out": nrm(ks[17], (DEPTH_2, D_MODEL, D_MODEL), D_MODEL ** -0.5),
        "w_ple_gate": nrm(ks[18], (DEPTH_2, D_MODEL, D_MODEL), D_MODEL ** -0.5),
        "w_ple_proj": nrm(ks[19], (DEPTH_2, PLE_DIM, D_MODEL), PLE_DIM ** -0.5),
    }

def second_block(x, p, positions, rel_bias, norm_pre, norm_post, w_in, da_lambda, da_subln,
              mla_q_norm, mla_w_qb, mla_kv_norm, mla_w_kvb, sw_sinks,
              w_br_a, w_br_b, w_br_c, w_out, w_ple_gate, w_ple_proj):
    B, S, _ = x.shape
    split_points = tuple(int(c) for c in np.cumsum(IN_SIZES)[:-1])
    for l in range(DEPTH_2):
        h = rms_norm(x, norm_pre[l])
        u = h @ w_in[l]
        (a_q, a_k, a_v, a_z, b_q, b_kv, b_kr, b_z,
         c_q, c_k, c_v, c_z, g) = jnp.split(u, split_points, axis=-1)

        lam_init = 0.8 - 0.6 * math.exp(-0.3 * l)
        lf = da_lambda[l].astype(jnp.float32)
        lam = jnp.exp(jnp.sum(lf[0] * lf[1])) - jnp.exp(jnp.sum(lf[2] * lf[3])) + lam_init
        oa = diff_attention(a_q.reshape(B, S, DA_HEADS, 2, HEAD_DIM),
                            a_k.reshape(B, S, DA_HEADS, 2, HEAD_DIM),
                            a_v.reshape(B, S, DA_HEADS, DA_V), lam, rel_bias)
        oa = (rms_norm(oa, da_subln[l]) * (1.0 - lam_init)).reshape(B, S, DA_WIDTH)

        qm = (rms_norm(b_q, mla_q_norm[l]) @ mla_w_qb[l]).reshape(B, S, MLA_HEADS, MLA_NOPE + MLA_ROPE)
        q_nope, q_rope = qm[..., :MLA_NOPE], rope(qm[..., MLA_NOPE:], positions)
        kvm = (rms_norm(b_kv, mla_kv_norm[l]) @ mla_w_kvb[l]).reshape(B, S, MLA_HEADS, MLA_NOPE + MLA_V)
        k_nope, v_m = kvm[..., :MLA_NOPE], kvm[..., MLA_NOPE:]
        k_rope = rope(b_kr, positions)
        ob = mla_attention(q_nope, q_rope, k_nope, k_rope, v_m).reshape(B, S, MLA_WIDTH)

        oc = sliding_window_attention(c_q.reshape(B, S, SW_HEADS, HEAD_DIM),
                                      c_k.reshape(B, S, SW_KV_HEADS, HEAD_DIM),
                                      c_v.reshape(B, S, SW_KV_HEADS, HEAD_DIM),
                                      sw_sinks[l], rel_bias)

        gates = jax.nn.sigmoid(g).reshape(B, S, N_BRANCHES, D_MODEL)
        y = (gates[:, :, 0] * ((oa * jax.nn.silu(a_z)) @ w_br_a[l])
             + gates[:, :, 1] * ((ob * jax.nn.silu(b_z)) @ w_br_b[l])
             + gates[:, :, 2] * ((oc * jax.nn.silu(c_z)) @ w_br_c[l]))
        x = x + rms_norm(y @ w_out[l], norm_post[l])

        x = x + jax.nn.sigmoid(x @ w_ple_gate[l]) * (p[l] @ w_ple_proj[l])
    return x


def setup_inputs(seed=0):
    out = dict(first_inputs(seed))
    for name, value in second_inputs(seed + 1).items():
        if name != "x":
            out[name + "_2"] = value
    return out


def reference(
    x, mem, positions, mem_ln_g, mem_ln_b, w_in_a, idx_kn_g, idx_kn_b, w_in_b, w_in_c, w_mem_kv,
    w_out, ln1_g, ln1_b, w_gate_up, w_down, ln2_g, ln2_b, p_2, positions_2, rel_bias_2,
    norm_pre_2, norm_post_2, w_in_2, da_lambda_2, da_subln_2, mla_q_norm_2, mla_w_qb_2,
    mla_kv_norm_2, mla_w_kvb_2, sw_sinks_2, w_br_a_2, w_br_b_2, w_br_c_2, w_out_2, w_ple_gate_2,
    w_ple_proj_2,
):
    x = first_block(
        x, mem, positions, mem_ln_g, mem_ln_b, w_in_a, idx_kn_g, idx_kn_b, w_in_b, w_in_c,
        w_mem_kv, w_out, ln1_g, ln1_b, w_gate_up, w_down, ln2_g, ln2_b,
    )
    return second_block(
        x, p_2, positions_2, rel_bias_2, norm_pre_2, norm_post_2, w_in_2, da_lambda_2,
        da_subln_2, mla_q_norm_2, mla_w_qb_2, mla_kv_norm_2, mla_w_kvb_2, sw_sinks_2, w_br_a_2,
        w_br_b_2, w_br_c_2, w_out_2, w_ple_gate_2, w_ple_proj_2,
    )


_drawn_inputs = setup_inputs


def setup_inputs(seed=0):
    import zlib

    import numpy as np

    out = dict(_drawn_inputs(seed))
    spreads = {}
    factors = {'mem_ln_g': 8.0,
     'idx_kn_g': 5.959,
     'idx_kn_b': 6.708,
     'mla_q_norm_2': 5.75,
     'mla_kv_norm_2': 2.772,
     'sw_sinks_2': 5.228}
    for name, (base, spread) in spreads.items():
        noise = np.random.default_rng([zlib.crc32(name.encode()), seed]).standard_normal(out[name].shape)
        drawn = base * np.exp(spread * noise) if base else spread * noise
        out[name] = __import__('jax').numpy.asarray(drawn.astype(out[name].dtype))
    for name, factor in factors.items():
        out[name] = (out[name] * factor).astype(out[name].dtype)
    return out
```

```python
import math
from contextlib import ExitStack

import numpy as np

import concourse.bass as bass
from concourse import mybir

F32 = mybir.dt.float32
F32R = mybir.dt.float32r
I32 = mybir.dt.int32
ALU = mybir.AluOpType
ACT = mybir.ActivationFunctionType
AX = mybir.AxisListType

P = 128
T = 2
N = T * P
D = 1024
DEPTH = 4
HD = 64
MIX = 768
HEADS = MIX // HD
MEMW = 256
IDXH = 8
TOPK = min(256, N // 4)
FF = 2816
ALPHA = (2 * DEPTH) ** 0.25
LN_EPS = 1e-5
RMS_EPS = 1e-6
DEPTH_2 = 2
DA_H, MLA_H, SW_H = 4, 8, 8
MLA_K = 96
BIAS_HEADS = DA_H + SW_H
REL_BUCKETS = 32
NEG = -1e30
SENTINEL = -3e38
SCALE = HD ** -0.5
MLA_SCALE = MLA_K ** -0.5
CAUSAL = 384
FULL = 512
REL_ROW = 384

CHUNK = 512
UK = 2
RAW = 6
SPLIT = 6
AHEAD = SPLIT - 1

TWO_PI_1 = 6.28125
TWO_PI_2 = float(np.float32(0.0019350051879882812))
TWO_PI_3 = 2 * math.pi - TWO_PI_1 - TWO_PI_2
ROUND = 12582912.0
PI_INSIDE = 3.1415925

C_AQ, C_AZ, C_BQ, C_BZ, C_CQ, C_CZ, C_G = 0, 1536, 2048, 2464, 2976, 3744, 4256


def t5_bucket_rows():
    rel = 255 - np.arange(REL_ROW)
    n = np.maximum(rel, 0)
    nf = np.maximum(n, 1).astype(np.float32)
    half = REL_BUCKETS // 2
    large = half + (np.log(nf / np.float32(half)) / np.float32(math.log(128 / half))
                    * np.float32(REL_BUCKETS - half)).astype(np.int32)
    bucket = np.where(n < half, n, np.minimum(large, REL_BUCKETS - 1))
    onehot = ((np.arange(REL_BUCKETS)[:, None] == bucket[None]) & (rel >= 0)[None]).astype(np.float32)
    mask = np.zeros((BIAS_HEADS, REL_ROW), np.float32)
    mask[:, rel < 0] = NEG
    mask[DA_H:, rel >= 128] = NEG
    return onehot, mask


def shape_constants():
    q0, k0 = np.arange(P)[:, None], np.arange(P)[None]
    q1, k1 = P + np.arange(P)[:, None], np.arange(N)[None]

    def mask(keep):
        both = np.concatenate([keep(q0, k0), keep(q1, k1)], 1)
        return np.where(both, 0.0, NEG).astype(np.float32)

    masks = np.stack([
        mask(lambda q, k: k <= q),
        mask(lambda q, k: (k <= q) & (q - k <= 128)),
        mask(lambda q, k: (k <= q) & ((q - k) % 4 == 0)),
        mask(lambda q, k: (k <= q) & ((q - k) % 16 == 0)),
    ], 1)
    inv_1 = np.power(500000.0, (-np.arange(8, dtype=np.float32) / np.float32(8)).astype(np.float64))
    inv_2 = np.power(10000.0, (-np.arange(16, dtype=np.float32) / np.float32(16)).astype(np.float64))
    inv = np.broadcast_to(np.concatenate([inv_1, inv_2]).astype(np.float32), (P, 24))
    onehot, rel_mask = t5_bucket_rows()
    return {
        "c_ident": np.eye(P, dtype=np.float32),
        "c_masks": np.ascontiguousarray(masks),
        "c_inv": np.ascontiguousarray(inv),
        "c_onehot": onehot,
        "c_relmask": rel_mask,
    }


def column_chunks(start, stop):
    return [(c, min(CHUNK, stop - c)) for c in range(start, stop, CHUNK)]


class Phase:

    def __init__(self, kind, layer=None, chunks=None, acts=None, t_need=None, batches=None,
                 steps=None, width=None, maps=None, scale=None, dv=None, flavour=None, mask=None,
                 block=None, stage_need=None, bias_need=None, serial=None, taken=None,
                 heads_out=None, fn=None, n=None, act_taken=None, dve_taken=None, src=None,
                 dst=None, low=None, z=None, mixer=None, gain=None, head=None, heads=None,
                 first=None, steps_before=0, index_before=0):
        self.kind = kind
        self.layer = layer
        self.chunks = chunks
        self.acts = acts
        self.t_need = t_need
        self.batches = batches
        self.steps = steps
        self.width = width
        self.maps = maps
        self.scale = scale
        self.dv = dv
        self.flavour = flavour
        self.mask = mask
        self.block = block
        self.stage_need = stage_need
        self.bias_need = bias_need
        self.serial = serial
        self.taken = taken
        self.heads_out = heads_out
        self.fn = fn
        self.n = n
        self.act_taken = act_taken
        self.dve_taken = dve_taken
        self.src = src
        self.dst = dst
        self.low = low
        self.z = z
        self.mixer = mixer
        self.gain = gain
        self.head = head
        self.heads = heads
        self.first = first
        self.steps_before = steps_before
        self.index_before = index_before


class Batch:

    def __init__(self, b, moves, dst, split, after, hi=0):
        self.b = b
        self.moves = moves
        self.dst = dst
        self.split = split
        self.after = after
        self.hi = hi


class Chunk:

    def __init__(self, c, index, acts, k_tiles, col, width, how, dst, eng, count, act_taken,
                 dve_taken_before, stage_before):
        self.c = c
        self.index = index
        self.acts = acts
        self.k_tiles = k_tiles
        self.col = col
        self.width = width
        self.how = how
        self.dst = dst
        self.eng = eng
        self.count = count
        self.act_taken = act_taken
        self.dve_taken_before = dve_taken_before
        self.stage_before = stage_before
        self.units = []
        self.last = None


class Unit:

    def __init__(self, u, k0, nk, chunk, weight):
        self.u = u
        self.k0 = k0
        self.nk = nk
        self.chunk = chunk
        self.weight = weight
        self.pre = []
        self.gain = None
        self.late_gain = None
        self.t_need = 0


class Step:

    def __init__(self, s, i, q, k, v, out):
        self.s = s
        self.i = i
        self.q = q
        self.k = k
        self.v = v
        self.out = out
        self.tb = []
        self.mixed = 0


class Turn:

    def __init__(self, b, j, blocks):
        self.b = b
        self.j = j
        self.blocks = blocks


class Gain:

    def __init__(self, j, g, b):
        self.j = j
        self.g = g
        self.b = b
        self.stage = None


class Plan:

    def __init__(self):
        self.phases = []
        self.units = []
        self.chunks = []
        self.n_t = 0
        self.n_hi = 0
        self.n_steps = 0
        self.n_stage = 0
        self.n_taken = {"dve": 0, "act": 0}
        self.n_index = 0
        self.n_mixed = 0
        self.n_bias = 0
        self.block = 1

    def add(self, kind, **kw):
        ph = Phase(kind, **kw)
        self.phases.append(ph)
        return ph

    def batch(self, source, moves, dst, split, after):
        b = Batch(self.n_t, moves, dst, split, after)
        self.n_t += 1
        if split:
            self.n_hi += 1
            b.hi = self.n_hi
        return b

    def split_batches(self, source, k0, nk, dst, d0, after):
        out = []
        for k in range(0, nk, 2):
            m = min(2, nk - k)
            moves = [(source, t, (k0 + k + j) * P, P) for j in range(m) for t in range(T)]
            out.append(self.batch(source, moves, (dst, d0 + k, m, P), True, after))
        return out

    def head_batches(self, source, cols, width, dst, d0, after):
        out = []
        for i in range(0, len(cols), 2):
            pair = cols[i:i + 2]
            moves = [(source, t, c, width) for c in pair for t in range(T)]
            out.append(self.batch(source, moves, (dst, d0 + i, len(pair), width), False, after))
        return out

    def linear(self, weight, k_tiles, acts, chunks, before=None, gains=None):
        ph = self.add("linear", chunks=[], acts=acts, t_need=self.n_t, steps_before=self.n_steps,
                      index_before=self.n_index)
        for ci, (col, width, how, dst) in enumerate(chunks):
            eng = "act" if how in ("silu", "sigmoid") else "dve"
            dve_taken_before = self.n_taken["dve"]
            self.n_taken[eng] += 1
            ch = Chunk(len(self.chunks), ci, acts, k_tiles, col, width, how, dst, eng, self.n_taken[eng],
                       self.n_taken["act"], dve_taken_before, self.n_stage)
            self.chunks.append(ch)
            ph.chunks.append(ch)
            for ui, k0 in enumerate(range(0, k_tiles, UK)):
                u = Unit(len(self.units), k0, min(UK, k_tiles - k0), ch, weight)
                if before and (ci, ui) in before:
                    u.pre = before[(ci, ui)]()
                if ci == 0 and ui == 0:
                    u.gain = gains
                u.t_need = self.n_t
                self.units.append(u)
                ch.units.append(u)
            ch.last = ch.units[-1].u
        return ph

    def transpose(self, batches):
        return self.add("transpose", batches=batches)

    def stage(self, fn, **kw):
        self.n_stage += 1
        return self.add("stage", fn=fn, n=self.n_stage, act_taken=self.n_taken["act"],
                        dve_taken=self.n_taken["dve"], steps_before=self.n_steps, **kw)

    def attention(self, steps, width, maps, depth, scale, heads_out, flavour="plain", mask=None):
        ph = self.add("attention", steps=[], width=width, maps=maps, scale=scale, dv=depth,
                      flavour=flavour, mask=mask, block=self.block, index_before=self.n_index,
                      bias_need=self.n_bias, stage_need=self.n_stage, serial=(flavour == "dilated"),
                      t_need=self.n_t, taken=dict(self.n_taken), heads_out=heads_out)
        for i, st in enumerate(steps):
            s = Step(self.n_steps, i, **st)
            self.n_steps += 1
            blocks = 3 if width == CAUSAL else 4
            if flavour in ("dilated", "differential"):
                self.n_mixed += 1
                s.mixed = self.n_mixed
            for j in range(len(s.v)):
                s.tb.append(Turn(self.n_t, j, blocks))
                self.n_t += 1
            ph.steps.append(s)
        return ph


def plan(w):
    p = Plan()
    gains = iter(range(100))

    def ln_gain(name_g, name_b, row):
        return Gain(next(gains), (name_g, row), (name_b, row))

    def stage_gain(gain, fn, **kw):
        ph = p.stage(fn, gain=gain, **kw)
        gain.stage = ph.n
        p_gains.append(gain)
        return ph

    p_gains = []
    p.gains = p_gains

    def stage_src():
        return ("stage", p.n_stage)

    g = ln_gain("mem_ln_g", "mem_ln_b", None)
    p.first_gain = g
    stage_gain(g, "mem_norm")
    p.transpose(p.split_batches("tmp", 0, 8, "x", 0, stage_src()))
    for l in range(DEPTH):
        p.linear(w["w_mem_kv"][l], 8, "x", [(0, 512, "mem_kv", l)])
    p.add("save_mem_kv", taken=p.n_taken["dve"])
    p.stage("mem_kv_saved")
    p.transpose(p.split_batches("x", 0, 8, "x", 0, stage_src()))

    for l in range(DEPTH):
        kind, j = l % 3, l // 3
        width = 3144 if kind == 0 else 2560
        qm = 2888 if kind == 0 else 2304
        win = (w["w_in_a"], w["w_in_b"], w["w_in_c"])[kind][j]
        src = ("U", width, 0)
        p.add("load_mem_kv", layer=l, steps_before=p.n_steps)
        p.linear(win, 8, "x", [(c, n, "copy", (src, c)) for c, n in column_chunks(0, width)])
        p.stage("rope_first", src=src, mixer=kind, layer=j)
        if kind == 0:
            p.transpose(p.head_batches(src, [2304 + 128 * i for i in range(4)], P, "QT", 0, stage_src())
                        + p.head_batches("KI", [0], P, "KT", 0, stage_src()))
            p.add("index_scores", t_need=p.n_t, taken=dict(p.n_taken), src=src, first=p.n_index)
            p.n_index += 2 * IDXH
            p.stage("top_k")
        p.transpose(p.head_batches(src, [P * i for i in range(6)], P, "QT", 0, stage_src())
                    + p.head_batches(src, [MIX + P * i for i in range(6)], P, "KT", 0, stage_src()))
        if kind == 1:
            steps = [dict(q=[(2 * g + b // 2, HD * (b % 2), HD) for g in range(3)],
                          k=[(2 * g + b // 2, HD * (b % 2), HD) for g in range(3)],
                          v=[(src, 2 * MIX + 192 * b)], out=192 * b) for b in range(4)]
            p.attention(steps, CAUSAL, 3, 192, SCALE, "tmp", "dilated")
        else:
            steps = [dict(q=[(i, HD * m, HD) for m in range(2)], k=[(i, HD * m, HD) for m in range(2)],
                          v=[(src, 2 * MIX + P * i + HD * m) for m in range(2)], out=P * i) for i in range(6)]
            p.attention(steps, CAUSAL, 2, HD, SCALE, "tmp", "plain", "selected" if kind == 0 else "causal")
        p.transpose(p.head_batches(src, [qm, qm + P], P, "QT", 0, ("out_taken", p.n_steps))
                    + p.head_batches("MKV", [0, P], P, "KT", 0, ("mem_kv_landed", 16 * (l + 1))))
        steps = [dict(q=[(i, HD * m, HD) for m in range(2)], k=[(i, HD * m, HD) for m in range(2)],
                      v=[("MKV", MEMW + P * i + HD * m) for m in range(2)], out=MIX + P * i) for i in range(2)]
        p.attention(steps, FULL, 2, HD, SCALE, "tmp")
        p.transpose(p.split_batches("tmp", 0, 8, "x", 0, ("out_taken", p.n_steps)))
        g = ln_gain("ln1_g", "ln1_b", l)
        p.linear(w["w_out"][l], 8, "x", [(c, n, "residual", c) for c, n in column_chunks(0, D)], gains=g)
        stage_gain(g, "layer_norm")
        p.transpose(p.split_batches("x", 0, 8, "x", 0, stage_src()))
        chunks, before = [], {}
        widths = column_chunks(0, FF)

        def h_batches(i):
            def make():
                return p.split_batches("H", 0, widths[i][1] // P, "h", widths[i][0] // P,
                                       ("acc_taken_dve", first_taken + i + 1))
            return make

        for i, (c, n) in enumerate(widths):
            chunks += [(c, n, "silu", ("G",)), (FF + c, n, "up", i)]
            if i:
                before[(2 * i + 1, 0)] = h_batches(i - 1)
        first_taken = p.n_taken["dve"]
        p.linear(w["w_gate_up"][l], 8, "x", chunks, before)
        g = ln_gain("ln2_g", "ln2_b", l)
        k_last = widths[-1][0] // P
        p.linear(w["w_down"][l], FF // P, "h", [(c, n, "residual", c) for c, n in column_chunks(0, D)],
                 {(0, k_last // UK): h_batches(len(widths) - 1)}, gains=g)
        stage_gain(g, "layer_norm")
        if l < DEPTH - 1:
            p.transpose(p.split_batches("x", 0, 8, "x", 0, stage_src()))

    p.block = 2
    for l in range(DEPTH_2):
        win = w["w_in_2"][l]
        g = ln_gain("norm_pre_2", None, l)
        p.units[-1].late_gain = g
        stage_gain(g, "rms_pre")
        p.transpose(p.split_batches("tmp", 0, 8, "x", 0, stage_src()))

        def branch(weight, gate, first):
            p.transpose(p.split_batches(mixed, 0, 4, "s", 0, stage_src()))
            p.linear(win, 8, "x", [(C_G + D * gate + c, n, "sigmoid", ("tmp", D, c))
                                   for c, n in column_chunks(0, D)])
            p.linear(weight[l], 4, "s", [(c, n, "branch_first" if first else "branch", c)
                                         for c, n in column_chunks(0, D)])

        src = ("U", 2048, 0)
        mixed = src
        p.add("load_bias", head=0, heads=DA_H, steps_before=p.n_steps)
        p.n_bias += 32 + (16 if l == 0 else 0)
        p.linear(win, 8, "x", [(c, n, "copy", (src, c)) for c, n in column_chunks(0, C_AZ)]
                 + [(C_AZ, 512, "silu", (src, C_AZ))])
        p.stage("nothing")
        p.transpose(p.head_batches(src, [P * i for i in range(4)], P, "QT", 0, stage_src())
                    + p.head_batches(src, [512 + P * i for i in range(4)], P, "KT", 0, stage_src()))
        steps = [dict(q=[(i, HD * m, HD) for m in range(2)], k=[(i, HD * m, HD) for m in range(2)],
                      v=[(src, 1024 + P * i)], out=P * i) for i in range(4)]
        p.attention(steps, CAUSAL, 2, P, SCALE, src, "differential", "bias")
        p.phases[-1].layer = l
        p.stage("sub_norm", src=src, layer=l)
        branch(w["w_br_a_2"], 0, True)

        low, qm, kvm = ("U", 928, 0), ("U", 768, 1856), ("U", 1024, 1856 + 1536)
        p.linear(win, 8, "x", [(C_BQ, 416, "copy", (low, 0)), (C_BZ, 512, "silu", (low, 416))])
        p.stage("latent_norm", src=low, layer=l)
        p.transpose(p.split_batches(low, 0, 3, "s", 0, stage_src()))
        p.linear(w["mla_w_qb_2"][l], 2, "s", [(c, n, "copy", (qm, c)) for c, n in column_chunks(0, 768)])
        kv = p.linear(w["mla_w_kvb_2"][l], 1, "s2", [(c, n, "copy", (kvm, c)) for c, n in column_chunks(0, 1024)])
        p.stage("latent_rope_q", src=qm, low=low)
        p.transpose(p.head_batches(qm, [MLA_K * i for i in range(8)], MLA_K, "QT", 0, stage_src()))
        p.stage("latent_keys", src=kvm, low=low, dst=qm, t_need=p.n_t)
        p.transpose(p.head_batches(qm, [MLA_K * i for i in range(8)], MLA_K, "KT", 0, stage_src()))
        steps = [dict(q=[(2 * i + m, 0, MLA_K) for m in range(2)], k=[(2 * i + m, 0, MLA_K) for m in range(2)],
                      v=[(kvm, P * (2 * i + m) + HD) for m in range(2)], out=P * i) for i in range(4)]
        p.attention(steps, CAUSAL, 2, HD, MLA_SCALE, qm, "plain", "causal")
        mixed = qm
        p.stage("gate_mixed", src=qm, z=(low, 416))
        branch(w["w_br_b_2"], 1, False)

        src = ("U", 1280, 0)
        p.add("load_bias", head=DA_H, heads=SW_H, steps_before=p.n_steps)
        p.n_bias += 32
        p.linear(win, 8, "x", [(C_CQ, 512, "copy", (src, 0)), (C_CQ + 512, 256, "copy", (src, 512)),
                               (C_CZ, 512, "silu", (src, 768))])
        p.stage("twice_keys", src=src)
        p.transpose(p.head_batches(src, [P * i for i in range(4)], P, "QT", 0, stage_src())
                    + p.head_batches(("U", 256, 2560), [0, P], P, "KT", 0, stage_src()))
        steps = [dict(q=[(i, HD * m, HD) for m in range(2)], k=[(i // 2, HD * m, HD) for m in range(2)],
                      v=[(src, 640 + HD * (i // 2)) for m in range(2)], out=P * i) for i in range(4)]
        p.attention(steps, CAUSAL, 2, HD, SCALE, src, "sinks", "bias")
        p.phases[-1].layer = l
        mixed = src
        p.stage("gate_mixed", src=src, z=(src, 768))
        branch(w["w_br_c_2"], 2, False)

        p.transpose(p.split_batches("Y", 0, 8, "x", 0, ("acc_taken_dve", p.n_taken["dve"])))
        g = ln_gain("norm_post_2", None, l)
        p.linear(w["w_out_2"][l], 8, "x", [(c, n, "copy", (("tmp", D, 0), c)) for c, n in column_chunks(0, D)],
                 gains=g)
        p.add("load_ple", layer=l)
        stage_gain(g, "rms_post")
        p.transpose(p.split_batches("x", 0, 8, "x", 0, stage_src())
                    + p.split_batches(("U", 256, 0), 0, 2, "s", 0, ("ple_landed", 16 * (l + 1))))
        p.linear(w["w_ple_gate_2"][l], 8, "x", [(c, n, "sigmoid", ("tmp", D, c)) for c, n in column_chunks(0, D)])
        p.linear(w["w_ple_proj_2"][l], 2, "s", [(c, n, "ple", c) for c, n in column_chunks(0, D)])
    return p


def build(nc, a, out):
    p = plan(a)
    rel_rows = nc.dram_tensor("rel_rows", [BIAS_HEADS, P, REL_ROW], F32, kind="Internal").ap()
    mem_kv = nc.dram_tensor("mem_kv", [DEPTH, P, T * 512], F32, kind="Internal").ap()
    gain_list = p.gains

    with ExitStack() as ctx:
        def sb(name, shape, dt=F32):
            return ctx.enter_context(nc.sbuf_tensor(name, shape, dt))

        def sem(name):
            return ctx.enter_context(nc.semaphore(name))

        raw = sb("raw", [P, RAW, UK, CHUNK])
        w_hi = sb("w_hi", [P, SPLIT, UK, CHUNK], F32R)
        w_lo = sb("w_lo", [P, SPLIT, UK, CHUNK], F32R)
        xT_hi = sb("xT_hi", [P, 8, N], F32R)
        xT_lo = sb("xT_lo", [P, 8, N], F32R)
        x = sb("x_rows", [P, T, D])
        tmp = sb("tmp", [P, T * D])
        gain = sb("gain", [P, 2, 2, D])
        ident = sb("ident", [P, P])
        knorm = sb("knorm", [P, 2, 2, HD])
        subln = sb("subln", [P, 2, P])
        qnorm = sb("qnorm", [P, 2, 256])
        kvnorm = sb("kvnorm", [P, 2, P])
        sinks = sb("sinks", [P, 2, SW_H])
        neg_sinks = sb("neg_sinks", [P, 2, SW_H])
        neg_lam = sb("neg_lam", [P, 2])
        trig = sb("trig", [P, 2, T, 24])
        stats = sb("stats", [P, T, 2, 6])
        small = sb("small", [P, 10, 16])
        neg_max = sb("neg_max", [P, 2, 4])
        sums = sb("sums", [P, 2, 4])
        sink_exp = sb("sink_exp", [P, 2, 4])
        recips = sb("recips", [P, 2, 4])

        att = ExitStack()
        with att:
            def sba(name, shape, dt=F32):
                return att.enter_context(nc.sbuf_tensor(name, shape, dt))
            U = sba("U", [P, 6304])
            QT = sba("QT", [P, 8, N])
            KT = sba("KT", [P, 8, N])
            L = sba("L", [P, 2048])
            PT = sba("PT", [P, 4, 512])
        ffn = ExitStack()
        with ffn:
            hT_hi = ffn.enter_context(nc.sbuf_tensor("hT_hi", [P, FF // P, N], F32R))
            hT_lo = ffn.enter_context(nc.sbuf_tensor("hT_lo", [P, FF // P, N], F32R))
            G = ffn.enter_context(nc.sbuf_tensor("G", [P, T, CHUNK], F32))
            H = ffn.enter_context(nc.sbuf_tensor("H", [P, T, CHUNK], F32))
        ctx.enter_context(nc.sbuf_tensor("attention_or_ffn", [P, 6304 + 4096 + 2048 + 2048], F32))
        first = ExitStack()
        with first:
            masks = first.enter_context(nc.sbuf_tensor("masks", [P, 4, CAUSAL], F32))
            selected = first.enter_context(nc.sbuf_tensor("selected", [P, CAUSAL], F32))
            scores = first.enter_context(nc.sbuf_tensor("scores", [P, CAUSAL], F32))
            MKV = first.enter_context(nc.sbuf_tensor("MKV", [P, T * 512], F32))
            KI = first.enter_context(nc.sbuf_tensor("KI", [P, T * P], F32))
        second = ExitStack()
        with second:
            causal_2 = second.enter_context(nc.sbuf_tensor("causal_2", [P, CAUSAL], F32))
            bias = second.enter_context(nc.sbuf_tensor("bias", [P, SW_H, CAUSAL], F32))
        ctx.enter_context(nc.sbuf_tensor("first_or_second", [P, 4 * CAUSAL + 2 * CAUSAL + T * 512 + T * P], F32))
        sT_hi = ctx.enter_context(nc.sbuf_tensor("sT_hi", [P, 4, N], F32R))
        sT_lo = ctx.enter_context(nc.sbuf_tensor("sT_lo", [P, 4, N], F32R))

        acc = ctx.enter_context(nc.psum_tensor("acc", [P, 4, 512], F32))
        tps = ctx.enter_context(nc.psum_tensor("tps", [P, 2, 512], F32))
        ops = ctx.enter_context(nc.psum_tensor("ops", [P, 2, 512], F32))

        S = {n: sem(n) for n in (
            "prologue_landed", "x_landed", "mem_landed", "lambda_terms", "lambda_exp", "angles",
            "trig_done", "rel_ready", "rel_rows_made", "rel_rows_saved", "mem_kv_saved",
            "mem_kv_landed", "bias_landed", "ple_landed", "out_landed", "hi_ready", "lo_ready",
            "unit_used", "acc_taken_dve", "acc_taken_act", "t_ready", "t_hi", "t_taken", "stage",
            "scores_ready", "logits_ready", "max_ready", "probs_ready", "mixed_ready", "pv_ready",
            "out_taken", "dve_chain", "act_chain", "index_ready", "index_relu", "index_added")}
        unit_landed = [sem(f"unit_landed{i}") for i in range(RAW)]
        gain_landed = [sem(f"gain_landed{i}") for i in range(2)]

        block = ctx.enter_context(nc.Block())

        def rows(src):
            if src == "x":
                return x[:]
            if src == "tmp":
                return tmp[:].rearrange("p (t c) -> p t c", t=T)
            if src == "H":
                return H[:]
            if src == "Y":
                return gain[:, :, 1, :]
            if src == "KI":
                return KI[:].rearrange("p (t c) -> p t c", t=T)
            if src == "MKV":
                return MKV[:].rearrange("p (t c) -> p t c", t=T)
            name, cols, off = src
            buf = {"U": U, "tmp": tmp}[name]
            if name == "tmp":
                off = 0
            return buf[:, off:off + T * cols].rearrange("p (t c) -> p t c", t=T)

        def act_split(name):
            return {"x": (xT_hi, xT_lo, 0), "h": (hT_hi, hT_lo, 0), "s": (sT_hi, sT_lo, 0),
                    "s2": (sT_hi, sT_lo, 2)}[name]

        def batch_dst(b, buf):
            _, d0, m, width = b.dst
            return buf[0:width, d0:d0 + m, :].rearrange("p k n -> p (k n)")

        def step_logits(ph, s):
            off = 0 if ph.serial else 1024 * (s.s % 2)
            return L[:, off:off + ph.maps * ph.width].rearrange("p (m c) -> p m c", m=ph.maps)

        def tile_cols(ph, t):
            if ph.width == FULL:
                return slice(256 * t, 256 * t + 256)
            return slice(0, P) if t == 0 else slice(P, CAUSAL)

        def step_banks(ph, s):
            return (0, 3) if ph.serial else (2 * (s.s % 2), 2 * (s.s % 2) + 2)

        def token_col(v):
            return v.rearrange("o (t p) -> p (o t)", p=P)

        PRO = [
            (ident[:], a["c_ident"]),
            (masks[:], a["c_masks"]),
            (knorm[:, :, 0, :], a["idx_kn_g"].partition_broadcast(P)),
            (knorm[:, :, 1, :], a["idx_kn_b"].partition_broadcast(P)),
            (subln[:], a["da_subln_2"].partition_broadcast(P)),
            (qnorm[:], a["mla_q_norm_2"].partition_broadcast(P)),
            (kvnorm[:], a["mla_kv_norm_2"].partition_broadcast(P)),
            (sinks[:], a["sw_sinks_2"].partition_broadcast(P)),
            (L[:, 0:512], a["da_lambda_2"].rearrange("l f d -> (l f d)").partition_broadcast(P)),
            (L[:, 512:536], a["c_inv"]),
            (L[:, 536:538].bitcast(I32), token_col(a["positions"])),
            (L[:, 538:540].bitcast(I32), token_col(a["positions_2"])),
            (L[0:REL_BUCKETS, 1024:1024 + BIAS_HEADS], a["rel_bias_2"]),
            (L[0:REL_BUCKETS, 1152:1152 + REL_ROW], a["c_onehot"]),
            (L[0:BIAS_HEADS, 1536:1536 + REL_ROW], a["c_relmask"]),
        ]

        @block.sync
        def _(sp):
            def load_gain(g):
                slot = g.j % 2
                if g.j >= 2:
                    sp.wait_ge(S["stage"], gain_list[g.j - 2].stage)
                name, row = g.g
                src = a[name] if row is None else a[name][row]
                sp.dma_start(gain[:, slot, 0, :], src.partition_broadcast(P)).then_inc(gain_landed[slot], 16)
                if g.b[0]:
                    name, row = g.b
                    src = a[name] if row is None else a[name][row]
                    sp.dma_start(gain[:, slot, 1, :], src.partition_broadcast(P)).then_inc(gain_landed[slot], 16)

            sp.dma_start(rows("tmp"), a["mem"][0].rearrange("(t p) d -> p t d", p=P)).then_inc(S["mem_landed"], 16)
            load_gain(p.first_gain)
            for u in p.units:
                if u.u >= RAW:
                    sp.wait_ge(S["lo_ready"], u.u - RAW + 1)
                ch = u.chunk
                src = u.weight[u.k0 * P:(u.k0 + u.nk) * P, ch.col:ch.col + ch.width]
                sp.dma_start(raw[:, u.u % RAW, 0:u.nk, 0:ch.width],
                             src.rearrange("(k p) n -> p k n", p=P)).then_inc(unit_landed[u.u % RAW], 16)
                if u.u == RAW - 1:
                    sp.dma_start(x[:], a["x"][0].rearrange("(t p) d -> p t d", p=P)).then_inc(S["x_landed"], 16)
                if u.gain is not None:
                    load_gain(u.gain)
                if u.late_gain is not None:
                    load_gain(u.late_gain)
            sp.wait_ge(S["acc_taken_dve"], p.n_taken["dve"])
            sp.dma_start(out[0].rearrange("(t p) d -> p t d", p=P), x[:]).then_inc(S["out_landed"], 16)
            sp.wait_ge(S["out_landed"], 16)

        @block.gpsimd
        def _(pool):
            for u in p.units:
                ch, slot, r = u.chunk, u.u % SPLIT, u.u % RAW
                pool.wait_ge(S["hi_ready"], u.u + 1)
                if u.u:
                    pool.wait_ge(S["lo_ready"], u.u)
                nc.gpsimd.tensor_tensor(w_lo[:, slot, 0:u.nk, 0:ch.width], raw[:, r, 0:u.nk, 0:ch.width],
                                        w_hi[:, slot, 0:u.nk, 0:ch.width].bitcast(F32),
                                        ALU.subtract).then_inc(S["lo_ready"], 1)

        @block.scalar
        def _(act):
            def split_unit(n):
                if n >= len(p.units):
                    return
                u = p.units[n]
                act.wait_ge(unit_landed[n % RAW], 16 * (n // RAW + 1))
                if n >= SPLIT:
                    act.wait_ge(S["unit_used"], n - SPLIT + 1)
                nc.scalar.copy(w_hi[:, n % SPLIT, 0:u.nk, 0:u.chunk.width],
                               raw[:, n % RAW, 0:u.nk, 0:u.chunk.width]).then_inc(S["hi_ready"], 1)

            def batch_hi(b):
                act.wait_ge(S["t_ready"], b.b + 1)
                hi, _, _ = act_split(b.dst[0])
                nc.scalar.copy(batch_dst(b, hi), tps[0:b.dst[3], b.b % 2, 0:b.dst[2] * N]).then_inc(S["t_hi"], 1)

            with nc.allow_non_contiguous_dma(reason="the positions, one to a partition"):
                for dst, src in PRO:
                    act.dma_start(dst, src).then_inc(S["prologue_landed"], 16)
            for n in range(AHEAD):
                split_unit(n)
            act.wait_ge(S["lambda_terms"], 1)
            nc.scalar.activation(small[:, 0, 4:8], small[:, 0, 0:4], ACT.Exp).then_inc(S["lambda_exp"], 1)
            act.wait_ge(S["angles"], 1)
            nc.scalar.activation(trig[:].rearrange("p s t f -> p (s t f)"), L[:, 640:736],
                                 ACT.Sin).then_inc(S["trig_done"], 1)
            act.wait_ge(S["rel_rows_made"], 1)
            act.dma_start(rel_rows, L[0:BIAS_HEADS, 1152:1152 + REL_ROW].unsqueeze(1)
                          .to_broadcast([BIAS_HEADS, P, REL_ROW])).then_inc(S["rel_rows_saved"], 16)
            bias_loads = 0
            mem_loads = 0

            for ph in p.phases:
                if ph.kind == "linear":
                    for ch in ph.chunks:
                        for u in ch.units:
                            for b in u.pre:
                                batch_hi(b)
                            split_unit(u.u + AHEAD)
                        if ch.eng != "act":
                            continue
                        act.wait_ge(S["unit_used"], ch.last + 1)
                        if ch.how == "silu":
                            if ch.dst[0] == "G":
                                dst = G[:, :, 0:ch.width]
                                if ch.index:
                                    act.wait_ge(S["acc_taken_dve"], p.chunks[ch.c - 1].count)
                            else:
                                act.wait_ge(S["stage"], ch.stage_before)
                                src, col = ch.dst
                                dst = rows(src)[:, :, col:col + ch.width]
                            fn = ACT.Silu
                        else:
                            _, _, col = ch.dst
                            dst = rows("tmp")[:, :, col:col + ch.width]
                            act.wait_ge(S["acc_taken_dve"], p.chunks[ch.c].dve_taken_before)
                            act.wait_ge(S["stage"], ch.stage_before)
                            fn = ACT.Sigmoid
                        bank = 2 * (ch.c % 2)
                        nc.scalar.activation(dst, acc[:, bank:bank + 2, 0:ch.width], fn).then_inc(S["acc_taken_act"], 1)
                elif ph.kind == "transpose":
                    for b in ph.batches:
                        if b.split:
                            batch_hi(b)
                elif ph.kind == "save_mem_kv":
                    act.wait_ge(S["acc_taken_dve"], ph.taken)
                    for l in range(DEPTH):
                        act.dma_start(mem_kv[l], U[:, 1024 * l:1024 * l + 1024]).then_inc(S["mem_kv_saved"], 16)
                elif ph.kind == "load_mem_kv":
                    if ph.layer == 0:
                        act.wait_ge(S["mem_kv_saved"], 16 * DEPTH)
                    else:
                        act.wait_ge(S["pv_ready"], ph.steps_before)
                    mem_loads += 1
                    act.dma_start(MKV[:], mem_kv[ph.layer]).then_inc(S["mem_kv_landed"], 16)
                elif ph.kind == "load_bias":
                    act.wait_ge(S["logits_ready"], ph.steps_before)
                    act.wait_ge(S["pv_ready"], ph.steps_before)
                    if bias_loads == 0:
                        act.wait_ge(S["rel_rows_saved"], 16)
                        act.dma_start(causal_2[:], a["c_masks"][:, 0, :]).then_inc(S["bias_landed"], 16)
                    bias_loads += 1
                    for off, lo, n in ((255, 0, P), (127, P, N)):
                        src = bass.AP(rel_rows.tensor, off + P * REL_ROW * ph.head,
                                      [[REL_ROW - 1, P], [P * REL_ROW, ph.heads], [1, n]])
                        act.dma_start(bias[:, 0:ph.heads, lo:lo + n], src).then_inc(S["bias_landed"], 16)
                elif ph.kind == "load_ple":
                    act.dma_start(rows(("U", 256, 0)), a["p_2"][ph.layer, 0].rearrange("(t p) d -> p t d", p=P)
                                  ).then_inc(S["ple_landed"], 16)
                elif ph.kind == "index_scores":
                    for i in range(2 * IDXH):
                        n = ph.first + i
                        t = i // IDXH
                        act.wait_ge(S["index_ready"], n + 1)
                        if n >= 2:
                            act.wait_ge(S["index_added"], n - 1)
                        w = P * (t + 1)
                        nc.scalar.activation(L[:, 512 * (n % 2):512 * (n % 2) + w], acc[:, n % 4, 0:w],
                                             ACT.Relu).then_inc(S["index_relu"], 1)
                elif ph.kind == "attention":
                    for s in ph.steps:
                        lg, slot = step_logits(ph, s), s.s % 2
                        act.wait_ge(S["max_ready"], s.s + 1)
                        if ph.flavour == "sinks":
                            nc.scalar.activation(sink_exp[:, slot, :], sink_exp[:, slot, :], ACT.Exp)
                        for m in range(1 if ph.serial else ph.maps):
                            for t in range(T):
                                part = lg[:, :, tile_cols(ph, t)] if ph.serial else lg[:, m, tile_cols(ph, t)]
                                c = 2 * m + t
                                ins = nc.scalar.activation(part, part, ACT.Exp, bias=neg_max[:, slot, c:c + 1],
                                                           accum_out=sums[:, slot, c:c + 1])
                        ins.then_inc(S["probs_ready"], 1)

        @block.tensor
        def _(pe):
            def do_batch(b):
                if b.b >= 2:
                    pe.wait_ge(S["t_taken"], b.b - 1)
                pe.wait_ge(S[b.after[0]], b.after[1])
                for i, (src, t, col, width) in enumerate(b.moves):
                    ins = nc.tensor.transpose(tps[0:width, b.b % 2, P * i:P * i + P],
                                              rows(src)[:, t, col:col + width], ident[:])
                ins.then_inc(S["t_ready"], 1)

            pe.wait_ge(S["prologue_landed"], 16 * len(PRO))
            nc.tensor.matmul(ops[0:BIAS_HEADS, 0, 0:REL_ROW], L[0:REL_BUCKETS, 1024:1024 + BIAS_HEADS],
                             L[0:REL_BUCKETS, 1152:1152 + REL_ROW], start=True, stop=True).then_inc(S["rel_ready"], 1)
            for ph in p.phases:
                if ph.kind == "transpose":
                    for b in ph.batches:
                        do_batch(b)
                elif ph.kind == "linear":
                    if ph.steps_before:
                        pe.wait_ge(S["logits_ready"], ph.steps_before)
                    if ph.index_before:
                        pe.wait_ge(S["index_relu"], ph.index_before)
                    for ch in ph.chunks:
                        if ch.c >= 2:
                            prev = p.chunks[ch.c - 2]
                            pe.wait_ge(S["acc_taken_" + prev.eng], prev.count)
                        hi, lo, off = act_split(ch.acts)
                        bank = 2 * (ch.c % 2)
                        for u in ch.units:
                            for b in u.pre:
                                do_batch(b)
                            pe.wait_ge(S["t_taken"], u.t_need if ch.acts == "h" and ch.index == 0 else ph.t_need)
                            pe.wait_ge(S["lo_ready"], u.u + 1)
                            slot = u.u % SPLIT
                            for k in range(u.nk):
                                kt = off + u.k0 + k
                                first_k, last_k = u.k0 + k == 0, u.k0 + k == ch.k_tiles - 1
                                for t in range(T):
                                    o = acc[:, bank + t, 0:ch.width]
                                    tok = slice(P * t, P * t + P)
                                    wh, wl = w_hi[:, slot, k, 0:ch.width], w_lo[:, slot, k, 0:ch.width]
                                    nc.tensor.matmul(o, hi[:, kt, tok], wh, start=first_k, stop=False)
                                    nc.tensor.matmul(o, hi[:, kt, tok], wl, start=False, stop=False)
                                    ins = nc.tensor.matmul(o, lo[:, kt, tok], wh, start=False, stop=last_k)
                            ins.then_inc(S["unit_used"], 1)
                elif ph.kind == "index_scores":
                    pe.wait_ge(S["t_taken"], ph.t_need)
                    pe.wait_ge(S["acc_taken_dve"], ph.taken["dve"])
                    pe.wait_ge(S["acc_taken_act"], ph.taken["act"])
                    for i in range(2 * IDXH):
                        n = ph.first + i
                        t, h = i // IDXH, i % IDXH
                        base = HD * (h % 2)
                        if n >= 4:
                            pe.wait_ge(S["index_relu"], n - 3)
                        w = P * (t + 1)
                        nc.tensor.matmul(acc[:, n % 4, 0:w], QT[base:base + HD, h // 2, P * t:P * t + P],
                                         KT[base:base + HD, 0, 0:w], start=True, stop=True
                                         ).then_inc(S["index_ready"], 1)
                elif ph.kind == "attention":
                    def do_scores(s):
                        lo_b, hi_b = step_banks(ph, s)
                        if s.i == 0:
                            pe.wait_ge(S["t_taken"], ph.t_need)
                            pe.wait_ge(S["acc_taken_dve"], ph.taken["dve"])
                            pe.wait_ge(S["acc_taken_act"], ph.taken["act"])
                            if ph.index_before:
                                pe.wait_ge(S["index_relu"], ph.index_before)
                            if s.s:
                                pe.wait_ge(S["logits_ready"], s.s)
                        elif ph.serial:
                            pe.wait_ge(S["logits_ready"], s.s)
                        elif s.i >= 2:
                            pe.wait_ge(S["logits_ready"], s.s - 1)
                        for m in range(ph.maps):
                            (qt, base, k), (kt, kbase, _) = s.q[m], s.k[m]
                            for t in range(T):
                                c = tile_cols(ph, t)
                                ins = nc.tensor.matmul(acc[:, lo_b + m, c], QT[base:base + k, qt, P * t:P * t + P],
                                                       KT[kbase:kbase + k, kt, 0:c.stop - c.start],
                                                       start=True, stop=True)
                        ins.then_inc(S["scores_ready"], 1)

                    def do_values(s):
                        lg = step_logits(ph, s)
                        if ph.flavour in ("dilated", "differential"):
                            pe.wait_ge(S["mixed_ready"], s.mixed)
                        else:
                            pe.wait_ge(S["probs_ready"], s.s + 1)
                        for tb in s.tb:
                            if tb.b >= 2:
                                pe.wait_ge(S["t_taken"], tb.b - 1)
                            for i in range(tb.blocks):
                                ins = nc.tensor.transpose(tps[:, tb.b % 2, P * i:P * i + P],
                                                          lg[:, tb.j, P * i:P * i + P], ident[:])
                            ins.then_inc(S["t_ready"], 1)
                        if s.s >= 2:
                            pe.wait_ge(S["out_taken"], s.s - 1)
                        for tb, (src, col) in zip(s.tb, s.v):
                            pe.wait_ge(S["t_taken"], tb.b + 1)
                            pt = PT[:, 2 * (s.s % 2) + tb.j, :]
                            for t in range(T):
                                o0 = (tb.j * T + t) * ph.dv
                                keys = range(T) if ph.width == FULL else range(t + 1)
                                for kt in keys:
                                    blk = tile_cols(ph, t).start + P * kt
                                    ins = nc.tensor.matmul(ops[:, s.s % 2, o0:o0 + ph.dv], pt[:, blk:blk + P],
                                                           rows(src)[:, kt, col:col + ph.dv],
                                                           start=kt == 0, stop=kt == keys[-1])
                        ins.then_inc(S["pv_ready"], 1)

                    if ph.serial:
                        for s in ph.steps:
                            do_scores(s)
                            do_values(s)
                    else:
                        do_scores(ph.steps[0])
                        for s in ph.steps:
                            if s.i + 1 < len(ph.steps):
                                do_scores(ph.steps[s.i + 1])
                            do_values(s)

        @block.vector
        def _(dve):
            v = nc.vector
            chain = [0]

            def link(ins):
                chain[0] += 1
                ins.then_inc(S["dve_chain"], 1)
                dve.wait_ge(S["dve_chain"], chain[0])

            def rsqrt(y, var, n):
                a1, a2 = small[:, 8, 0:n], small[:, 9, 0:n]
                link(v.tensor_scalar(a1.bitcast(I32), var.bitcast(I32), 1, None, ALU.logical_shift_right))
                link(v.tensor_scalar(y.bitcast(I32), a1.bitcast(I32), -1.0, float(0x5F3759DF), ALU.mult, ALU.add))
                for _ in range(3):
                    link(v.tensor_tensor(a1, y, y, ALU.mult))
                    link(v.tensor_tensor(a2, a1, var, ALU.mult))
                    link(v.tensor_scalar(a1, a2, -0.5, 1.5, ALU.mult, ALU.add))
                    link(v.tensor_tensor(y, y, a1, ALU.mult))

            def norm_rows(src, dst, g, width, eps, done=None):
                mv, rs = small[:, 1, 0:4], small[:, 2, 0:2]
                for t in range(T):
                    ins = v.bn_aggr(mv[:, 2 * t:2 * t + 2], stats[:, t, 0:-(-width // 512), :])
                link(ins)
                var = small[:, 3, 0:2]
                link(v.tensor_scalar(var, mv[:, 1:4:2], eps, None, ALU.add))
                rsqrt(rs, var, 2)
                for t in range(T):
                    ins = v.tensor_scalar(dst[:, t, :], src[:, t, :], mv[:, 2 * t:2 * t + 1], rs[:, t:t + 1],
                                          ALU.subtract, ALU.mult)
                link(ins)
                gg, bb = g
                link(v.tensor_tensor(dst, dst, gg.unsqueeze(1).to_broadcast([P, T, width]), ALU.mult))
                ins = v.tensor_tensor(dst, dst, bb.unsqueeze(1).to_broadcast([P, T, width]), ALU.add)
                if done is None:
                    link(ins)
                else:
                    ins.then_inc(done, 1)

            def rms_rows(src, dst, g, width, done=None):
                ms, rs = small[:, 1, 0:2], small[:, 2, 0:2]
                for t in range(T):
                    ins = v.tensor_tensor_reduce(out=L[:, 0:width], in0=src[:, t, :], in1=src[:, t, :],
                                                 scale=1.0, scalar=0.0, op0=ALU.mult, op1=ALU.add,
                                                 accum_out=ms[:, t:t + 1])
                    link(ins)
                link(v.tensor_scalar(small[:, 3, 0:2], ms, 1.0 / width, RMS_EPS, ALU.mult, ALU.add))
                rsqrt(rs, small[:, 3, 0:2], 2)
                for t in range(T):
                    ins = v.scalar_tensor_tensor(out=dst[:, t, :], in0=src[:, t, :], scalar=rs[:, t:t + 1],
                                                 in1=g, op0=ALU.mult, op1=ALU.mult)
                if done is None:
                    link(ins)
                else:
                    ins.then_inc(done, 1)

            def rope(heads, n, f0, half, out=None):
                x1, x2 = heads[:, :, :, 0:half], heads[:, :, :, half:2 * half]
                size = T * n * half
                cs = trig[:, 1, :, f0:f0 + half].unsqueeze(2).to_broadcast([P, T, n, half])
                sn = trig[:, 0, :, f0:f0 + half].unsqueeze(2).to_broadcast([P, T, n, half])
                tm = [L[:, i * size:(i + 1) * size].rearrange("p (t n f) -> p t n f", t=T, n=n) for i in range(4)]
                v.tensor_tensor(tm[0], x1, cs, ALU.mult)
                v.tensor_tensor(tm[1], x2, sn, ALU.mult)
                v.tensor_tensor(tm[2], x2, cs, ALU.mult)
                link(v.tensor_tensor(tm[3], x1, sn, ALU.mult))
                v.tensor_tensor(x1, tm[0], tm[1], ALU.subtract)
                link(v.tensor_tensor(x2, tm[2], tm[3], ALU.add))

            dve.wait_ge(S["prologue_landed"], 16 * len(PRO))
            lf = L[:, 0:512].rearrange("p (l f d) -> p l f d", l=2, f=4)
            pr = L[:, 768:1024].rearrange("p (l f d) -> p l f d", l=2, f=2)
            link(v.tensor_tensor(pr, lf[:, :, 0:4:2, :], lf[:, :, 1:4:2, :], ALU.mult))
            v.tensor_reduce(small[:, 0, 0:4], pr.rearrange("p l f d -> p (l f) d"), AX.X,
                            ALU.add).then_inc(S["lambda_terms"], 1)
            link(v.tensor_copy(L[:, 540:544], L[:, 536:540].bitcast(I32)))
            ang = L[:, 544:592].rearrange("p (t f) -> p t f", t=T)
            for t in range(T):
                v.tensor_scalar(ang[:, t, 0:8], L[:, 512:520], L[:, 540 + t:541 + t], None, ALU.mult)
                ins = v.tensor_scalar(ang[:, t, 8:24], L[:, 520:536], L[:, 542 + t:543 + t], None, ALU.mult)
            link(ins)
            n_turn, r = L[:, 592:640], L[:, 640:736]
            angf = L[:, 544:592]
            for i, quarter in enumerate((0.0, 0.25)):
                rr = r[:, 48 * i:48 * i + 48]
                link(v.tensor_scalar(n_turn, angf, 1 / (2 * math.pi), quarter, ALU.mult, ALU.add))
                link(v.tensor_scalar(n_turn, n_turn, ROUND, None, ALU.add))
                link(v.tensor_scalar(n_turn, n_turn, ROUND, None, ALU.subtract))
                link(v.scalar_tensor_tensor(out=rr, in0=n_turn, scalar=-TWO_PI_1, in1=angf, op0=ALU.mult, op1=ALU.add))
                link(v.scalar_tensor_tensor(out=rr, in0=n_turn, scalar=-TWO_PI_2, in1=rr, op0=ALU.mult, op1=ALU.add))
                link(v.scalar_tensor_tensor(out=rr, in0=n_turn, scalar=-TWO_PI_3, in1=rr, op0=ALU.mult, op1=ALU.add))
                if i:
                    link(v.tensor_scalar(rr, rr, math.pi / 2, None, ALU.add))
            v.tensor_scalar(r, r, PI_INSIDE, -PI_INSIDE, ALU.min, ALU.max).then_inc(S["angles"], 1)
            link(v.tensor_scalar(neg_sinks[:], sinks[:], -1.0, None, ALU.mult))
            dve.wait_ge(S["rel_ready"], 1)
            v.tensor_tensor(L[0:BIAS_HEADS, 1152:1152 + REL_ROW], ops[0:BIAS_HEADS, 0, 0:REL_ROW],
                            L[0:BIAS_HEADS, 1536:1536 + REL_ROW], ALU.add).then_inc(S["rel_rows_made"], 1)
            dve.wait_ge(S["lambda_exp"], 1)
            for l in range(DEPTH_2):
                lam_init = 0.8 - 0.6 * math.exp(-0.3 * l)
                link(v.tensor_tensor(small[:, 0, 8 + l:9 + l], small[:, 0, 5 + 2 * l:6 + 2 * l],
                                     small[:, 0, 4 + 2 * l:5 + 2 * l], ALU.subtract))
                link(v.tensor_scalar(neg_lam[:, l:l + 1], small[:, 0, 8 + l:9 + l], lam_init, None, ALU.subtract))
            dve.wait_ge(S["trig_done"], 1)
            dve.wait_ge(S["rel_rows_saved"], 16)

            gain_count = [0, 0]

            def gains(g):
                slot = g.j % 2
                gain_count[slot] += 32 if g.b[0] else 16
                dve.wait_ge(gain_landed[slot], gain_count[slot])
                return gain[:, slot, 0, :], gain[:, slot, 1, :]

            def take_batch(b):
                _, d0, m, width = b.dst
                ps = tps[0:width, b.b % 2, 0:m * N]
                if b.split:
                    hi, lo, _ = act_split(b.dst[0])
                    dve.wait_ge(S["t_hi"], b.hi)
                    ins = v.tensor_tensor(batch_dst(b, lo), ps, batch_dst(b, hi).bitcast(F32), ALU.subtract)
                else:
                    dve.wait_ge(S["t_ready"], b.b + 1)
                    ins = v.tensor_copy(batch_dst(b, {"QT": QT, "KT": KT}[b.dst[0]]), ps)
                ins.then_inc(S["t_taken"], 1)

            def take_chunk(ch):
                bank = 2 * (ch.c % 2)
                ps = acc[:, bank:bank + 2, 0:ch.width]
                dve.wait_ge(S["unit_used"], ch.last + 1)
                dve.wait_ge(S["stage"], ch.stage_before)
                if ch.how == "copy":
                    src, col = ch.dst
                    ins = v.tensor_copy(rows(src)[:, :, col:col + ch.width], ps)
                elif ch.how == "mem_kv":
                    l = ch.dst
                    ins = v.tensor_copy(rows(("U", 512, 1024 * l)), ps)
                elif ch.how == "residual":
                    c = slice(ch.dst, ch.dst + ch.width)
                    y = rows("tmp")
                    for t in range(T):
                        ins = v.scalar_tensor_tensor(out=y[:, t, c], in0=x[:, t, c], scalar=ALPHA, in1=ps[:, t, :],
                                                     op0=ALU.mult, op1=ALU.add)
                    link(ins)
                    for t in range(T):
                        ins = v.bn_stats(stats[:, t, ch.dst // 512, :], y[:, t, c])
                elif ch.how == "up":
                    dve.wait_ge(S["acc_taken_act"], ch.act_taken)
                    ins = v.tensor_tensor(H[:, :, 0:ch.width], G[:, :, 0:ch.width], ps, ALU.mult)
                elif ch.how in ("branch_first", "branch"):
                    dve.wait_ge(S["acc_taken_act"], ch.act_taken)
                    c = slice(ch.dst, ch.dst + ch.width)
                    y, gate = rows("Y")[:, :, c], rows("tmp")[:, :, c]
                    if ch.how == "branch_first":
                        ins = v.tensor_tensor(y, gate, ps, ALU.mult)
                    else:
                        link(v.tensor_tensor(gate, gate, ps, ALU.mult))
                        ins = v.tensor_tensor(y, y, gate, ALU.add)
                elif ch.how == "ple":
                    dve.wait_ge(S["acc_taken_act"], ch.act_taken)
                    c = slice(ch.dst, ch.dst + ch.width)
                    gate = rows("tmp")[:, :, c]
                    link(v.tensor_tensor(gate, gate, ps, ALU.mult))
                    ins = v.tensor_tensor(x[:, :, c], x[:, :, c], gate, ALU.add)
                ins.then_inc(S["acc_taken_dve"], 1)

            index_done = [0]

            def index_scores(ph):
                wi = rows(ph.src)[:, :, 2816:2816 + IDXH]
                link(v.tensor_scalar(wi, wi, (IDXH * HD) ** -0.5, None, ALU.mult))
                for i in range(2 * IDXH):
                    t, h = i // IDXH, i % IDXH
                    n = index_done[0]
                    w = P * (t + 1)
                    dst = scores[:, 0:P] if t == 0 else scores[:, P:CAUSAL]
                    relu = L[:, 512 * (n % 2):512 * (n % 2) + w]
                    dve.wait_ge(S["index_relu"], n + 1)
                    if h == 0:
                        ins = v.tensor_scalar(dst, relu, wi[:, t, 0:1], None, ALU.mult)
                    else:
                        ins = v.scalar_tensor_tensor(out=dst, in0=relu, scalar=wi[:, t, h:h + 1], in1=dst,
                                                     op0=ALU.mult, op1=ALU.add)
                    ins.then_inc(S["index_added"], 1)
                    index_done[0] += 1
                    dve.wait_ge(S["index_added"], index_done[0])
                link(v.tensor_tensor(scores[:], scores[:], masks[:, 0, :], ALU.add))

            def top_k(done):
                best = small[:, 4:6, 0:8]
                for _ in range(TOPK // 8):
                    for t, c in ((0, slice(0, P)), (1, slice(P, CAUSAL))):
                        ins = v.max(best[:, t, :], scores[:, c])
                    link(ins)
                    for t, c in ((0, slice(0, P)), (1, slice(P, CAUSAL))):
                        ins = v.match_replace(scores[:, c], best[:, t, :], scores[:, c], SENTINEL)
                    link(ins)
                link(v.tensor_scalar(selected[:], scores[:], SENTINEL, NEG, ALU.not_equal, ALU.mult))
                v.tensor_tensor(selected[:], selected[:], masks[:, 0, :], ALU.add).then_inc(done, 1)

            def do_stage(ph):
                done = S["stage"]
                if ph.n > 1:
                    dve.wait_ge(done, ph.n - 1)
                fn = ph.fn
                if fn == "mem_norm":
                    dve.wait_ge(S["mem_landed"], 16)
                    m = rows("tmp")
                    for t in range(T):
                        for c in range(2):
                            ins = v.bn_stats(stats[:, t, c, :], m[:, t, 512 * c:512 * c + 512])
                    link(ins)
                    norm_rows(m, m, gains(ph.gain), D, LN_EPS, done)
                elif fn == "mem_kv_saved":
                    dve.wait_ge(S["mem_kv_saved"], 16 * DEPTH)
                    dve.wait_ge(S["x_landed"], 16)
                    v.memset(small[:, 7, 0:1], 0.0).then_inc(done, 1)
                elif fn == "nothing":
                    dve.wait_ge(S["acc_taken_dve"], ph.dve_taken)
                    v.memset(small[:, 7, 0:1], 0.0).then_inc(done, 1)
                elif fn == "layer_norm":
                    dve.wait_ge(S["acc_taken_dve"], ph.dve_taken)
                    norm_rows(rows("tmp"), x[:], gains(ph.gain), D, LN_EPS, done)
                elif fn == "rope_first":
                    dve.wait_ge(S["acc_taken_dve"], ph.dve_taken)
                    r = rows(ph.src)
                    rope(r[:, :, 0:2 * MIX].rearrange("p t (n d) -> p t n d", d=HD), 2 * HEADS, 0, 8)
                    if ph.mixer == 0:
                        rope(r[:, :, 2304:2816].rearrange("p t (n d) -> p t n d", d=HD), IDXH, 0, 8)
                        ki = r[:, :, 2824:2888]
                        for t in range(T):
                            ins = v.bn_stats(stats[:, t, 0, :], ki[:, t, :])
                        link(ins)
                        norm_rows(ki, ki, (knorm[:, ph.layer, 0, :], knorm[:, ph.layer, 1, :]), HD, LN_EPS)
                        rope(ki.unsqueeze(2), 1, 0, 8)
                        twice = rows("KI").rearrange("p t (m d) -> p t m d", m=2)
                        v.tensor_copy(twice, ki.unsqueeze(2).to_broadcast([P, T, 2, HD])).then_inc(done, 1)
                    else:
                        v.memset(small[:, 7, 0:1], 0.0).then_inc(done, 1)
                elif fn == "top_k":
                    top_k(done)
                elif fn == "rms_pre":
                    dve.wait_ge(S["acc_taken_dve"], ph.dve_taken)
                    rms_rows(x[:], rows("tmp"), gains(ph.gain)[0], D, done)
                elif fn == "rms_post":
                    dve.wait_ge(S["acc_taken_dve"], ph.dve_taken)
                    z = rows("tmp")
                    rms_rows(z, z, gains(ph.gain)[0], D)
                    v.tensor_tensor(x[:], x[:], z, ALU.add).then_inc(done, 1)
                elif fn == "sub_norm":
                    dve.wait_ge(S["out_taken"], ph.steps_before)
                    o = rows(ph.src)[:, :, 0:512]
                    lam_init = 0.8 - 0.6 * math.exp(-0.3 * ph.layer)
                    sq = L[:, 0:1024].rearrange("p (t c) -> p t c", t=T)
                    link(v.tensor_tensor(sq, o, o, ALU.mult))
                    link(v.tensor_reduce(small[:, 1, 0:8], sq.rearrange("p t (h e) -> p (t h) e", e=P), AX.X, ALU.add))
                    link(v.tensor_scalar(small[:, 3, 0:8], small[:, 1, 0:8], 1.0 / P, RMS_EPS, ALU.mult, ALU.add))
                    rsqrt(small[:, 2, 0:8], small[:, 3, 0:8], 8)
                    link(v.tensor_scalar(small[:, 2, 0:8], small[:, 2, 0:8], 1.0 - lam_init, None, ALU.mult))
                    heads = o.rearrange("p t (h e) -> p t h e", e=P)
                    rs = small[:, 2, 0:8].rearrange("p (t h) -> p t h", t=T).unsqueeze(3).to_broadcast([P, T, DA_H, P])
                    link(v.tensor_tensor(heads, heads, rs, ALU.mult))
                    gg = subln[:, ph.layer, :].unsqueeze(1).unsqueeze(1).to_broadcast([P, T, DA_H, P])
                    link(v.tensor_tensor(heads, heads, gg, ALU.mult))
                    dve.wait_ge(S["acc_taken_act"], ph.act_taken)
                    v.tensor_tensor(o, o, rows(ph.src)[:, :, 1536:2048], ALU.mult).then_inc(done, 1)
                elif fn == "gate_mixed":
                    dve.wait_ge(S["out_taken"], ph.steps_before)
                    dve.wait_ge(S["acc_taken_act"], ph.act_taken)
                    o = rows(ph.src)[:, :, 0:512]
                    src, col = ph.z
                    v.tensor_tensor(o, o, rows(src)[:, :, col:col + 512], ALU.mult).then_inc(done, 1)
                elif fn == "latent_norm":
                    dve.wait_ge(S["acc_taken_dve"], ph.dve_taken)
                    r = rows(ph.src)
                    rms_rows(r[:, :, 0:256], r[:, :, 0:256], qnorm[:, ph.layer, :], 256)
                    rms_rows(r[:, :, 256:384], r[:, :, 256:384], kvnorm[:, ph.layer, :], P)
                    rope(r[:, :, 384:416].unsqueeze(2), 1, 8, 16)
                    v.memset(small[:, 7, 0:1], 0.0).then_inc(done, 1)
                elif fn == "latent_rope_q":
                    dve.wait_ge(S["acc_taken_dve"], ph.dve_taken)
                    heads = rows(ph.src).rearrange("p t (n d) -> p t n d", d=MLA_K)
                    rope(heads[:, :, :, HD:MLA_K], MLA_H, 8, 16)
                    v.memset(small[:, 7, 0:1], 0.0).then_inc(done, 1)
                elif fn == "latent_keys":
                    dve.wait_ge(S["t_ready"], ph.t_need)
                    heads = rows(ph.dst).rearrange("p t (n d) -> p t n d", d=MLA_K)
                    kv = rows(ph.src).rearrange("p t (n d) -> p t n d", d=P)
                    for t in range(T):
                        v.tensor_copy(heads[:, t, :, 0:HD], kv[:, t, :, 0:HD])
                        kr = rows(ph.low)[:, t, 384:416].unsqueeze(1).to_broadcast([P, MLA_H, 32])
                        ins = v.tensor_copy(heads[:, t, :, HD:MLA_K], kr)
                    ins.then_inc(done, 1)
                elif fn == "twice_keys":
                    dve.wait_ge(S["acc_taken_dve"], ph.dve_taken)
                    k2 = rows(("U", 256, 2560)).rearrange("p t (h m d) -> p t h m d", h=2, m=2)
                    for t in range(T):
                        k1 = rows(ph.src)[:, t, 512:640].rearrange("p (h d) -> p h d", h=2)
                        ins = v.tensor_copy(k2[:, t], k1.unsqueeze(2).to_broadcast([P, 2, 2, HD]))
                    ins.then_inc(done, 1)
                else:
                    raise ValueError(fn)

            bias_count = [0]

            def attention(ph):
                def mask_of(s):
                    if ph.flavour == "dilated":
                        return masks[:, 1:4, :]
                    if ph.mask == "bias":
                        if ph.flavour == "sinks":
                            return bias[:, 2 * s.i:2 * s.i + 2, :]
                        return bias[:, s.i:s.i + 1, :].to_broadcast([P, 2, CAUSAL])
                    if ph.mask == "selected":
                        return selected[:].unsqueeze(1).to_broadcast([P, 2, CAUSAL])
                    m = masks[:, 0, :] if ph.block == 1 else causal_2[:]
                    return m.unsqueeze(1).to_broadcast([P, 2, CAUSAL])

                if ph.mask == "bias":
                    dve.wait_ge(S["bias_landed"], ph.bias_need)
                if ph.mask == "selected":
                    dve.wait_ge(S["stage"], ph.stage_need)

                def logits(s):
                    lo_b, hi_b = step_banks(ph, s)
                    lg, slot = step_logits(ph, s), s.s % 2
                    dve.wait_ge(S["scores_ready"], s.s + 1)
                    ps = acc[:, lo_b:lo_b + ph.maps, 0:ph.width]
                    if ph.width == FULL:
                        ins = v.tensor_scalar(lg, ps, ph.scale, None, ALU.mult)
                    else:
                        ins = v.scalar_tensor_tensor(out=lg, in0=ps, scalar=ph.scale, in1=mask_of(s),
                                                     op0=ALU.mult, op1=ALU.add)
                    ins.then_inc(S["logits_ready"], 1)
                    dve.wait_ge(S["logits_ready"], s.s + 1)
                    nm = neg_max[:, slot, :]
                    for t in range(T):
                        part = lg[:, :, tile_cols(ph, t)]
                        if ph.serial:
                            ins = v.tensor_reduce(nm[:, t:t + 1], part, AX.XY, ALU.max, negate=True)
                        else:
                            ins = v.tensor_reduce(nm[:, t:t + 3:2], part, AX.X, ALU.max, negate=True)
                    if ph.flavour == "sinks":
                        link(ins)
                        nm2 = nm.rearrange("p (m t) -> p m t", m=2)
                        h = slice(2 * s.i, 2 * s.i + 2)
                        link(v.tensor_tensor(nm2, nm2, neg_sinks[:, ph.layer, h].unsqueeze(2).to_broadcast([P, 2, T]),
                                             ALU.min))
                        ins = v.tensor_tensor(sink_exp[:, slot, :].rearrange("p (m t) -> p m t", m=2), nm2,
                                              sinks[:, ph.layer, h].unsqueeze(2).to_broadcast([P, 2, T]), ALU.add)
                    ins.then_inc(S["max_ready"], 1)

                def outputs(s):
                    lg, slot = step_logits(ph, s), s.s % 2
                    dve.wait_ge(S["probs_ready"], s.s + 1)
                    rc, sm = recips[:, slot, :], sums[:, slot, :]
                    if ph.flavour == "sinks":
                        link(v.tensor_tensor(sm, sm, sink_exp[:, slot, :], ALU.add))
                    n = 2 if ph.serial else 4
                    link(v.reciprocal(rc[:, 0:n], sm[:, 0:n]))
                    if ph.flavour == "dilated":
                        link(v.tensor_tensor(lg[:, 0, :], lg[:, 0, :], lg[:, 1, :], ALU.add))
                        v.tensor_tensor(lg[:, 0, :], lg[:, 0, :], lg[:, 2, :], ALU.add).then_inc(S["mixed_ready"], 1)
                    elif ph.flavour == "differential":
                        link(v.tensor_scalar(rc[:, 2:4], rc[:, 2:4], neg_lam[:, ph.layer:ph.layer + 1], None, ALU.mult))
                        for t in range(T):
                            c = tile_cols(ph, t)
                            ins = v.tensor_scalar(lg[:, 1, c], lg[:, 1, c], rc[:, 2 + t:3 + t], None, ALU.mult)
                        link(ins)
                        for t in range(T):
                            c = tile_cols(ph, t)
                            ins = v.scalar_tensor_tensor(out=lg[:, 0, c], in0=lg[:, 0, c], scalar=rc[:, t:t + 1],
                                                         in1=lg[:, 1, c], op0=ALU.mult, op1=ALU.add)
                        ins.then_inc(S["mixed_ready"], 1)
                    for tb in s.tb:
                        dve.wait_ge(S["t_ready"], tb.b + 1)
                        v.tensor_copy(PT[:, 2 * (s.s % 2) + tb.j, 0:tb.blocks * P],
                                      tps[:, tb.b % 2, 0:tb.blocks * P]).then_inc(S["t_taken"], 1)
                    dve.wait_ge(S["pv_ready"], s.s + 1)
                    dst = rows(ph.heads_out)
                    if ph.flavour == "differential":
                        ins = v.tensor_copy(dst[:, :, s.out:s.out + P],
                                            ops[:, slot, 0:T * P].rearrange("p (t e) -> p t e", t=T))
                    elif ph.serial:
                        o = ops[:, slot, 0:T * ph.dv].rearrange("p (t e) -> p t e", t=T)
                        ins = v.tensor_tensor(dst[:, :, s.out:s.out + ph.dv], o,
                                              rc[:, 0:T].unsqueeze(2).to_broadcast([P, T, ph.dv]), ALU.mult)
                    else:
                        o = ops[:, slot, 0:4 * HD].rearrange("p (m t e) -> p m t e", m=2, t=T)
                        d4 = dst[:, :, s.out:s.out + P].rearrange("p t (m e) -> p m t e", m=2)
                        r4 = rc.rearrange("p (m t) -> p m t", m=2).unsqueeze(3).to_broadcast([P, 2, T, HD])
                        ins = v.tensor_tensor(d4, o, r4, ALU.mult)
                    ins.then_inc(S["out_taken"], 1)

                if ph.serial:
                    for s in ph.steps:
                        logits(s)
                        outputs(s)
                else:
                    logits(ph.steps[0])
                    for s in ph.steps:
                        if s.i + 1 < len(ph.steps):
                            logits(ph.steps[s.i + 1])
                        outputs(s)

            for ph in p.phases:
                if ph.kind == "stage":
                    do_stage(ph)
                elif ph.kind == "transpose":
                    for b in ph.batches:
                        take_batch(b)
                elif ph.kind == "linear":
                    for ch in ph.chunks:
                        for u in ch.units:
                            for b in u.pre:
                                take_batch(b)
                        if ch.eng == "dve":
                            take_chunk(ch)
                elif ph.kind == "index_scores":
                    index_scores(ph)
                elif ph.kind == "attention":
                    attention(ph)


_CONSTS = ("c_ident", "c_masks", "c_inv", "c_onehot", "c_relmask")


def kernel(**inputs):
    import concourse.bacc as bacc
    from concourse.bass_utils import run_bass_kernel_spmd

    nc = bacc.Bacc("TRN2", target_bir_lowering=False, num_devices=1)
    arrays, aps = {}, {}
    given = {k: np.ascontiguousarray(v) for k, v in inputs.items()}
    for name, arr in {**given, **shape_constants()}.items():
        arrays[f"in_{name}"] = arr
        aps[name] = nc.dram_tensor(f"in_{name}", arr.shape, mybir.dt.from_np(arr.dtype), kind="ExternalInput").ap()
    out = nc.dram_tensor("out", (1, N, D), F32, kind="ExternalOutput").ap()
    build(nc, aps, out)
    r = run_bass_kernel_spmd(nc, [arrays], core_ids=[0])
    return r.results[0]["out"]
```

```python
import math
from contextlib import ExitStack

import numpy as np

import concourse.bass as bass
from concourse import mybir

F32 = mybir.dt.float32
F32R = mybir.dt.float32r
I32 = mybir.dt.int32
ALU = mybir.AluOpType
ACT = mybir.ActivationFunctionType
AX = mybir.AxisListType

P = 128
T = 2
N = T * P
D = 1024
DEPTH = 4
HD = 64
MIX = 768
HEADS = MIX // HD
MEMW = 256
IDXH = 8
TOPK = min(256, N // 4)
FF = 2816
ALPHA = (2 * DEPTH) ** 0.25
LN_EPS = 1e-5
RMS_EPS = 1e-6
DEPTH_2 = 2
DA_H, MLA_H, SW_H = 4, 8, 8
MLA_K = 96
BIAS_HEADS = DA_H + SW_H
REL_BUCKETS = 32
NEG = -1e30
SENTINEL = -3e38
SCALE = HD ** -0.5
MLA_SCALE = MLA_K ** -0.5
CAUSAL = 384
FULL = 512
REL_ROW = 384

CHUNK = 512
UK = 2
RAW = 6
SPLIT = 6
AHEAD = SPLIT - 1

TWO_PI_1 = 6.28125
TWO_PI_2 = float(np.float32(0.0019350051879882812))
TWO_PI_3 = 2 * math.pi - TWO_PI_1 - TWO_PI_2
ROUND = 12582912.0
PI_INSIDE = 3.1415925

C_AQ, C_AZ, C_BQ, C_BZ, C_CQ, C_CZ, C_G = 0, 1536, 2048, 2464, 2976, 3744, 4256


def t5_bucket_rows():
    rel = 255 - np.arange(REL_ROW)
    n = np.maximum(rel, 0)
    nf = np.maximum(n, 1).astype(np.float32)
    half = REL_BUCKETS // 2
    large = half + (np.log(nf / np.float32(half)) / np.float32(math.log(128 / half))
                    * np.float32(REL_BUCKETS - half)).astype(np.int32)
    bucket = np.where(n < half, n, np.minimum(large, REL_BUCKETS - 1))
    onehot = ((np.arange(REL_BUCKETS)[:, None] == bucket[None]) & (rel >= 0)[None]).astype(np.float32)
    mask = np.zeros((BIAS_HEADS, REL_ROW), np.float32)
    mask[:, rel < 0] = NEG
    mask[DA_H:, rel >= 128] = NEG
    return onehot, mask


def shape_constants():
    q0, k0 = np.arange(P)[:, None], np.arange(P)[None]
    q1, k1 = P + np.arange(P)[:, None], np.arange(N)[None]

    def mask(keep):
        both = np.concatenate([keep(q0, k0), keep(q1, k1)], 1)
        return np.where(both, 0.0, NEG).astype(np.float32)

    masks = np.stack([
        mask(lambda q, k: k <= q),
        mask(lambda q, k: (k <= q) & (q - k <= 128)),
        mask(lambda q, k: (k <= q) & ((q - k) % 4 == 0)),
        mask(lambda q, k: (k <= q) & ((q - k) % 16 == 0)),
    ], 1)
    inv_1 = np.power(500000.0, (-np.arange(8, dtype=np.float32) / np.float32(8)).astype(np.float64))
    inv_2 = np.power(10000.0, (-np.arange(16, dtype=np.float32) / np.float32(16)).astype(np.float64))
    inv = np.broadcast_to(np.concatenate([inv_1, inv_2]).astype(np.float32), (P, 24))
    onehot, rel_mask = t5_bucket_rows()
    return {
        "c_ident": np.eye(P, dtype=np.float32),
        "c_masks": np.ascontiguousarray(masks),
        "c_inv": np.ascontiguousarray(inv),
        "c_onehot": onehot,
        "c_relmask": rel_mask,
    }


def column_chunks(start, stop):
    return [(c, min(CHUNK, stop - c)) for c in range(start, stop, CHUNK)]


class Phase:

    def __init__(self, kind, layer=None, chunks=None, t_need=0, batches=None, steps=None, block=None,
                 stage_need=0, bias_need=0, fn=None, n=None, incs=1, act_taken=0, dve_taken=0,
                 act_need=0, src=None, dst=None, low=None, z=None, gain=None, head=None,
                 heads=None, first=0, steps_before=0, index_before=0):
        self.kind = kind
        self.layer = layer
        self.chunks = chunks
        self.t_need = t_need
        self.batches = batches
        self.steps = steps
        self.block = block
        self.stage_need = stage_need
        self.bias_need = bias_need
        self.fn = fn
        self.n = n
        self.incs = incs
        self.act_taken = act_taken
        self.dve_taken = dve_taken
        self.act_need = act_need
        self.src = src
        self.dst = dst
        self.low = low
        self.z = z
        self.gain = gain
        self.head = head
        self.heads = heads
        self.first = first
        self.steps_before = steps_before
        self.index_before = index_before


class Batch:

    def __init__(self, b, moves, dst, split, after, hi=0):
        self.b = b
        self.moves = moves
        self.dst = dst
        self.split = split
        self.after = after
        self.hi = hi


class Chunk:

    def __init__(self, c, index, acts, k_tiles, col, width, how, dst, eng, count, act_taken,
                 dve_taken_before, stage_before, bank, free_when):
        self.c = c
        self.index = index
        self.acts = acts
        self.k_tiles = k_tiles
        self.col = col
        self.width = width
        self.how = how
        self.dst = dst
        self.eng = eng
        self.count = count
        self.act_taken = act_taken
        self.dve_taken_before = dve_taken_before
        self.stage_before = stage_before
        self.bank = bank
        self.free_when = free_when
        self.units = []
        self.last = None


class Unit:

    def __init__(self, u, k0, nk, chunk, weight):
        self.u = u
        self.k0 = k0
        self.nk = nk
        self.chunk = chunk
        self.weight = weight
        self.pre = []
        self.gain = None
        self.late_gain = None
        self.t_need = 0


class Step:

    def __init__(self, q, k, v, out, width=CAUSAL, dv=HD, scale=SCALE, flavour="plain", mask=None,
                 heads_out=None, pre=None, v_taken=0, bias_row=0):
        self.q = q
        self.k = k
        self.v = v
        self.out = out
        self.width = width
        self.dv = dv
        self.scale = scale
        self.flavour = flavour
        self.mask = mask
        self.heads_out = heads_out
        self.pre = pre
        self.v_taken = v_taken
        self.bias_row = bias_row
        self.maps = len(q)
        self.s = 0
        self.i = 0
        self.bank = 0
        self.free_when = []
        self.before = []
        self.fill = []
        self.tb = []
        self.mixed = 0


class Turn:

    def __init__(self, b, j, blocks):
        self.b = b
        self.j = j
        self.blocks = blocks


class Gain:

    def __init__(self, j, g, b):
        self.j = j
        self.g = g
        self.b = b
        self.stage = None


class Plan:

    def __init__(self):
        self.phases = []
        self.units = []
        self.chunks = []
        self.n_t = 0
        self.n_hi = 0
        self.n_steps = 0
        self.n_stage = 0
        self.n_taken = {"dve": 0, "act": 0}
        self.n_index = 0
        self.n_mixed = 0
        self.n_bias = 0
        self.block = 1
        self.k_ready = {"x": [0] * 8, "h": [0] * (FF // P), "s": [0] * 4, "s2": [0] * 4}
        self.bank_held = [None] * 4
        self.pair = 1
        self.fixed_pair = None

    def take_banks(self, bank, n, then):
        waits = []
        for b in range(bank, bank + n):
            if self.bank_held[b] is not None and self.bank_held[b] not in waits:
                waits.append(self.bank_held[b])
            self.bank_held[b] = then
        return waits

    def add(self, kind, **kw):
        ph = Phase(kind, **kw)
        self.phases.append(ph)
        return ph

    def batch(self, source, moves, dst, split, after):
        b = Batch(self.n_t, moves, dst, split, after)
        self.n_t += 1
        if split:
            self.n_hi += 1
            b.hi = self.n_hi
        return b

    def split_batches(self, source, k0, nk, dst, d0, after):
        out = []
        for k in range(0, nk, 4):
            m = min(4, nk - k)
            for t in range(T) if m > 2 else (None,):
                tiles = range(T) if t is None else (t,)
                moves = [(source, tt, (k0 + k + j) * P, P) for j in range(m) for tt in tiles]
                when = after[t or 0] if isinstance(after, list) else after
                out.append(self.batch(source, moves, (dst, d0 + k, m, P, t), True, when))
            for j in range(m):
                self.k_ready[dst][d0 + k + j] = self.n_t
                if dst == "s" and d0 + k + j >= 2:
                    self.k_ready["s2"][d0 + k + j - 2] = self.n_t
        return out

    def row_batches(self, source, dst, after):
        out = []
        for t in range(T):
            for k in (0, 4):
                moves = [(source, t, (k + j) * P, P) for j in range(4)]
                out.append(self.batch(source, moves, (dst, k, 4, P, t), True, after[t]))
                for j in range(4):
                    self.k_ready[dst][k + j] = self.n_t
        return out

    def head_batches(self, source, cols, width, dst, d0, after):
        out = []
        for i in range(0, len(cols), 2):
            pair = cols[i:i + 2]
            moves = [(source, t, c, width) for c in pair for t in range(T)]
            out.append(self.batch(source, moves, (dst, d0 + i, len(pair), width, None), False, after))
        return out

    def open_chunk(self, weight, k_tiles, acts, spec, index, before=None):
        col, width, how, dst = spec
        eng = "act" if how in ("silu", "sigmoid") else "dve"
        before_dve = self.n_taken["dve"]
        self.n_taken[eng] += 1
        count = self.n_taken[eng]
        self.pair = 1 - self.pair if self.fixed_pair is None else self.fixed_pair
        bank = 2 * self.pair
        ch = Chunk(len(self.chunks), index, acts, k_tiles, col, width, how, dst, eng, count,
                   self.n_taken["act"], before_dve, self.n_stage, bank,
                   self.take_banks(bank, T, ("acc_taken_" + eng, count)))
        self.chunks.append(ch)
        for ui, k0 in enumerate(range(0, k_tiles, UK)):
            u = Unit(len(self.units), k0, min(UK, k_tiles - k0), ch, weight)
            if before and (index, ui) in before:
                u.pre = before[(index, ui)]()
            u.t_need = max(self.k_ready[acts][k0:k0 + u.nk])
            self.units.append(u)
            ch.units.append(u)
        ch.last = ch.units[-1].u
        return ch

    def linear(self, weight, k_tiles, acts, chunks, before=None, gains=None):
        ph = self.add("linear", chunks=[])
        for ci, spec in enumerate(chunks):
            ch = self.open_chunk(weight, k_tiles, acts, spec, ci, before)
            ph.chunks.append(ch)
            if ci == 0:
                ch.units[0].gain = gains
        return ph

    def transpose(self, batches):
        return self.add("transpose", batches=batches)

    def stage(self, fn, incs=1, **kw):
        self.n_stage += incs
        return self.add("stage", fn=fn, n=self.n_stage, incs=incs, act_taken=self.n_taken["act"],
                        dve_taken=self.n_taken["dve"], steps_before=self.n_steps, **kw)

    def attention(self, steps, layer=None, fill=(), fill_steps=1):
        ph = self.add("attention", t_need=self.n_t, steps=steps, layer=layer, block=self.block, first=self.n_steps,
                      index_before=self.n_index, bias_need=self.n_bias, stage_need=self.n_stage)
        fill_pair = 1 - self.pair
        total = sum(-(-f[1] // UK) for f in fill)
        per_step = -(-total // fill_steps)
        waiting = list(fill)
        opened = []

        def scores_of(i):
            s = steps[i]
            s.s, s.i = self.n_steps, i
            self.n_steps += 1
            if s.pre is not None:
                s.before = s.pre()
            if fill and i < fill_steps + 1:
                s.bank = 2 - 2 * fill_pair
            else:
                s.bank = 0 if s.maps > 2 else 2 * (i % 2)
            s.free_when = self.take_banks(s.bank, s.maps, ("logits_ready", s.s + 1))

        scores_of(0)
        for i, s in enumerate(steps):
            if i + 1 < len(steps):
                scores_of(i + 1)
            self.fixed_pair = fill_pair
            while len(s.fill) < per_step and (waiting or opened):
                if not opened:
                    weight, k_tiles, acts, spec = waiting.pop(0)
                    opened += self.open_chunk(weight, k_tiles, acts, spec, 0).units
                s.fill.append(opened.pop(0))
            self.fixed_pair = None
            if s.flavour in ("dilated", "differential"):
                self.n_mixed += 1
                s.mixed = self.n_mixed
            for j in range(len(s.v)):
                s.tb.append(Turn(self.n_t, j, 3 if s.width == CAUSAL else 4))
                self.n_t += 1
        assert not waiting and not opened
        return ph


def plan(w):
    p = Plan()
    gains = iter(range(100))

    def ln_gain(name_g, name_b, row):
        return Gain(next(gains), (name_g, row), (name_b, row))

    def stage_gain(gain, fn, **kw):
        ph = p.stage(fn, gain=gain, **kw)
        gain.stage = ph.n
        p_gains.append(gain)
        return ph

    p_gains = []
    p.gains = p_gains

    def stage_src():
        return ("stage", p.n_stage)

    def norm_src():
        return [("stage", p.n_stage - 1), ("stage", p.n_stage)]

    def norm_src_at(gain):
        return [("stage", gain.stage - 1), ("stage", gain.stage)]

    def taken(n=None):
        return ("acc_taken_dve", p.n_taken["dve"] if n is None else n)

    def lin_copy(win, src, cols, dst0=None):
        at = cols[0][0] if dst0 is None else dst0
        p.linear(win, 8, "x", [(c, n, "copy", (src, at + c - cols[0][0])) for c, n in cols])

    g = ln_gain("mem_ln_g", "mem_ln_b", None)
    p.first_gain = g
    stage_gain(g, "mem_norm", incs=2)
    p.transpose(p.row_batches("tmp", "x", norm_src()))
    p.linear(w["w_mem_kv"][0], 8, "x", [(0, 512, "mem_kv", 0)])
    p.add("tables")
    for l in range(1, DEPTH):
        p.linear(w["w_mem_kv"][l], 8, "x", [(0, 512, "mem_kv", l)])
    p.add("save_mem_kv", dve_taken=p.n_taken["dve"])
    p.transpose(p.row_batches("x", "x", [("x_landed", 16)] * 2))

    for l in range(DEPTH):
        kind, j = l % 3, l // 3
        width = 3144 if kind == 0 else 2560
        qm = 2888 if kind == 0 else 2304
        win = (w["w_in_a"], w["w_in_b"], w["w_in_c"])[kind][j]
        src = ("U", width, 0)
        v_a = (2 * MIX, 512)
        p.add("load_mem_kv", layer=l, steps_before=p.n_steps)
        if kind == 0:
            lin_copy(win, src, [(2304, 512), (2816, 72)])
            p.stage("rope_index", src=src, layer=j)
            lin_copy(win, src, [(0, 512)])
            p.transpose(p.head_batches(src, [2304 + P * i for i in range(4)], P, "QT", 0, stage_src())
                        + p.head_batches("KI", [0], P, "KT", 0, stage_src()))
            lin_copy(win, src, [(512, 512)])
            p.add("index_scores", t_need=p.n_t, src=src, first=p.n_index, steps_before=p.n_steps)
            p.n_index += 2 * IDXH
            p.stage("top_k", src=(0, 4))
            lin_copy(win, src, [(1024, 512)])
            p.stage("top_k", src=(4, 8))
            lin_copy(win, src, [v_a])
            p.stage("rope_heads", src=src)
            lin_copy(win, src, [(2048, 256)])
            fill = [(win, 8, "x", (qm, 256, "copy", (src, qm)))]
        else:
            lin_copy(win, src, [(0, 512), (512, 512), (1024, 512)])
            p.stage("rope_heads", src=src)
            lin_copy(win, src, [v_a])
            fill = [(win, 8, "x", (2048, 512, "copy", (src, 2048)))]
            if kind == 1:
                lin_copy(win, src, [(2048, 512)])
                fill = []
        roped = ("stage", p.n_stage)
        v_now = p.n_taken["dve"]
        v_all = v_now + len(fill)
        p.transpose(p.head_batches(src, [P * i for i in range(6)], P, "QT", 0, roped)
                    + p.head_batches(src, [MIX + P * i for i in range(6)], P, "KT", 0, roped))

        def memory_tiles(l=l, src=src, qm=qm, v_all=v_all):
            return (p.head_batches(src, [qm, qm + P], P, "QT", 6, ("acc_taken_dve", v_all))
                    + p.head_batches("MKV", [0, P], P, "KT", 6, ("mem_kv_landed", 16 * (l + 1))))

        first_step = p.n_steps

        def first_half(first_step=first_step, n=4):
            return p.split_batches("tmp", 0, 4, "x", 0, ("out_taken", first_step + n))

        if kind == 1:
            steps = [Step(q=[(2 * g + b // 2, HD * (b % 2), HD) for g in range(3)],
                          k=[(2 * g + b // 2, HD * (b % 2), HD) for g in range(3)],
                          v=[(src, 2 * MIX + 192 * b)], out=192 * b, dv=192, flavour="dilated",
                          heads_out="tmp", v_taken=v_now) for b in range(4)]
        else:
            steps = [Step(q=[(i, HD * m, HD) for m in range(2)], k=[(i, HD * m, HD) for m in range(2)],
                          v=[(src, 2 * MIX + P * i + HD * m) for m in range(2)], out=P * i,
                          mask="selected" if kind == 0 else "causal", heads_out="tmp",
                          v_taken=v_now if i < 4 else v_all) for i in range(6)]
        steps += [Step(q=[(6 + i, HD * m, HD) for m in range(2)], k=[(6 + i, HD * m, HD) for m in range(2)],
                       v=[("MKV", MEMW + P * i + HD * m) for m in range(2)], out=MIX + P * i, width=FULL,
                       heads_out="tmp", pre=memory_tiles if i == 0 else None) for i in range(2)]
        late = kind != 1
        if late:
            steps[-1].pre = first_half
        p.attention(steps, fill=fill, fill_steps=4)
        p.transpose(([] if late else p.split_batches("tmp", 0, 4, "x", 0, ("out_taken", p.n_steps)))
                    + p.split_batches("tmp", 4, 4, "x", 4, ("out_taken", p.n_steps)))
        g = ln_gain("ln1_g", "ln1_b", l)
        p.linear(w["w_out"][l], 8, "x", [(c, n, "residual", c) for c, n in column_chunks(0, D)], gains=g)
        stage_gain(g, "layer_norm", incs=2)
        p.transpose(p.row_batches("x", "x", norm_src()))
        chunks, before = [], {}
        widths = column_chunks(0, FF)
        first_taken = p.n_taken["dve"]

        def h_batches(i, first_taken=first_taken):
            def make():
                return p.split_batches("H", 0, widths[i][1] // P, "h", widths[i][0] // P,
                                       ("acc_taken_dve", first_taken + i + 1))
            return make

        for i, (c, n) in enumerate(widths):
            chunks += [(c, n, "silu", ("G",)), (FF + c, n, "up", i)]
            if i:
                before[(2 * i + 1, 0)] = h_batches(i - 1)
        p.linear(w["w_gate_up"][l], 8, "x", chunks, before)
        g = ln_gain("ln2_g", "ln2_b", l)
        k_last = widths[-1][0] // P
        p.linear(w["w_down"][l], FF // P, "h", [(c, n, "residual", c) for c, n in column_chunks(0, D)],
                 {(0, k_last // UK): h_batches(len(widths) - 1)}, gains=g)
        stage_gain(g, "layer_norm", incs=2)
        if l < DEPTH - 1:
            p.transpose(p.row_batches("x", "x", norm_src()))

    p.block = 2
    da, low, qm, kvm = ("U", 2048, 0), ("U", 928, 4096), ("U", 768, 0), ("U", 1024, 1536)
    sw, sw_z, sw_k = ("U", 768, 5952), ("U", 512, 1536), ("U", 256, 2560)
    ple_rows, ple_out = ("U", 256, 3072), ("U", D, 0)
    for l in range(DEPTH_2):
        win = w["w_in_2"][l]
        g = ln_gain("norm_pre_2", None, l)
        p.units[-1].late_gain = g
        stage_gain(g, "rms_pre", incs=2)
        p.transpose(p.row_batches("tmp", "x", norm_src()))

        def gate(i):
            return [(C_G + D * i + c, n, "sigmoid", ("tmp", D, c)) for c, n in column_chunks(0, D)]

        def branch(weight, mixed, first, between=()):
            p.transpose(p.split_batches(mixed, 0, 4, "s", 0, stage_src()))
            for fn, kw in between:
                p.stage(fn, **kw)
            p.linear(weight[l], 4, "s", [(c, n, "branch_first" if first else "branch", c)
                                         for c, n in column_chunks(0, D)])

        p.add("load_bias", head=0, heads=DA_H, steps_before=p.n_steps)
        p.n_bias += 32 + (16 if l == 0 else 0)
        n = p.n_taken["dve"]
        lin_copy(win, da, [(0, 512), (512, 512), (1024, 512)])
        p.transpose(p.head_batches(da, [P * i for i in range(4)], P, "QT", 0, taken(n + 1))
                    + p.head_batches(da, [512 + P * i for i in range(4)], P, "KT", 0, taken(n + 2)))
        steps = [Step(q=[(i, HD * m, HD) for m in range(2)], k=[(i, HD * m, HD) for m in range(2)],
                      v=[(da, 1024 + P * i)], out=P * i, dv=P, flavour="differential", mask="bias",
                      heads_out=da, v_taken=n + 3, bias_row=i) for i in range(4)]
        p.attention(steps, layer=l, fill_steps=4,
                    fill=[(win, 8, "x", (C_AZ, 512, "silu", (da, C_AZ))),
                          (win, 8, "x", (C_BQ, 416, "copy", (low, 0))),
                          (win, 8, "x", (C_BZ, 512, "silu", (low, 416)))])
        p.stage("sub_norm", src=da, layer=l)
        p.linear(win, 8, "x", gate(0))
        branch(w["w_br_a_2"], da, True, [("latent_norm", dict(src=low, layer=l))])

        p.transpose(p.split_batches(low, 0, 2, "s", 0, stage_src()) + p.split_batches(low, 2, 1, "s", 2, stage_src()))
        p.linear(w["mla_w_qb_2"][l], 2, "s", [(c, n, "copy", (qm, c)) for c, n in column_chunks(0, 768)])
        p.linear(w["mla_w_kvb_2"][l], 1, "s2", [(c, n, "copy", (kvm, c)) for c, n in column_chunks(0, 1024)])
        p.stage("latent_rope_q", src=qm, low=low)
        lin_copy(win, sw, [(C_CQ, 512)], 0)
        p.transpose(p.head_batches(qm, [MLA_K * i for i in range(8)], MLA_K, "QT", 0, stage_src()))
        p.stage("latent_keys", src=kvm, low=low, dst=qm, t_need=p.n_t)
        lin_copy(win, sw, [(C_CQ + 512, 256)], 512)
        p.transpose(p.head_batches(qm, [MLA_K * i for i in range(8)], MLA_K, "KT", 0, stage_src()))
        steps = [Step(q=[(2 * i + m, 0, MLA_K) for m in range(2)], k=[(2 * i + m, 0, MLA_K) for m in range(2)],
                      v=[(kvm, P * (2 * i + m) + HD) for m in range(2)], out=P * i, scale=MLA_SCALE,
                      mask="causal", heads_out=qm) for i in range(4)]
        p.attention(steps, layer=l, fill_steps=4, fill=[(win, 8, "x", c) for c in gate(1)])
        p.stage("gate_mixed", src=qm, z=(low, 416))
        p.stage("twice_keys", src=sw, dst=sw_k)
        keys_twice = stage_src()
        p.linear(win, 8, "x", [(C_CZ, 512, "silu", (sw_z, 0))])
        branch(w["w_br_b_2"], qm, False)

        p.add("load_bias", head=DA_H, heads=SW_H, steps_before=p.n_steps)
        p.n_bias += 32
        p.transpose(p.head_batches(sw, [P * i for i in range(4)], P, "QT", 0, keys_twice)
                    + p.head_batches(sw_k, [0, P], P, "KT", 0, keys_twice))
        steps = [Step(q=[(i, HD * m, HD) for m in range(2)], k=[(i // 2, HD * m, HD) for m in range(2)],
                      v=[(sw, 640 + HD * (i // 2)) for m in range(2)], out=P * i, flavour="sinks",
                      mask="bias", heads_out=sw, bias_row=2 * i) for i in range(4)]
        p.attention(steps, layer=l, fill_steps=4, fill=[(win, 8, "x", c) for c in gate(2)])
        p.add("load_ple", layer=l)
        p.stage("gate_mixed", src=sw, z=(sw_z, 0))
        branch(w["w_br_c_2"], sw, False)

        p.transpose(p.split_batches("Y", 0, 8, "x", 0, taken())
                    + p.split_batches(ple_rows, 0, 2, "s", 0, ("ple_landed", 16 * (l + 1))))
        g = ln_gain("norm_post_2", None, l)
        p.linear(w["w_out_2"][l], 8, "x", [(c, n, "copy", (("tmp", D, 0), c)) for c, n in column_chunks(0, D)],
                 gains=g)
        stage_gain(g, "rms_post", incs=2)
        p.linear(w["w_ple_proj_2"][l], 2, "s", [(c, n, "copy", (ple_out, c)) for c, n in column_chunks(0, D)])
        p.transpose(p.row_batches("x", "x", norm_src_at(g)))
        for c, n in column_chunks(0, D):
            p.linear(w["w_ple_gate_2"][l], 8, "x", [(c, n, "sigmoid", ("tmp", D, c))])
        for i, (c, n) in enumerate(column_chunks(0, D)):
            p.stage("ple_add", src=ple_out, dst=(c, n), act_need=p.n_taken["act"] - 1 + i)
    return p


def build(nc, a, out):
    p = plan(a)
    rel_rows = nc.dram_tensor("rel_rows", [BIAS_HEADS, P, REL_ROW], F32, kind="Internal").ap()
    mem_kv = nc.dram_tensor("mem_kv", [DEPTH, P, T * 512], F32, kind="Internal").ap()
    gain_list = p.gains

    with ExitStack() as ctx:
        def sb(name, shape, dt=F32):
            return ctx.enter_context(nc.sbuf_tensor(name, shape, dt))

        def sem(name):
            return ctx.enter_context(nc.semaphore(name))

        raw = sb("raw", [P, RAW, UK, CHUNK])
        w_hi = sb("w_hi", [P, SPLIT, UK, CHUNK], F32R)
        w_lo = sb("w_lo", [P, SPLIT, UK, CHUNK], F32R)
        xT_hi = sb("xT_hi", [P, 8, N], F32R)
        xT_lo = sb("xT_lo", [P, 8, N], F32R)
        x = sb("x_rows", [P, T, D])
        tmp = sb("tmp", [P, T * D])
        gain = sb("gain", [P, 2, 2, D])
        ident = sb("ident", [P, P])
        knorm = sb("knorm", [P, 2, 2, HD])
        subln = sb("subln", [P, 2, P])
        qnorm = sb("qnorm", [P, 2, 256])
        kvnorm = sb("kvnorm", [P, 2, P])
        sinks = sb("sinks", [P, 2, SW_H])
        neg_sinks = sb("neg_sinks", [P, 2, SW_H])
        neg_lam = sb("neg_lam", [P, 2])
        trig = sb("trig", [P, 2, T, 24])
        stats = sb("stats", [P, T, 2, 6])
        small = sb("small", [P, 10, 16])
        neg_max = sb("neg_max", [P, 2, 4])
        sums = sb("sums", [P, 2, 4])
        sink_exp = sb("sink_exp", [P, 2, 4])
        recips = sb("recips", [P, 2, 4])

        att = ExitStack()
        with att:
            def sba(name, shape, dt=F32):
                return att.enter_context(nc.sbuf_tensor(name, shape, dt))
            U = sba("U", [P, 7488])
            QT = sba("QT", [P, 8, N])
            KT = sba("KT", [P, 8, N])
            L = sba("L", [P, 2 * 3 * CAUSAL])
            PT = sba("PT", [P, 2, 512])
        ffn = ExitStack()
        with ffn:
            hT_hi = ffn.enter_context(nc.sbuf_tensor("hT_hi", [P, FF // P, N], F32R))
            hT_lo = ffn.enter_context(nc.sbuf_tensor("hT_lo", [P, FF // P, N], F32R))
            G = ffn.enter_context(nc.sbuf_tensor("G", [P, T, CHUNK], F32))
            H = ffn.enter_context(nc.sbuf_tensor("H", [P, T, CHUNK], F32))
        ctx.enter_context(nc.sbuf_tensor("attention_or_ffn", [P, 7488 + 4096 + 6 * CAUSAL + 1024], F32))
        first = ExitStack()
        with first:
            masks = first.enter_context(nc.sbuf_tensor("masks", [P, 4, CAUSAL], F32))
            selected = first.enter_context(nc.sbuf_tensor("selected", [P, CAUSAL], F32))
            scores = first.enter_context(nc.sbuf_tensor("scores", [P, CAUSAL], F32))
            MKV = first.enter_context(nc.sbuf_tensor("MKV", [P, T * 512], F32))
            KI = first.enter_context(nc.sbuf_tensor("KI", [P, T * P], F32))
        second = ExitStack()
        with second:
            causal_2 = second.enter_context(nc.sbuf_tensor("causal_2", [P, CAUSAL], F32))
            bias = second.enter_context(nc.sbuf_tensor("bias", [P, SW_H, CAUSAL], F32))
        ctx.enter_context(nc.sbuf_tensor("first_or_second", [P, 4 * CAUSAL + 2 * CAUSAL + T * 512 + T * P], F32))
        sT_hi = ctx.enter_context(nc.sbuf_tensor("sT_hi", [P, 4, N], F32R))
        sT_lo = ctx.enter_context(nc.sbuf_tensor("sT_lo", [P, 4, N], F32R))

        acc = ctx.enter_context(nc.psum_tensor("acc", [P, 4, 512], F32))
        tps = ctx.enter_context(nc.psum_tensor("tps", [P, 2, 512], F32))
        ops = ctx.enter_context(nc.psum_tensor("ops", [P, 2, 512], F32))

        S = {n: sem(n) for n in (
            "ident_landed", "prologue_landed", "x_landed", "mem_landed", "lambda_terms", "lambda_exp", "angles",
            "trig_done", "rel_ready", "rel_rows_made", "rel_rows_saved", "mem_kv_saved",
            "mem_kv_landed", "bias_landed", "ple_landed", "out_landed", "hi_ready", "lo_ready",
            "unit_used", "acc_taken_dve", "acc_taken_act", "t_ready", "t_hi", "t_taken", "stage",
            "scores_ready", "logits_ready", "max_ready", "probs_ready", "mixed_ready", "pv_ready",
            "out_taken", "dve_chain", "act_chain", "index_ready", "index_relu", "index_added")}
        unit_landed = [sem(f"unit_landed{i}") for i in range(RAW)]
        gain_landed = [sem(f"gain_landed{i}") for i in range(2)]

        block = ctx.enter_context(nc.Block())

        def rows(src):
            if src == "x":
                return x[:]
            if src == "tmp":
                return tmp[:].rearrange("p (t c) -> p t c", t=T)
            if src == "H":
                return H[:]
            if src == "Y":
                return gain[:, :, 1, :]
            if src == "KI":
                return KI[:].rearrange("p (t c) -> p t c", t=T)
            if src == "MKV":
                return MKV[:].rearrange("p (t c) -> p t c", t=T)
            name, cols, off = src
            buf = {"U": U, "tmp": tmp}[name]
            if name == "tmp":
                off = 0
            return buf[:, off:off + T * cols].rearrange("p (t c) -> p t c", t=T)

        def act_split(name):
            return {"x": (xT_hi, xT_lo, 0), "h": (hT_hi, hT_lo, 0), "s": (sT_hi, sT_lo, 0),
                    "s2": (sT_hi, sT_lo, 2)}[name]

        def batch_dst(b, buf):
            _, d0, m, width, t = b.dst
            if t is None:
                return buf[0:width, d0:d0 + m, :].rearrange("p k n -> p (k n)")
            return buf[0:width, d0:d0 + m, P * t:P * t + P]

        def batch_src(b):
            _, _, m, width, t = b.dst
            if t is None:
                return tps[0:width, b.b % 2, 0:m * N]
            return tps[0:width, b.b % 2, 0:m * P].rearrange("p (k n) -> p k n", k=m)

        def step_logits(s):
            off = 3 * CAUSAL * (s.s % 2)
            return L[:, off:off + s.maps * s.width].rearrange("p (m c) -> p m c", m=s.maps)

        def tile_cols(s, t):
            if s.width == FULL:
                return slice(256 * t, 256 * t + 256)
            return slice(0, P) if t == 0 else slice(P, CAUSAL)

        def token_col(v):
            return v.rearrange("o (t p) -> p (o t)", p=P)

        PRO = [
            (masks[:], a["c_masks"]),
            (knorm[:, :, 0, :], a["idx_kn_g"].partition_broadcast(P)),
            (knorm[:, :, 1, :], a["idx_kn_b"].partition_broadcast(P)),
            (subln[:], a["da_subln_2"].partition_broadcast(P)),
            (qnorm[:], a["mla_q_norm_2"].partition_broadcast(P)),
            (kvnorm[:], a["mla_kv_norm_2"].partition_broadcast(P)),
            (sinks[:], a["sw_sinks_2"].partition_broadcast(P)),
            (L[:, 0:512], a["da_lambda_2"].rearrange("l f d -> (l f d)").partition_broadcast(P)),
            (L[:, 512:536], a["c_inv"]),
            (L[:, 536:538].bitcast(I32), token_col(a["positions"])),
            (L[:, 538:540].bitcast(I32), token_col(a["positions_2"])),
            (L[0:REL_BUCKETS, 1024:1024 + BIAS_HEADS], a["rel_bias_2"]),
            (L[0:REL_BUCKETS, 1152:1152 + REL_ROW], a["c_onehot"]),
            (L[0:BIAS_HEADS, 1536:1536 + REL_ROW], a["c_relmask"]),
        ]

        @block.sync
        def _(sp):
            def load_gain(g):
                slot = g.j % 2
                if g.j >= 2:
                    sp.wait_ge(S["stage"], gain_list[g.j - 2].stage)
                name, row = g.g
                src = a[name] if row is None else a[name][row]
                sp.dma_start(gain[:, slot, 0, :], src.partition_broadcast(P)).then_inc(gain_landed[slot], 16)
                if g.b[0]:
                    name, row = g.b
                    src = a[name] if row is None else a[name][row]
                    sp.dma_start(gain[:, slot, 1, :], src.partition_broadcast(P)).then_inc(gain_landed[slot], 16)

            sp.dma_start(rows("tmp"), a["mem"][0].rearrange("(t p) d -> p t d", p=P)).then_inc(S["mem_landed"], 16)
            load_gain(p.first_gain)
            for u in p.units:
                if u.u >= RAW:
                    sp.wait_ge(S["lo_ready"], u.u - RAW + 1)
                ch = u.chunk
                src = u.weight[u.k0 * P:(u.k0 + u.nk) * P, ch.col:ch.col + ch.width]
                sp.dma_start(raw[:, u.u % RAW, 0:u.nk, 0:ch.width],
                             src.rearrange("(k p) n -> p k n", p=P)).then_inc(unit_landed[u.u % RAW], 16)
                if u.u == RAW - 1:
                    sp.dma_start(x[:], a["x"][0].rearrange("(t p) d -> p t d", p=P)).then_inc(S["x_landed"], 16)
                if u.gain is not None:
                    load_gain(u.gain)
                if u.late_gain is not None:
                    load_gain(u.late_gain)
            sp.wait_ge(S["stage"], p.n_stage)
            sp.dma_start(out[0].rearrange("(t p) d -> p t d", p=P), x[:]).then_inc(S["out_landed"], 16)
            sp.wait_ge(S["out_landed"], 16)

        @block.gpsimd
        def _(pool):
            for u in p.units:
                ch, slot, r = u.chunk, u.u % SPLIT, u.u % RAW
                pool.wait_ge(S["hi_ready"], u.u + 1)
                if u.u:
                    pool.wait_ge(S["lo_ready"], u.u)
                nc.gpsimd.tensor_tensor(w_lo[:, slot, 0:u.nk, 0:ch.width], raw[:, r, 0:u.nk, 0:ch.width],
                                        w_hi[:, slot, 0:u.nk, 0:ch.width].bitcast(F32),
                                        ALU.subtract).then_inc(S["lo_ready"], 1)

        @block.scalar
        def _(act):
            def split_unit(n):
                if n >= len(p.units):
                    return
                u = p.units[n]
                act.wait_ge(unit_landed[n % RAW], 16 * (n // RAW + 1))
                if n >= SPLIT:
                    act.wait_ge(S["unit_used"], n - SPLIT + 1)
                nc.scalar.copy(w_hi[:, n % SPLIT, 0:u.nk, 0:u.chunk.width],
                               raw[:, n % RAW, 0:u.nk, 0:u.chunk.width]).then_inc(S["hi_ready"], 1)

            def batch_hi(b):
                act.wait_ge(S["t_ready"], b.b + 1)
                hi, _, _ = act_split(b.dst[0])
                nc.scalar.copy(batch_dst(b, hi), batch_src(b)).then_inc(S["t_hi"], 1)

            act.dma_start(ident[:], a["c_ident"]).then_inc(S["ident_landed"], 16)
            with nc.allow_non_contiguous_dma(reason="the positions, one to a partition"):
                for dst, src in PRO:
                    act.dma_start(dst, src).then_inc(S["prologue_landed"], 16)
            for n in range(AHEAD):
                split_unit(n)
            bias_loads = 0

            def take_chunk(ch):
                act.wait_ge(S["unit_used"], ch.last + 1)
                act.wait_ge(S["stage"], ch.stage_before)
                if ch.how == "silu":
                    fn = ACT.Silu
                    if ch.dst[0] == "G":
                        dst = G[:, :, 0:ch.width]
                        if ch.index:
                            act.wait_ge(S["acc_taken_dve"], ch.dve_taken_before)
                    else:
                        src, col = ch.dst
                        dst = rows(src)[:, :, col:col + ch.width]
                else:
                    fn = ACT.Sigmoid
                    _, _, col = ch.dst
                    dst = rows("tmp")[:, :, col:col + ch.width]
                    act.wait_ge(S["acc_taken_dve"], ch.dve_taken_before)
                nc.scalar.activation(dst, acc[:, ch.bank:ch.bank + 2, 0:ch.width], fn).then_inc(S["acc_taken_act"], 1)

            def after_unit(u):
                split_unit(u.u + AHEAD)
                if u.u == u.chunk.last and u.chunk.eng == "act":
                    take_chunk(u.chunk)

            def exponentials(s):
                lg, slot = step_logits(s), s.s % 2
                act.wait_ge(S["max_ready"], s.s + 1)
                if s.flavour == "sinks":
                    nc.scalar.activation(sink_exp[:, slot, :], sink_exp[:, slot, :], ACT.Exp)
                for m in range(1 if s.flavour == "dilated" else s.maps):
                    for t in range(T):
                        part = lg[:, :, tile_cols(s, t)] if s.flavour == "dilated" else lg[:, m, tile_cols(s, t)]
                        c = 2 * m + t
                        ins = nc.scalar.activation(part, part, ACT.Exp, bias=neg_max[:, slot, c:c + 1],
                                                   accum_out=sums[:, slot, c:c + 1])
                ins.then_inc(S["probs_ready"], 1)

            for ph in p.phases:
                if ph.kind == "linear":
                    for ch in ph.chunks:
                        for u in ch.units:
                            for b in u.pre:
                                batch_hi(b)
                            after_unit(u)
                elif ph.kind == "tables":
                    act.wait_ge(S["lambda_terms"], 1)
                    nc.scalar.activation(small[:, 0, 4:8], small[:, 0, 0:4], ACT.Exp).then_inc(S["lambda_exp"], 1)
                    act.wait_ge(S["angles"], 1)
                    nc.scalar.activation(trig[:].rearrange("p s t f -> p (s t f)"), L[:, 640:736],
                                         ACT.Sin).then_inc(S["trig_done"], 1)
                    act.wait_ge(S["rel_rows_made"], 1)
                    act.dma_start(rel_rows, L[0:BIAS_HEADS, 1152:1152 + REL_ROW].unsqueeze(1)
                                  .to_broadcast([BIAS_HEADS, P, REL_ROW])).then_inc(S["rel_rows_saved"], 16)
                elif ph.kind == "transpose":
                    for b in ph.batches:
                        if b.split:
                            batch_hi(b)
                elif ph.kind == "save_mem_kv":
                    act.wait_ge(S["acc_taken_dve"], ph.dve_taken)
                    for l in range(DEPTH):
                        act.dma_start(mem_kv[l], U[:, 1024 * l:1024 * l + 1024]).then_inc(S["mem_kv_saved"], 16)
                elif ph.kind == "load_mem_kv":
                    if ph.layer == 0:
                        act.wait_ge(S["mem_kv_saved"], 16 * DEPTH)
                    else:
                        act.wait_ge(S["pv_ready"], ph.steps_before)
                    act.dma_start(MKV[:], mem_kv[ph.layer]).then_inc(S["mem_kv_landed"], 16)
                elif ph.kind == "load_bias":
                    act.wait_ge(S["logits_ready"], ph.steps_before)
                    act.wait_ge(S["pv_ready"], ph.steps_before)
                    if bias_loads == 0:
                        act.wait_ge(S["rel_rows_saved"], 16)
                        act.dma_start(causal_2[:], a["c_masks"][:, 0, :]).then_inc(S["bias_landed"], 16)
                    bias_loads += 1
                    for off, lo, n in ((255, 0, P), (127, P, N)):
                        src = bass.AP(rel_rows.tensor, off + P * REL_ROW * ph.head,
                                      [[REL_ROW - 1, P], [P * REL_ROW, ph.heads], [1, n]])
                        act.dma_start(bias[:, 0:ph.heads, lo:lo + n], src).then_inc(S["bias_landed"], 16)
                elif ph.kind == "load_ple":
                    act.dma_start(rows(("U", 256, 3072)), a["p_2"][ph.layer, 0].rearrange("(t p) d -> p t d", p=P)
                                  ).then_inc(S["ple_landed"], 16)
                elif ph.kind == "index_scores":
                    for i in range(2 * IDXH):
                        n = ph.first + i
                        t = i // IDXH
                        act.wait_ge(S["index_ready"], n + 1)
                        if n >= 2:
                            act.wait_ge(S["index_added"], n - 1)
                        w = P * (t + 1)
                        nc.scalar.activation(L[:, 512 * (n % 2):512 * (n % 2) + w], ops[:, n % 2, 0:w],
                                             ACT.Relu).then_inc(S["index_relu"], 1)
                elif ph.kind == "attention":
                    for s in ph.steps:
                        if s.i + 1 < len(ph.steps):
                            for b in ph.steps[s.i + 1].before:
                                if b.split:
                                    batch_hi(b)
                        exponentials(s)
                        for u in s.fill:
                            after_unit(u)

        @block.tensor
        def _(pe):
            def do_batch(b):
                if b.b >= 2:
                    pe.wait_ge(S["t_taken"], b.b - 1)
                pe.wait_ge(S[b.after[0]], b.after[1])
                for i, (src, t, col, width) in enumerate(b.moves):
                    ins = nc.tensor.transpose(tps[0:width, b.b % 2, P * i:P * i + P],
                                              rows(src)[:, t, col:col + width], ident[:])
                ins.then_inc(S["t_ready"], 1)

            def do_unit(u):
                ch = u.chunk
                if u.k0 == 0:
                    for name, count in ch.free_when:
                        pe.wait_ge(S[name], count)
                for b in u.pre:
                    do_batch(b)
                pe.wait_ge(S["t_taken"], u.t_need)
                pe.wait_ge(S["lo_ready"], u.u + 1)
                hi, lo, off = act_split(ch.acts)
                slot = u.u % SPLIT
                for k in range(u.nk):
                    kt = off + u.k0 + k
                    first_k, last_k = u.k0 + k == 0, u.k0 + k == ch.k_tiles - 1
                    for t in range(T):
                        o = acc[:, ch.bank + t, 0:ch.width]
                        tok = slice(P * t, P * t + P)
                        wh, wl = w_hi[:, slot, k, 0:ch.width], w_lo[:, slot, k, 0:ch.width]
                        nc.tensor.matmul(o, hi[:, kt, tok], wh, start=first_k, stop=False)
                        nc.tensor.matmul(o, hi[:, kt, tok], wl, start=False, stop=False)
                        ins = nc.tensor.matmul(o, lo[:, kt, tok], wh, start=False, stop=last_k)
                ins.then_inc(S["unit_used"], 1)

            def do_scores(s):
                for b in s.before:
                    do_batch(b)
                if s.before:
                    pe.wait_ge(S["t_taken"], s.before[-1].b + 1)
                for name, count in s.free_when:
                    pe.wait_ge(S[name], count)
                for m in range(s.maps):
                    (qt, base, k), (kt, kbase, _) = s.q[m], s.k[m]
                    for t in range(T):
                        c = tile_cols(s, t)
                        ins = nc.tensor.matmul(acc[:, s.bank + m, c], QT[base:base + k, qt, P * t:P * t + P],
                                               KT[kbase:kbase + k, kt, 0:c.stop - c.start],
                                               start=True, stop=True)
                ins.then_inc(S["scores_ready"], 1)

            def turn(s):
                lg = step_logits(s)
                if s.mixed:
                    pe.wait_ge(S["mixed_ready"], s.mixed)
                else:
                    pe.wait_ge(S["probs_ready"], s.s + 1)
                for tb in s.tb:
                    pe.wait_ge(S["t_taken"], tb.b - 1)
                    for i in range(tb.blocks):
                        ins = nc.tensor.transpose(tps[:, tb.b % 2, P * i:P * i + P],
                                                  lg[:, tb.j, P * i:P * i + P], ident[:])
                    ins.then_inc(S["t_ready"], 1)

            def do_values(s):
                if s.s >= 2:
                    pe.wait_ge(S["out_taken"], s.s - 1)
                if s.v_taken:
                    pe.wait_ge(S["acc_taken_dve"], s.v_taken)
                for tb, (src, col) in zip(s.tb, s.v):
                    pe.wait_ge(S["t_taken"], tb.b + 1)
                    for t in range(T):
                        o0 = (tb.j * T + t) * s.dv
                        keys = range(T) if s.width == FULL else range(t + 1)
                        for kt in keys:
                            blk = tile_cols(s, t).start + P * kt
                            ins = nc.tensor.matmul(ops[:, s.s % 2, o0:o0 + s.dv], PT[:, tb.j, blk:blk + P],
                                                   rows(src)[:, kt, col:col + s.dv],
                                                   start=kt == 0, stop=kt == keys[-1])
                ins.then_inc(S["pv_ready"], 1)

            pe.wait_ge(S["ident_landed"], 16)
            for ph in p.phases:
                if ph.kind == "transpose":
                    for b in ph.batches:
                        do_batch(b)
                elif ph.kind == "linear":
                    for ch in ph.chunks:
                        for u in ch.units:
                            do_unit(u)
                elif ph.kind == "tables":
                    pe.wait_ge(S["prologue_landed"], 16 * len(PRO))
                    nc.tensor.matmul(ops[0:BIAS_HEADS, 0, 0:REL_ROW], L[0:REL_BUCKETS, 1024:1024 + BIAS_HEADS],
                                     L[0:REL_BUCKETS, 1152:1152 + REL_ROW], start=True, stop=True
                                     ).then_inc(S["rel_ready"], 1)
                elif ph.kind == "index_scores":
                    pe.wait_ge(S["t_taken"], ph.t_need)
                    pe.wait_ge(S["rel_rows_made"], 1)
                    if ph.steps_before:
                        pe.wait_ge(S["out_taken"], ph.steps_before)
                    for i in range(2 * IDXH):
                        n = ph.first + i
                        t, h = i // IDXH, i % IDXH
                        base = HD * (h % 2)
                        if n >= 2:
                            pe.wait_ge(S["index_relu"], n - 1)
                        w = P * (t + 1)
                        nc.tensor.matmul(ops[:, n % 2, 0:w], QT[base:base + HD, h // 2, P * t:P * t + P],
                                         KT[base:base + HD, 0, 0:w], start=True, stop=True
                                         ).then_inc(S["index_ready"], 1)
                elif ph.kind == "attention":
                    pe.wait_ge(S["t_taken"], ph.t_need)
                    if ph.index_before:
                        pe.wait_ge(S["index_relu"], ph.index_before)
                    do_scores(ph.steps[0])
                    for s in ph.steps:
                        if s.i + 1 < len(ph.steps):
                            do_scores(ph.steps[s.i + 1])
                        if s.i:
                            do_values(ph.steps[s.i - 1])
                        for u in s.fill:
                            do_unit(u)
                        turn(s)
                    do_values(ph.steps[-1])

        @block.vector
        def _(dve):
            v = nc.vector
            chain = [0]

            def link(ins):
                chain[0] += 1
                ins.then_inc(S["dve_chain"], 1)
                dve.wait_ge(S["dve_chain"], chain[0])

            def rsqrt(y, var, n):
                a1, a2 = small[:, 8, 0:n], small[:, 9, 0:n]
                link(v.tensor_scalar(a1.bitcast(I32), var.bitcast(I32), 1, None, ALU.logical_shift_right))
                link(v.tensor_scalar(y.bitcast(I32), a1.bitcast(I32), -1.0, float(0x5F3759DF), ALU.mult, ALU.add))
                for _ in range(3):
                    link(v.tensor_tensor(a1, y, y, ALU.mult))
                    link(v.scalar_tensor_tensor(out=a2, in0=a1, scalar=-0.5, in1=var, op0=ALU.mult, op1=ALU.mult))
                    link(v.scalar_tensor_tensor(out=y, in0=a2, scalar=1.5, in1=y, op0=ALU.add, op1=ALU.mult))

            def norm_rows(src, dst, g, width, eps, done=None):
                mv, rs = small[:, 1, 0:4], small[:, 2, 0:2]
                for t in range(T):
                    ins = v.bn_aggr(mv[:, 2 * t:2 * t + 2], stats[:, t, 0:-(-width // 512), :])
                link(ins)
                var = small[:, 3, 0:2]
                link(v.tensor_scalar(var, mv[:, 1:4:2], eps, None, ALU.add))
                rsqrt(rs, var, 2)
                gg, bb = g
                for t in range(T):
                    link(v.scalar_tensor_tensor(out=src[:, t, :], in0=src[:, t, :], scalar=mv[:, 2 * t:2 * t + 1],
                                                in1=gg, op0=ALU.subtract, op1=ALU.mult))
                    ins = v.scalar_tensor_tensor(out=dst[:, t, :], in0=src[:, t, :], scalar=rs[:, t:t + 1],
                                                 in1=bb, op0=ALU.mult, op1=ALU.add)
                    if done is None:
                        link(ins)
                    else:
                        ins.then_inc(done, 1)

            def rms_rows(src, dst, g, width, done=None):
                ms, rs = small[:, 1, 0:2], small[:, 2, 0:2]
                for t in range(T):
                    ins = v.tensor_tensor_reduce(out=L[:, 0:width], in0=src[:, t, :], in1=src[:, t, :],
                                                 scale=1.0, scalar=0.0, op0=ALU.mult, op1=ALU.add,
                                                 accum_out=ms[:, t:t + 1])
                    link(ins)
                link(v.tensor_scalar(small[:, 3, 0:2], ms, 1.0 / width, RMS_EPS, ALU.mult, ALU.add))
                rsqrt(rs, small[:, 3, 0:2], 2)
                for t in range(T):
                    ins = v.scalar_tensor_tensor(out=dst[:, t, :], in0=src[:, t, :], scalar=rs[:, t:t + 1],
                                                 in1=g, op0=ALU.mult, op1=ALU.mult)
                    if done is None:
                        link(ins)
                    else:
                        ins.then_inc(done, 1)

            def rope(heads, n, f0, half, out=None):
                x1, x2 = heads[:, :, :, 0:half], heads[:, :, :, half:2 * half]
                size = T * n * half
                cs = trig[:, 1, :, f0:f0 + half].unsqueeze(2).to_broadcast([P, T, n, half])
                sn = trig[:, 0, :, f0:f0 + half].unsqueeze(2).to_broadcast([P, T, n, half])
                tm = [L[:, i * size:(i + 1) * size].rearrange("p (t n f) -> p t n f", t=T, n=n) for i in range(4)]
                v.tensor_tensor(tm[0], x1, cs, ALU.mult)
                v.tensor_tensor(tm[1], x2, sn, ALU.mult)
                v.tensor_tensor(tm[2], x2, cs, ALU.mult)
                link(v.tensor_tensor(tm[3], x1, sn, ALU.mult))
                v.tensor_tensor(x1, tm[0], tm[1], ALU.subtract)
                link(v.tensor_tensor(x2, tm[2], tm[3], ALU.add))

            def tables():
                dve.wait_ge(S["prologue_landed"], 16 * len(PRO))
                lf = L[:, 0:512].rearrange("p (l f d) -> p l f d", l=2, f=4)
                pr = L[:, 768:1024].rearrange("p (l f d) -> p l f d", l=2, f=2)
                link(v.tensor_tensor(pr, lf[:, :, 0:4:2, :], lf[:, :, 1:4:2, :], ALU.mult))
                v.tensor_reduce(small[:, 0, 0:4], pr.rearrange("p l f d -> p (l f) d"), AX.X,
                                ALU.add).then_inc(S["lambda_terms"], 1)
                link(v.tensor_copy(L[:, 540:544], L[:, 536:540].bitcast(I32)))
                ang = L[:, 544:592].rearrange("p (t f) -> p t f", t=T)
                for t in range(T):
                    v.tensor_scalar(ang[:, t, 0:8], L[:, 512:520], L[:, 540 + t:541 + t], None, ALU.mult)
                    ins = v.tensor_scalar(ang[:, t, 8:24], L[:, 520:536], L[:, 542 + t:543 + t], None, ALU.mult)
                link(ins)
                n_turn, r = L[:, 592:640], L[:, 640:736]
                angf = L[:, 544:592]
                for i, quarter in enumerate((0.0, 0.25)):
                    rr = r[:, 48 * i:48 * i + 48]
                    link(v.tensor_scalar(n_turn, angf, 1 / (2 * math.pi), quarter, ALU.mult, ALU.add))
                    link(v.tensor_scalar(n_turn, n_turn, ROUND, None, ALU.add))
                    link(v.tensor_scalar(n_turn, n_turn, ROUND, None, ALU.subtract))
                    link(v.scalar_tensor_tensor(out=rr, in0=n_turn, scalar=-TWO_PI_1, in1=angf, op0=ALU.mult, op1=ALU.add))
                    link(v.scalar_tensor_tensor(out=rr, in0=n_turn, scalar=-TWO_PI_2, in1=rr, op0=ALU.mult, op1=ALU.add))
                    link(v.scalar_tensor_tensor(out=rr, in0=n_turn, scalar=-TWO_PI_3, in1=rr, op0=ALU.mult, op1=ALU.add))
                    if i:
                        link(v.tensor_scalar(rr, rr, math.pi / 2, None, ALU.add))
                v.tensor_scalar(r, r, PI_INSIDE, -PI_INSIDE, ALU.min, ALU.max).then_inc(S["angles"], 1)
                link(v.tensor_scalar(neg_sinks[:], sinks[:], -1.0, None, ALU.mult))
                dve.wait_ge(S["rel_ready"], 1)
                v.tensor_tensor(L[0:BIAS_HEADS, 1152:1152 + REL_ROW], ops[0:BIAS_HEADS, 0, 0:REL_ROW],
                                L[0:BIAS_HEADS, 1536:1536 + REL_ROW], ALU.add).then_inc(S["rel_rows_made"], 1)
                dve.wait_ge(S["lambda_exp"], 1)
                for l in range(DEPTH_2):
                    lam_init = 0.8 - 0.6 * math.exp(-0.3 * l)
                    link(v.tensor_tensor(small[:, 0, 8 + l:9 + l], small[:, 0, 5 + 2 * l:6 + 2 * l],
                                         small[:, 0, 4 + 2 * l:5 + 2 * l], ALU.subtract))
                    link(v.tensor_scalar(neg_lam[:, l:l + 1], small[:, 0, 8 + l:9 + l], lam_init, None, ALU.subtract))
                dve.wait_ge(S["trig_done"], 1)
                dve.wait_ge(S["rel_rows_saved"], 16)

            gain_count = [0, 0]

            def gains(g):
                slot = g.j % 2
                gain_count[slot] += 32 if g.b[0] else 16
                dve.wait_ge(gain_landed[slot], gain_count[slot])
                return gain[:, slot, 0, :], gain[:, slot, 1, :]

            def take_batch(b):
                ps = batch_src(b)
                if b.split:
                    hi, lo, _ = act_split(b.dst[0])
                    dve.wait_ge(S["t_hi"], b.hi)
                    ins = v.tensor_tensor(batch_dst(b, lo), ps, batch_dst(b, hi).bitcast(F32), ALU.subtract)
                else:
                    dve.wait_ge(S["t_ready"], b.b + 1)
                    ins = v.tensor_copy(batch_dst(b, {"QT": QT, "KT": KT}[b.dst[0]]), ps)
                ins.then_inc(S["t_taken"], 1)

            def take_chunk(ch):
                ps = acc[:, ch.bank:ch.bank + 2, 0:ch.width]
                dve.wait_ge(S["unit_used"], ch.last + 1)
                dve.wait_ge(S["stage"], ch.stage_before)
                if ch.how == "copy":
                    if not saved[0]:
                        saved[0] = True
                        dve.wait_ge(S["mem_kv_saved"], 16 * DEPTH)
                    src, col = ch.dst
                    ins = v.tensor_copy(rows(src)[:, :, col:col + ch.width], ps)
                elif ch.how == "mem_kv":
                    l = ch.dst
                    ins = v.tensor_copy(rows(("U", 512, 1024 * l)), ps)
                elif ch.how == "residual":
                    c = slice(ch.dst, ch.dst + ch.width)
                    y = rows("tmp")
                    for t in range(T):
                        ins = v.scalar_tensor_tensor(out=y[:, t, c], in0=x[:, t, c], scalar=ALPHA, in1=ps[:, t, :],
                                                     op0=ALU.mult, op1=ALU.add)
                    link(ins)
                    for t in range(T):
                        ins = v.bn_stats(stats[:, t, ch.dst // 512, :], y[:, t, c])
                elif ch.how == "up":
                    dve.wait_ge(S["acc_taken_act"], ch.act_taken)
                    ins = v.tensor_tensor(H[:, :, 0:ch.width], G[:, :, 0:ch.width], ps, ALU.mult)
                elif ch.how in ("branch_first", "branch"):
                    dve.wait_ge(S["acc_taken_act"], ch.act_taken)
                    c = slice(ch.dst, ch.dst + ch.width)
                    y, gate = rows("Y")[:, :, c], rows("tmp")[:, :, c]
                    if ch.how == "branch_first":
                        ins = v.tensor_tensor(y, gate, ps, ALU.mult)
                    else:
                        link(v.tensor_tensor(gate, gate, ps, ALU.mult))
                        ins = v.tensor_tensor(y, y, gate, ALU.add)
                ins.then_inc(S["acc_taken_dve"], 1)

            index_done = [0]
            saved = [False]

            def index_scores(ph):
                wi = rows(ph.src)[:, :, 2816:2816 + IDXH]
                for i in range(2 * IDXH):
                    t, h = i // IDXH, i % IDXH
                    n = index_done[0]
                    w = P * (t + 1)
                    dst = scores[:, 0:P] if t == 0 else scores[:, P:CAUSAL]
                    relu = L[:, 512 * (n % 2):512 * (n % 2) + w]
                    dve.wait_ge(S["index_relu"], n + 1)
                    if h == 0:
                        ins = v.tensor_scalar(dst, relu, wi[:, t, 0:1], None, ALU.mult)
                    else:
                        ins = v.scalar_tensor_tensor(out=dst, in0=relu, scalar=wi[:, t, h:h + 1], in1=dst,
                                                     op0=ALU.mult, op1=ALU.add)
                    ins.then_inc(S["index_added"], 1)
                    index_done[0] += 1
                    dve.wait_ge(S["index_added"], index_done[0])
                link(v.tensor_tensor(scores[:], scores[:], masks[:, 0, :], ALU.add))

            def top_k(rounds, done):
                best = small[:, 4:6, 0:8]
                for _ in range(*rounds):
                    for t, c in ((0, slice(0, P)), (1, slice(P, CAUSAL))):
                        ins = v.max(best[:, t, :], scores[:, c])
                    link(ins)
                    for t, c in ((0, slice(0, P)), (1, slice(P, CAUSAL))):
                        ins = v.match_replace(scores[:, c], best[:, t, :], scores[:, c], SENTINEL)
                    link(ins)
                if rounds[1] < TOPK // 8:
                    v.memset(small[:, 7, 0:1], 0.0).then_inc(done, 1)
                    return
                link(v.tensor_scalar(selected[:], scores[:], SENTINEL, NEG, ALU.not_equal, ALU.mult))
                v.tensor_tensor(selected[:], selected[:], masks[:, 0, :], ALU.add).then_inc(done, 1)

            def do_stage(ph):
                done = S["stage"]
                if ph.n > ph.incs:
                    dve.wait_ge(done, ph.n - ph.incs)
                fn = ph.fn
                if fn == "mem_norm":
                    dve.wait_ge(S["mem_landed"], 16)
                    m = rows("tmp")
                    for t in range(T):
                        for c in range(2):
                            ins = v.bn_stats(stats[:, t, c, :], m[:, t, 512 * c:512 * c + 512])
                    link(ins)
                    norm_rows(m, m, gains(ph.gain), D, LN_EPS, done)
                elif fn == "layer_norm":
                    dve.wait_ge(S["acc_taken_dve"], ph.dve_taken)
                    norm_rows(rows("tmp"), x[:], gains(ph.gain), D, LN_EPS, done)
                elif fn == "rope_index":
                    dve.wait_ge(S["acc_taken_dve"], ph.dve_taken)
                    r = rows(ph.src)
                    ki = r[:, :, 2824:2888]
                    for t in range(T):
                        ins = v.bn_stats(stats[:, t, 0, :], ki[:, t, :])
                    link(ins)
                    norm_rows(ki, ki, (knorm[:, ph.layer, 0, :], knorm[:, ph.layer, 1, :]), HD, LN_EPS)
                    rope(ki.unsqueeze(2), 1, 0, 8)
                    twice = rows("KI").rearrange("p t (m d) -> p t m d", m=2)
                    v.tensor_copy(twice, ki.unsqueeze(2).to_broadcast([P, T, 2, HD]))
                    rope(r[:, :, 2304:2816].rearrange("p t (n d) -> p t n d", d=HD), IDXH, 0, 8)
                    wi = r[:, :, 2816:2816 + IDXH]
                    v.tensor_scalar(wi, wi, (IDXH * HD) ** -0.5, None, ALU.mult).then_inc(done, 1)
                elif fn == "rope_heads":
                    dve.wait_ge(S["acc_taken_dve"], ph.dve_taken)
                    rope(rows(ph.src)[:, :, 0:2 * MIX].rearrange("p t (n d) -> p t n d", d=HD), 2 * HEADS, 0, 8)
                    v.memset(small[:, 7, 0:1], 0.0).then_inc(done, 1)
                elif fn == "top_k":
                    top_k(ph.src, done)
                elif fn == "rms_pre":
                    dve.wait_ge(S["acc_taken_dve"], ph.dve_taken)
                    rms_rows(x[:], rows("tmp"), gains(ph.gain)[0], D, done)
                elif fn == "rms_post":
                    dve.wait_ge(S["acc_taken_dve"], ph.dve_taken)
                    z = rows("tmp")
                    rms_rows(z, z, gains(ph.gain)[0], D)
                    for t in range(T):
                        v.tensor_tensor(x[:, t], x[:, t], z[:, t], ALU.add).then_inc(done, 1)
                elif fn == "ple_add":
                    dve.wait_ge(S["acc_taken_act"], ph.act_need)
                    dve.wait_ge(S["acc_taken_dve"], ph.dve_taken)
                    c = slice(ph.dst[0], ph.dst[0] + ph.dst[1])
                    gate = rows("tmp")[:, :, c]
                    link(v.tensor_tensor(gate, gate, rows(ph.src)[:, :, c], ALU.mult))
                    v.tensor_tensor(x[:, :, c], x[:, :, c], gate, ALU.add).then_inc(done, 1)
                elif fn == "sub_norm":
                    dve.wait_ge(S["out_taken"], ph.steps_before)
                    o = rows(ph.src)[:, :, 0:512]
                    lam_init = 0.8 - 0.6 * math.exp(-0.3 * ph.layer)
                    sq = L[:, 0:1024].rearrange("p (t c) -> p t c", t=T)
                    link(v.tensor_tensor(sq, o, o, ALU.mult))
                    link(v.tensor_reduce(small[:, 1, 0:8], sq.rearrange("p t (h e) -> p (t h) e", e=P), AX.X, ALU.add))
                    link(v.tensor_scalar(small[:, 3, 0:8], small[:, 1, 0:8], 1.0 / P, RMS_EPS, ALU.mult, ALU.add))
                    rsqrt(small[:, 2, 0:8], small[:, 3, 0:8], 8)
                    link(v.tensor_scalar(small[:, 2, 0:8], small[:, 2, 0:8], 1.0 - lam_init, None, ALU.mult))
                    heads = o.rearrange("p t (h e) -> p t h e", e=P)
                    rs = small[:, 2, 0:8].rearrange("p (t h) -> p t h", t=T).unsqueeze(3).to_broadcast([P, T, DA_H, P])
                    link(v.tensor_tensor(heads, heads, rs, ALU.mult))
                    gg = subln[:, ph.layer, :].unsqueeze(1).unsqueeze(1).to_broadcast([P, T, DA_H, P])
                    link(v.tensor_tensor(heads, heads, gg, ALU.mult))
                    dve.wait_ge(S["acc_taken_act"], ph.act_taken)
                    v.tensor_tensor(o, o, rows(ph.src)[:, :, 1536:2048], ALU.mult).then_inc(done, 1)
                elif fn == "gate_mixed":
                    dve.wait_ge(S["out_taken"], ph.steps_before)
                    dve.wait_ge(S["acc_taken_act"], ph.act_taken)
                    o = rows(ph.src)[:, :, 0:512]
                    src, col = ph.z
                    v.tensor_tensor(o, o, rows(src)[:, :, col:col + 512], ALU.mult).then_inc(done, 1)
                elif fn == "latent_norm":
                    dve.wait_ge(S["acc_taken_dve"], ph.dve_taken)
                    r = rows(ph.src)
                    rms_rows(r[:, :, 0:256], r[:, :, 0:256], qnorm[:, ph.layer, :], 256)
                    rms_rows(r[:, :, 256:384], r[:, :, 256:384], kvnorm[:, ph.layer, :], P)
                    rope(r[:, :, 384:416].unsqueeze(2), 1, 8, 16)
                    v.memset(small[:, 7, 0:1], 0.0).then_inc(done, 1)
                elif fn == "latent_rope_q":
                    dve.wait_ge(S["acc_taken_dve"], ph.dve_taken)
                    heads = rows(ph.src).rearrange("p t (n d) -> p t n d", d=MLA_K)
                    rope(heads[:, :, :, HD:MLA_K], MLA_H, 8, 16)
                    v.memset(small[:, 7, 0:1], 0.0).then_inc(done, 1)
                elif fn == "latent_keys":
                    dve.wait_ge(S["t_ready"], ph.t_need)
                    heads = rows(ph.dst).rearrange("p t (n d) -> p t n d", d=MLA_K)
                    kv = rows(ph.src).rearrange("p t (n d) -> p t n d", d=P)
                    for t in range(T):
                        v.tensor_copy(heads[:, t, :, 0:HD], kv[:, t, :, 0:HD])
                        kr = rows(ph.low)[:, t, 384:416].unsqueeze(1).to_broadcast([P, MLA_H, 32])
                        ins = v.tensor_copy(heads[:, t, :, HD:MLA_K], kr)
                    ins.then_inc(done, 1)
                elif fn == "twice_keys":
                    dve.wait_ge(S["acc_taken_dve"], ph.dve_taken)
                    k2 = rows(ph.dst).rearrange("p t (h m d) -> p t h m d", h=2, m=2)
                    for t in range(T):
                        k1 = rows(ph.src)[:, t, 512:640].rearrange("p (h d) -> p h d", h=2)
                        ins = v.tensor_copy(k2[:, t], k1.unsqueeze(2).to_broadcast([P, 2, 2, HD]))
                    ins.then_inc(done, 1)
                else:
                    raise ValueError(fn)

            def attention(ph):
                def mask_of(s):
                    if s.flavour == "dilated":
                        return masks[:, 1:4, :]
                    if s.flavour == "sinks":
                        return bias[:, s.bias_row:s.bias_row + 2, :]
                    if s.mask == "bias":
                        return bias[:, s.bias_row:s.bias_row + 1, :].to_broadcast([P, 2, CAUSAL])
                    if s.mask == "selected":
                        return selected[:].unsqueeze(1).to_broadcast([P, 2, CAUSAL])
                    m = masks[:, 0, :] if ph.block == 1 else causal_2[:]
                    return m.unsqueeze(1).to_broadcast([P, 2, CAUSAL])

                if ph.steps[0].mask == "bias":
                    dve.wait_ge(S["bias_landed"], ph.bias_need)
                if ph.steps[0].mask == "selected":
                    dve.wait_ge(S["stage"], ph.stage_need)

                def logits(s):
                    for b in s.before:
                        take_batch(b)
                    lg, slot = step_logits(s), s.s % 2
                    dve.wait_ge(S["scores_ready"], s.s + 1)
                    ps = acc[:, s.bank:s.bank + s.maps, 0:s.width]
                    if s.width == FULL:
                        ins = v.tensor_scalar(lg, ps, s.scale, None, ALU.mult)
                    else:
                        ins = v.scalar_tensor_tensor(out=lg, in0=ps, scalar=s.scale, in1=mask_of(s),
                                                     op0=ALU.mult, op1=ALU.add)
                    ins.then_inc(S["logits_ready"], 1)
                    dve.wait_ge(S["logits_ready"], s.s + 1)
                    nm = neg_max[:, slot, :]
                    for t in range(T):
                        part = lg[:, :, tile_cols(s, t)]
                        if s.flavour == "dilated":
                            ins = v.tensor_reduce(nm[:, t:t + 1], part, AX.XY, ALU.max, negate=True)
                        else:
                            ins = v.tensor_reduce(nm[:, t:t + 3:2], part, AX.X, ALU.max, negate=True)
                    if s.flavour == "sinks":
                        link(ins)
                        nm2 = nm.rearrange("p (m t) -> p m t", m=2)
                        h = slice(2 * s.i, 2 * s.i + 2)
                        link(v.tensor_tensor(nm2, nm2, neg_sinks[:, ph.layer, h].unsqueeze(2).to_broadcast([P, 2, T]),
                                             ALU.min))
                        ins = v.tensor_tensor(sink_exp[:, slot, :].rearrange("p (m t) -> p m t", m=2), nm2,
                                              sinks[:, ph.layer, h].unsqueeze(2).to_broadcast([P, 2, T]), ALU.add)
                    ins.then_inc(S["max_ready"], 1)

                def combine(s):
                    lg, slot = step_logits(s), s.s % 2
                    dve.wait_ge(S["probs_ready"], s.s + 1)
                    rc, sm = recips[:, slot, :], sums[:, slot, :]
                    if s.flavour == "dilated":
                        link(v.tensor_tensor(lg[:, 0, :], lg[:, 0, :], lg[:, 1, :], ALU.add))
                        v.tensor_tensor(lg[:, 0, :], lg[:, 0, :], lg[:, 2, :], ALU.add).then_inc(S["mixed_ready"], 1)
                        link(v.reciprocal(rc[:, 0:2], sm[:, 0:2]))
                        return
                    if s.flavour == "sinks":
                        link(v.tensor_tensor(sm, sm, sink_exp[:, slot, :], ALU.add))
                    link(v.reciprocal(rc, sm))
                    if s.flavour == "differential":
                        link(v.tensor_scalar(rc[:, 2:4], rc[:, 2:4], neg_lam[:, ph.layer:ph.layer + 1], None, ALU.mult))
                        for t in range(T):
                            c = tile_cols(s, t)
                            ins = v.tensor_scalar(lg[:, 1, c], lg[:, 1, c], rc[:, 2 + t:3 + t], None, ALU.mult)
                        link(ins)
                        for t in range(T):
                            c = tile_cols(s, t)
                            ins = v.scalar_tensor_tensor(out=lg[:, 0, c], in0=lg[:, 0, c], scalar=rc[:, t:t + 1],
                                                         in1=lg[:, 1, c], op0=ALU.mult, op1=ALU.add)
                        ins.then_inc(S["mixed_ready"], 1)

                def take_turns(s):
                    for tb in s.tb:
                        dve.wait_ge(S["t_ready"], tb.b + 1)
                        v.tensor_copy(PT[:, tb.j, 0:tb.blocks * P],
                                      tps[:, tb.b % 2, 0:tb.blocks * P]).then_inc(S["t_taken"], 1)

                def outputs(s):
                    slot, rc = s.s % 2, recips[:, s.s % 2, :]
                    dve.wait_ge(S["pv_ready"], s.s + 1)
                    dst = rows(s.heads_out)[:, :, s.out:s.out + (s.dv if s.mixed else P)]
                    if s.flavour == "differential":
                        ins = v.tensor_copy(dst, ops[:, slot, 0:T * P].rearrange("p (t e) -> p t e", t=T))
                    elif s.flavour == "dilated":
                        o = ops[:, slot, 0:T * s.dv].rearrange("p (t e) -> p t e", t=T)
                        ins = v.tensor_tensor(dst, o, rc[:, 0:T].unsqueeze(2).to_broadcast([P, T, s.dv]), ALU.mult)
                    else:
                        o = ops[:, slot, 0:4 * HD].rearrange("p (m t e) -> p m t e", m=2, t=T)
                        r4 = rc.rearrange("p (m t) -> p m t", m=2).unsqueeze(3).to_broadcast([P, 2, T, HD])
                        ins = v.tensor_tensor(dst.rearrange("p t (m e) -> p m t e", m=2), o, r4, ALU.mult)
                    ins.then_inc(S["out_taken"], 1)

                logits(ph.steps[0])
                for s in ph.steps:
                    if s.i + 1 < len(ph.steps):
                        logits(ph.steps[s.i + 1])
                    if s.i:
                        outputs(ph.steps[s.i - 1])
                    for u in s.fill:
                        if u.u == u.chunk.last and u.chunk.eng == "dve":
                            take_chunk(u.chunk)
                    combine(s)
                    take_turns(s)
                outputs(ph.steps[-1])

            for ph in p.phases:
                if ph.kind == "stage":
                    do_stage(ph)
                elif ph.kind == "transpose":
                    for b in ph.batches:
                        take_batch(b)
                elif ph.kind == "linear":
                    for ch in ph.chunks:
                        for u in ch.units:
                            for b in u.pre:
                                take_batch(b)
                        if ch.eng == "dve":
                            take_chunk(ch)
                elif ph.kind == "tables":
                    tables()
                elif ph.kind == "index_scores":
                    index_scores(ph)
                elif ph.kind == "attention":
                    attention(ph)


_CONSTS = ("c_ident", "c_masks", "c_inv", "c_onehot", "c_relmask")


def kernel(**inputs):
    import concourse.bacc as bacc
    from concourse.bass_utils import run_bass_kernel_spmd

    nc = bacc.Bacc("TRN2", target_bir_lowering=False, num_devices=1)
    arrays, aps = {}, {}
    given = {k: np.ascontiguousarray(v) for k, v in inputs.items()}
    for name, arr in {**given, **shape_constants()}.items():
        arrays[f"in_{name}"] = arr
        aps[name] = nc.dram_tensor(f"in_{name}", arr.shape, mybir.dt.from_np(arr.dtype), kind="ExternalInput").ap()
    out = nc.dram_tensor("out", (1, N, D), F32, kind="ExternalOutput").ap()
    build(nc, aps, out)
    r = run_bass_kernel_spmd(nc, [arrays], core_ids=[0])
    return r.results[0]["out"]
```

```python
import math
from contextlib import ExitStack

import numpy as np

import concourse.bass as bass
from concourse import mybir

F32 = mybir.dt.float32
F32R = mybir.dt.float32r
I32 = mybir.dt.int32
ALU = mybir.AluOpType
ACT = mybir.ActivationFunctionType
AX = mybir.AxisListType

P = 128
T = 2
N = T * P
D = 1024
DEPTH = 4
HD = 64
MIX = 768
HEADS = MIX // HD
MEMW = 256
IDXH = 8
TOPK = min(256, N // 4)
FF = 2816
ALPHA = (2 * DEPTH) ** 0.25
LN_EPS = 1e-5
RMS_EPS = 1e-6
DEPTH_2 = 2
DA_H, MLA_H, SW_H = 4, 8, 8
MLA_K = 96
BIAS_HEADS = DA_H + SW_H
REL_BUCKETS = 32
NEG = -1e30
SENTINEL = -3e38
SCALE = HD ** -0.5
MLA_SCALE = MLA_K ** -0.5
CAUSAL = 384
FULL = 512
REL_ROW = 384

CHUNK = 512
UK = 2
RAW = 6
SPLIT = 6
AHEAD = SPLIT - 1

TWO_PI_1 = 6.28125
TWO_PI_2 = float(np.float32(0.0019350051879882812))
TWO_PI_3 = 2 * math.pi - TWO_PI_1 - TWO_PI_2
ROUND = 12582912.0
PI_INSIDE = 3.1415925

C_AQ, C_AZ, C_BQ, C_BZ, C_CQ, C_CZ, C_G = 0, 1536, 2048, 2464, 2976, 3744, 4256


def t5_bucket_rows():
    rel = 255 - np.arange(REL_ROW)
    n = np.maximum(rel, 0)
    nf = np.maximum(n, 1).astype(np.float32)
    half = REL_BUCKETS // 2
    large = half + (np.log(nf / np.float32(half)) / np.float32(math.log(128 / half))
                    * np.float32(REL_BUCKETS - half)).astype(np.int32)
    bucket = np.where(n < half, n, np.minimum(large, REL_BUCKETS - 1))
    onehot = ((np.arange(REL_BUCKETS)[:, None] == bucket[None]) & (rel >= 0)[None]).astype(np.float32)
    mask = np.zeros((BIAS_HEADS, REL_ROW), np.float32)
    mask[:, rel < 0] = NEG
    mask[DA_H:, rel >= 128] = NEG
    return onehot, mask


def shape_constants():
    q0, k0 = np.arange(P)[:, None], np.arange(P)[None]
    q1, k1 = P + np.arange(P)[:, None], np.arange(N)[None]

    def mask(keep):
        both = np.concatenate([keep(q0, k0), keep(q1, k1)], 1)
        return np.where(both, 0.0, NEG).astype(np.float32)

    masks = np.stack([
        mask(lambda q, k: k <= q),
        mask(lambda q, k: (k <= q) & (q - k <= 128)),
        mask(lambda q, k: (k <= q) & ((q - k) % 4 == 0)),
        mask(lambda q, k: (k <= q) & ((q - k) % 16 == 0)),
    ], 1)
    inv_1 = np.power(500000.0, (-np.arange(8, dtype=np.float32) / np.float32(8)).astype(np.float64))
    inv_2 = np.power(10000.0, (-np.arange(16, dtype=np.float32) / np.float32(16)).astype(np.float64))
    inv = np.broadcast_to(np.concatenate([inv_1, inv_2]).astype(np.float32), (P, 24))
    onehot, rel_mask = t5_bucket_rows()
    return {
        "c_ident": np.eye(P, dtype=np.float32),
        "c_masks": np.ascontiguousarray(masks),
        "c_inv": np.ascontiguousarray(inv),
        "c_onehot": onehot,
        "c_relmask": rel_mask,
    }


def column_chunks(start, stop):
    return [(c, min(CHUNK, stop - c)) for c in range(start, stop, CHUNK)]


class Phase:

    def __init__(self, kind, layer=None, chunks=None, t_need=0, batches=None, steps=None, block=None,
                 stage_need=0, bias_need=0, fn=None, n=None, incs=1, act_taken=0, dve_taken=0,
                 act_need=0, src=None, dst=None, low=None, z=None, gain=None, head=None,
                 heads=None, first=0, steps_before=0, index_before=0):
        self.kind = kind
        self.layer = layer
        self.chunks = chunks
        self.t_need = t_need
        self.batches = batches
        self.steps = steps
        self.block = block
        self.stage_need = stage_need
        self.bias_need = bias_need
        self.fn = fn
        self.n = n
        self.incs = incs
        self.act_taken = act_taken
        self.dve_taken = dve_taken
        self.act_need = act_need
        self.src = src
        self.dst = dst
        self.low = low
        self.z = z
        self.gain = gain
        self.head = head
        self.heads = heads
        self.first = first
        self.steps_before = steps_before
        self.index_before = index_before


class Batch:

    def __init__(self, b, moves, dst, split, after, hi=0):
        self.b = b
        self.moves = moves
        self.dst = dst
        self.split = split
        self.after = after
        self.hi = hi


class Chunk:

    def __init__(self, c, index, acts, k_tiles, col, width, how, dst, eng, count, act_taken,
                 dve_taken_before, stage_before, bank, free_when):
        self.c = c
        self.index = index
        self.acts = acts
        self.k_tiles = k_tiles
        self.col = col
        self.width = width
        self.how = how
        self.dst = dst
        self.eng = eng
        self.count = count
        self.act_taken = act_taken
        self.dve_taken_before = dve_taken_before
        self.stage_before = stage_before
        self.bank = bank
        self.free_when = free_when
        self.units = []
        self.last = None


class Unit:

    def __init__(self, u, k0, nk, chunk, weight):
        self.u = u
        self.k0 = k0
        self.nk = nk
        self.chunk = chunk
        self.weight = weight
        self.pre = []
        self.gain = None
        self.late_gain = None
        self.t_need = 0
        self.out_need = 0
        self.index = []


class Step:

    def __init__(self, q, k, v, out, width=CAUSAL, dv=HD, scale=SCALE, flavour="plain", mask=None,
                 heads_out=None, pre=None, v_taken=0, bias_row=0):
        self.q = q
        self.k = k
        self.v = v
        self.out = out
        self.width = width
        self.dv = dv
        self.scale = scale
        self.flavour = flavour
        self.mask = mask
        self.heads_out = heads_out
        self.pre = pre
        self.v_taken = v_taken
        self.bias_row = bias_row
        self.maps = len(q)
        self.s = 0
        self.i = 0
        self.bank = 0
        self.free_when = []
        self.before = []
        self.fill = []
        self.tb = []
        self.mixed = 0
        self.normal = 0
        self.pool_normal = 0
        self.ahead = []


class Turn:

    def __init__(self, b, j, blocks):
        self.b = b
        self.j = j
        self.blocks = blocks


class IndexGroup:

    def __init__(self, n, t, heads, src, t_need, steps_before):
        self.n = n
        self.t = t
        self.heads = heads
        self.src = src
        self.t_need = t_need
        self.steps_before = steps_before


class Gain:

    def __init__(self, j, g, b):
        self.j = j
        self.g = g
        self.b = b
        self.stage = None


class Plan:

    def __init__(self):
        self.phases = []
        self.units = []
        self.chunks = []
        self.n_t = 0
        self.n_hi = 0
        self.n_steps = 0
        self.n_stage = 0
        self.n_taken = {"dve": 0, "act": 0}
        self.n_index = 0
        self.n_mixed = 0
        self.n_normal = 0
        self.n_pool_normal = 0
        self.n_bias = 0
        self.block = 1
        self.k_ready = {"x": [0] * 8, "h": [0] * (FF // P), "s": [0] * 4, "s2": [0] * 4,
                        "mixed": [0] * 8}
        self.out_ready = [0] * 8
        self.bank_held = [None] * 4
        self.pair = 1
        self.fixed_pair = None

    def take_banks(self, bank, n, then):
        waits = []
        for b in range(bank, bank + n):
            if self.bank_held[b] is not None and self.bank_held[b] not in waits:
                waits.append(self.bank_held[b])
            self.bank_held[b] = then
        return waits

    def add(self, kind, **kw):
        ph = Phase(kind, **kw)
        self.phases.append(ph)
        return ph

    def batch(self, source, moves, dst, split, after):
        b = Batch(self.n_t, moves, dst, split, after)
        self.n_t += 1
        if split:
            self.n_hi += 1
            b.hi = self.n_hi
        return b

    def split_batches(self, source, k0, nk, dst, d0, after):
        out = []
        for k in range(0, nk, 4):
            m = min(4, nk - k)
            for t in range(T) if m > 2 else (None,):
                tiles = range(T) if t is None else (t,)
                moves = [(source, tt, (k0 + k + j) * P, P) for j in range(m) for tt in tiles]
                when = after[t or 0] if isinstance(after, list) else after
                out.append(self.batch(source, moves, (dst, d0 + k, m, P, t), True, when))
            for j in range(m):
                self.k_ready[dst][d0 + k + j] = self.n_t
                if dst == "s" and d0 + k + j >= 2:
                    self.k_ready["s2"][d0 + k + j - 2] = self.n_t
        return out

    def half_batches(self, source, half, dst, after):
        k = 4 * half
        out = [self.batch(source, [(source, t, (k + j) * P, P) for j in range(4)], (dst, k, 4, P, t), True, after[t])
               for t in range(T)]
        self.k_ready[dst][k:k + 4] = [self.n_t] * 4
        return out

    def head_batches(self, source, cols, width, dst, d0, after):
        out = []
        for i in range(0, len(cols), 2):
            pair = cols[i:i + 2]
            moves = [(source, t, c, width) for c in pair for t in range(T)]
            out.append(self.batch(source, moves, (dst, d0 + i, len(pair), width, None), False, after))
        return out

    def open_chunk(self, weight, k_tiles, acts, spec, index, before=None):
        col, width, how, dst = spec
        eng = "act" if how in ("silu", "sigmoid") else "dve"
        before_dve = self.n_taken["dve"]
        self.n_taken[eng] += 1
        count = self.n_taken[eng]
        self.pair = 1 - self.pair if self.fixed_pair is None else self.fixed_pair
        bank = 2 * self.pair
        ch = Chunk(len(self.chunks), index, acts, k_tiles, col, width, how, dst, eng, count,
                   self.n_taken["act"], before_dve, self.n_stage, bank,
                   self.take_banks(bank, T, ("acc_taken_" + eng, count)))
        self.chunks.append(ch)
        for ui, k0 in enumerate(range(0, k_tiles, UK)):
            u = Unit(len(self.units), k0, min(UK, k_tiles - k0), ch, weight)
            if before and (index, ui) in before:
                u.pre = before[(index, ui)]()
            u.t_need = max(self.k_ready[acts][k0:k0 + u.nk])
            if acts == "mixed":
                u.out_need = max(self.out_ready[k0:k0 + u.nk])
            self.units.append(u)
            ch.units.append(u)
        ch.last = ch.units[-1].u
        return ch

    def linear(self, weight, k_tiles, acts, chunks, before=None, gains=None):
        ph = self.add("linear", chunks=[])
        for ci, spec in enumerate(chunks):
            ch = self.open_chunk(weight, k_tiles, acts, spec, ci, before)
            ph.chunks.append(ch)
            if ci == 0:
                ch.units[0].gain = gains
        return ph

    def transpose(self, batches):
        return self.add("transpose", batches=batches)

    def stage(self, fn, incs=1, **kw):
        self.n_stage += incs
        return self.add("stage", fn=fn, n=self.n_stage, incs=incs, act_taken=self.n_taken["act"],
                        dve_taken=self.n_taken["dve"], steps_before=self.n_steps, **kw)

    def attention(self, steps, layer=None, fill=(), fill_steps=1):
        ph = self.add("attention", t_need=self.n_t, steps=steps, layer=layer, block=self.block, first=self.n_steps,
                      index_before=self.n_index, bias_need=self.n_bias, stage_need=self.n_stage)
        fill_pair = 1 - self.pair
        total = sum(-(-f[1] // UK) for f in fill)
        per_step = -(-total // fill_steps)
        waiting = list(fill)
        opened = []

        def scores_of(i):
            s = steps[i]
            s.s, s.i = self.n_steps, i
            self.n_steps += 1
            if s.pre is not None:
                s.before = s.pre()
            if fill and i < fill_steps + 1:
                s.bank = 2 - 2 * fill_pair
            elif fill:
                s.bank = 2 * (fill_pair if (i - fill_steps) % 2 else 1 - fill_pair)
            else:
                s.bank = 0 if s.maps > 2 else 2 * (i % 2)
            s.free_when = self.take_banks(s.bank, s.maps, ("logits_ready", s.s + 1))
            return s

        scored = 1
        scores_of(0)
        for i, s in enumerate(steps):
            ahead = 1 if s.maps > 2 or fill and i < fill_steps else 2
            while scored <= min(i + ahead, len(steps) - 1):
                s.ahead.append(scores_of(scored))
                scored += 1
            self.fixed_pair = fill_pair
            while len(s.fill) < per_step and (waiting or opened):
                if not opened:
                    weight, k_tiles, acts, spec = waiting.pop(0)
                    opened += self.open_chunk(weight, k_tiles, acts, spec, 0).units
                s.fill.append(opened.pop(0))
            self.fixed_pair = None
            if s.flavour == "differential":
                self.n_mixed += 1
                s.mixed = self.n_mixed
            if self.block == 1:
                self.n_normal += 1
                s.normal = self.n_normal
                if s.flavour != "dilated":
                    self.n_pool_normal += 1
                    s.pool_normal = self.n_pool_normal
                for _, tile, _, _ in s.out:
                    self.out_ready[tile] = s.s + 1
            for j in range(1 if s.flavour in ("dilated", "differential") else s.maps):
                s.tb.append(Turn(self.n_t, j, 3 if s.width == CAUSAL else 4))
                self.n_t += 1
        assert not waiting and not opened
        return ph


def plan(w):
    p = Plan()
    gains = iter(range(100))

    def ln_gain(name_g, name_b, row):
        return Gain(next(gains), (name_g, row), (name_b, row))

    def norm(gain, fn, source, rest="norm_rest", between=None):
        p.stage(fn, gain=gain, incs=2)
        if between:
            between()
        if source:
            p.transpose(p.half_batches(source, 0, "x", norm_src()))
        ph = p.stage(rest, gain=gain, incs=2)
        gain.stage = ph.n
        p_gains.append(gain)
        after = norm_src()
        return {(0, 1): lambda: p.half_batches(source, 1, "x", after)}

    p_gains = []
    p.gains = p_gains

    def stage_src():
        return ("stage", p.n_stage)

    def norm_src():
        return [("stage", p.n_stage - 1), ("stage", p.n_stage)]

    def taken(n=None):
        return ("acc_taken_dve", p.n_taken["dve"] if n is None else n)

    def lin_copy(win, src, cols, dst0=None, before=None):
        at = cols[0][0] if dst0 is None else dst0
        return p.linear(win, 8, "x", [(c, n, "copy", (src, at + c - cols[0][0])) for c, n in cols], before)

    g = ln_gain("mem_ln_g", "mem_ln_b", None)
    p.first_gain = g
    second = norm(g, "mem_norm", "tmp")
    p.linear(w["w_mem_kv"][0], 8, "x", [(0, 512, "mem_kv", 0)], second)
    p.add("tables")
    for l in range(1, DEPTH):
        p.linear(w["w_mem_kv"][l], 8, "x", [(0, 512, "mem_kv", l)])
    mem_taken = p.n_taken["dve"]
    landed = [("x_landed", 16)] * T
    p.transpose(p.half_batches("x", 0, "x", landed))
    p.add("save_mem_kv", dve_taken=mem_taken)
    second = {(0, 1): lambda: p.half_batches("x", 1, "x", landed)}

    for l in range(DEPTH):
        kind, j = l % 3, l // 3
        width = 3144 if kind == 0 else 2560
        qm = 2888 if kind == 0 else 2304
        win = (w["w_in_a"], w["w_in_b"], w["w_in_c"])[kind][j]
        src = ("U", width, 0)
        v_a = (2 * MIX, 512)
        load = dict(layer=l, steps_before=p.n_steps)
        if kind == 0:
            lin_copy(win, src, [(2304, 292), (2596, 292)], before=second)
            p.stage("rope_index", src=src, layer=j)
            lin_copy(win, src, [(0, 512)])
            p.add("load_mem_kv", **load)
            p.transpose(p.head_batches(src, [2304 + P * i for i in range(4)], P, "QT", 0, stage_src())
                        + p.head_batches("KI", [0], P, "KT", 0, stage_src()))
            lin_copy(win, src, [(512, 512)])
            groups = []
            for t in range(T):
                per_bank = 512 // (P * (t + 1))
                for h in range(0, IDXH, 2 * per_bank):
                    for half in range(2):
                        heads = range(h + half, h + 2 * per_bank, 2)
                        groups.append(IndexGroup(p.n_index, t, heads, src, p.n_t, p.n_steps))
                        p.n_index += 1
            index_units = lin_copy(win, src, [(1024, 512)]).chunks[0].units
            for u in index_units:
                left = len(index_units) - (u.u - index_units[0].u)
                for _ in range(-(-len(groups) // left)):
                    u.index.append(groups.pop(0))
            p.stage("top_k", src=(0, 4))
            p.stage("rope_heads", src=src)
            roped = stage_src()
            p.stage("top_k", src=(4, 8))
            lin_copy(win, src, [v_a, (2048, 256)])
            fill = [(win, 8, "x", (qm, 256, "copy", (src, qm)))]
        else:
            lin_copy(win, src, [(0, 512), (512, 512), (1024, 512)], before=second)
            p.add("load_mem_kv", **load)
            p.stage("rope_heads", src=src)
            roped = stage_src()
            lin_copy(win, src, [v_a])
            fill = [(win, 8, "x", (2048, 512, "copy", (src, 2048)))]
            if kind == 1:
                lin_copy(win, src, [(2048, 512)])
                fill = []
        v_now = p.n_taken["dve"]
        v_all = v_now + len(fill)
        p.transpose(p.head_batches(src, [P * i for i in range(6)], P, "QT", 0, roped)
                    + p.head_batches(src, [MIX + P * i for i in range(6)], P, "KT", 0, roped))

        def memory_tiles(l=l, src=src, qm=qm, v_all=v_all):
            return (p.head_batches(src, [qm, qm + P], P, "QT", 6, ("acc_taken_dve", v_all))
                    + p.head_batches("MKV", [0, P], P, "KT", 6, ("mem_kv_landed", 16 * (l + 1))))

        def pair(i, src, col, tile, **kw):
            return Step(q=[(i, HD * m, HD) for m in range(2)], k=[(i, HD * m, HD) for m in range(2)],
                        v=[(src, col + HD * m, HD, m, 0, HD * m) for m in range(2)], out=[(0, tile, 0, P)], **kw)

        if kind == 1:
            def dilated(b):
                whole, part = 3 * (b // 2) + 2 * (b % 2), 3 * (b // 2) + 1
                at = HD * (b % 2)
                return Step(q=[(2 * g + b // 2, at, HD) for g in range(3)],
                            k=[(2 * g + b // 2, at, HD) for g in range(3)],
                            v=[(src, 2 * MIX + P * whole, P, 0, 0, 0), (src, 2 * MIX + P * part + at, HD, 0, 1, at)],
                            out=[(0, whole, 0, P), (1, part, at, at + HD)], flavour="dilated", v_taken=v_now)

            steps = [dilated(b) for b in range(4)]
        else:
            steps = [pair(i, src, 2 * MIX + P * i, i, mask="selected" if kind == 0 else "causal",
                          v_taken=v_now if i < 4 else v_all) for i in range(6)]
        steps += [pair(6 + i, "MKV", MEMW + P * i, 6 + i, width=FULL,
                       pre=memory_tiles if i == 0 else None) for i in range(2)]
        p.attention(steps, fill=fill, fill_steps=4)
        g = ln_gain("ln1_g", "ln1_b", l)
        p.linear(w["w_out"][l], 8, "mixed", [(c, n, "residual", c) for c, n in column_chunks(0, D)], gains=g)
        second = norm(g, "layer_norm", "x")
        chunks, before = [], dict(second)
        widths = column_chunks(0, FF)
        first_taken = p.n_taken["dve"]

        def h_batches(i, first_taken=first_taken):
            def make():
                return p.split_batches("H", 0, widths[i][1] // P, "h", widths[i][0] // P,
                                       ("acc_taken_dve", first_taken + i + 1))
            return make

        for i, (c, n) in enumerate(widths):
            chunks += [(c, n, "silu", ("G",)), (FF + c, n, "up", i)]
            if i:
                before[(2 * i + 1, 0)] = h_batches(i - 1)
        p.linear(w["w_gate_up"][l], 8, "x", chunks, before)
        g = ln_gain("ln2_g", "ln2_b", l)
        k_last = widths[-1][0] // P
        p.linear(w["w_down"][l], FF // P, "h", [(c, n, "residual", c) for c, n in column_chunks(0, D)],
                 {(0, k_last // UK): h_batches(len(widths) - 1)}, gains=g)
        second = norm(g, "layer_norm", "x" if l < DEPTH - 1 else None)

    p.block = 2
    da, low, qm, kvm = ("U", 2048, 0), ("U", 928, 4096), ("U", 768, 0), ("U", 1024, 1536)
    sw, sw_z, sw_k = ("U", 768, 5952), ("U", 512, 1536), ("U", 256, 2560)
    ple_rows, ple_out = ("U", 256, 3072), ("U", D, 0)
    for l in range(DEPTH_2):
        win = w["w_in_2"][l]
        g = ln_gain("norm_pre_2", None, l)
        p.units[-1].late_gain = g
        second = norm(g, "rms_pre", "tmp", "rms_pre_rest")

        def gate(i):
            return [(C_G + D * i + c, n, "sigmoid", ("tmp", D, c)) for c, n in column_chunks(0, D)]

        def branch(weight, mixed, first, between=()):
            p.transpose(p.split_batches(mixed, 0, 4, "s", 0, stage_src()))
            for fn, kw in between:
                p.stage(fn, **kw)
            p.linear(weight[l], 4, "s", [(c, n, "branch_first" if first else "branch", c)
                                         for c, n in column_chunks(0, D)])

        p.add("load_bias", head=0, heads=DA_H, steps_before=p.n_steps)
        p.n_bias += 32 + (16 if l == 0 else 0)
        n = p.n_taken["dve"]
        lin_copy(win, da, [(0, 512), (512, 512), (1024, 512)], before=second)
        p.transpose(p.head_batches(da, [P * i for i in range(4)], P, "QT", 0, taken(n + 1))
                    + p.head_batches(da, [512 + P * i for i in range(4)], P, "KT", 0, taken(n + 2)))
        steps = [Step(q=[(i, HD * m, HD) for m in range(2)], k=[(i, HD * m, HD) for m in range(2)],
                      v=[(da, 1024 + P * i)], out=P * i, dv=P, flavour="differential", mask="bias",
                      heads_out=da, v_taken=n + 3, bias_row=i) for i in range(4)]
        p.attention(steps, layer=l, fill_steps=4,
                    fill=[(win, 8, "x", (C_AZ, 512, "silu", (da, C_AZ))),
                          (win, 8, "x", (C_BQ, 416, "copy", (low, 0))),
                          (win, 8, "x", (C_BZ, 512, "silu", (low, 416)))])
        p.stage("sub_norm", src=da, layer=l)
        p.linear(win, 8, "x", gate(0))
        branch(w["w_br_a_2"], da, True, [("latent_norm", dict(src=low, layer=l))])

        p.transpose(p.split_batches(low, 0, 2, "s", 0, stage_src()) + p.split_batches(low, 2, 1, "s", 2, stage_src()))
        p.linear(w["mla_w_qb_2"][l], 2, "s", [(c, n, "copy", (qm, c)) for c, n in column_chunks(0, 768)])
        p.linear(w["mla_w_kvb_2"][l], 1, "s2", [(c, n, "copy", (kvm, c)) for c, n in column_chunks(0, 1024)])
        p.stage("latent_rope_q", src=qm, low=low)
        lin_copy(win, sw, [(C_CQ, 512)], 0)
        p.transpose(p.head_batches(qm, [MLA_K * i for i in range(8)], MLA_K, "QT", 0, stage_src()))
        p.stage("latent_keys", src=kvm, low=low, dst=qm, t_need=p.n_t)
        lin_copy(win, sw, [(C_CQ + 512, 256)], 512)
        p.transpose(p.head_batches(qm, [MLA_K * i for i in range(8)], MLA_K, "KT", 0, stage_src()))
        steps = [Step(q=[(2 * i + m, 0, MLA_K) for m in range(2)], k=[(2 * i + m, 0, MLA_K) for m in range(2)],
                      v=[(kvm, P * (2 * i + m) + HD) for m in range(2)], out=P * i, scale=MLA_SCALE,
                      mask="causal", heads_out=qm) for i in range(4)]
        p.attention(steps, layer=l, fill_steps=4, fill=[(win, 8, "x", c) for c in gate(1)])
        p.stage("gate_mixed", src=qm, z=(low, 416))
        p.stage("twice_keys", src=sw, dst=sw_k)
        keys_twice = stage_src()
        p.linear(win, 8, "x", [(C_CZ, 512, "silu", (sw_z, 0))])
        branch(w["w_br_b_2"], qm, False)

        p.add("load_bias", head=DA_H, heads=SW_H, steps_before=p.n_steps)
        p.n_bias += 32
        p.transpose(p.head_batches(sw, [P * i for i in range(4)], P, "QT", 0, keys_twice)
                    + p.head_batches(sw_k, [0, P], P, "KT", 0, keys_twice))
        steps = [Step(q=[(i, HD * m, HD) for m in range(2)], k=[(i // 2, HD * m, HD) for m in range(2)],
                      v=[(sw, 640 + HD * (i // 2)) for m in range(2)], out=P * i, flavour="sinks",
                      mask="bias", heads_out=sw, bias_row=2 * i) for i in range(4)]
        p.attention(steps, layer=l, fill_steps=4, fill=[(win, 8, "x", c) for c in gate(2)])
        p.add("load_ple", layer=l)
        p.stage("gate_mixed", src=sw, z=(sw_z, 0))
        branch(w["w_br_c_2"], sw, False)

        p.transpose(p.split_batches("Y", 0, 8, "x", 0, taken())
                    + p.split_batches(ple_rows, 0, 2, "s", 0, ("ple_landed", 16 * (l + 1))))
        g = ln_gain("norm_post_2", None, l)
        p.linear(w["w_out_2"][l], 8, "x", [(c, n, "copy", (("tmp", D, 0), c)) for c, n in column_chunks(0, D)],
                 gains=g)
        def ple_rows_product(l=l):
            p.linear(w["w_ple_proj_2"][l], 2, "s", [(c, n, "copy", (ple_out, c)) for c, n in column_chunks(0, D)])

        second = norm(g, "rms_post", "x", "rms_post_rest", ple_rows_product)
        p.linear(w["w_ple_gate_2"][l], 8, "x", [(c, n, "sigmoid", ("tmp", D, c)) for c, n in column_chunks(0, D)],
                 second)
        for i, (c, n) in enumerate(column_chunks(0, D)):
            p.stage("ple_add", src=ple_out, dst=(c, n), act_need=p.n_taken["act"] - 1 + i)
    return p


def build(nc, a, out):
    p = plan(a)
    rel_rows = nc.dram_tensor("rel_rows", [BIAS_HEADS, P, REL_ROW], F32, kind="Internal").ap()
    mem_kv = nc.dram_tensor("mem_kv", [DEPTH, P, T * 512], F32, kind="Internal").ap()
    gain_list = p.gains

    with ExitStack() as ctx:
        def sb(name, shape, dt=F32):
            return ctx.enter_context(nc.sbuf_tensor(name, shape, dt))

        def sem(name):
            return ctx.enter_context(nc.semaphore(name))

        raw = sb("raw", [P, RAW, UK, CHUNK])
        w_hi = sb("w_hi", [P, SPLIT, UK, CHUNK], F32R)
        w_lo = sb("w_lo", [P, SPLIT, UK, CHUNK], F32R)
        xT_hi = sb("xT_hi", [P, 8, N], F32R)
        xT_lo = sb("xT_lo", [P, 8, N], F32R)
        x = sb("x_rows", [P, T, D])
        tmp = sb("tmp", [P, T * D])
        gain = sb("gain", [P, 2, 2, D])
        ident = sb("ident", [P, P])
        knorm = sb("knorm", [P, 2, 2, HD])
        subln = sb("subln", [P, 2, P])
        qnorm = sb("qnorm", [P, 2, 256])
        kvnorm = sb("kvnorm", [P, 2, P])
        sinks = sb("sinks", [P, 2, SW_H])
        neg_sinks = sb("neg_sinks", [P, 2, SW_H])
        neg_lam = sb("neg_lam", [P, 2])
        trig = sb("trig", [P, 2, T, 24])
        stats = sb("stats", [P, T, 2, 6])
        small = sb("small", [P, 10, 16])
        neg_max = sb("neg_max", [P, 2, 4])
        sums = sb("sums", [P, 2, 4])
        sink_exp = sb("sink_exp", [P, 2, 4])
        recips = sb("recips", [P, 2, 4])

        att = ExitStack()
        with att:
            def sba(name, shape, dt=F32):
                return att.enter_context(nc.sbuf_tensor(name, shape, dt))
            U = sba("U", [P, 7488])
            QT = sba("QT", [P, 8, N])
            KT = sba("KT", [P, 8, N])
            L = sba("L", [P, 2 * 3 * CAUSAL])
            PT = sba("PT", [P, 2, 512])
        ffn = ExitStack()
        with ffn:
            hT_hi = ffn.enter_context(nc.sbuf_tensor("hT_hi", [P, FF // P, N], F32R))
            hT_lo = ffn.enter_context(nc.sbuf_tensor("hT_lo", [P, FF // P, N], F32R))
            G = ffn.enter_context(nc.sbuf_tensor("G", [P, T, CHUNK], F32))
            H = ffn.enter_context(nc.sbuf_tensor("H", [P, T, CHUNK], F32))
        ctx.enter_context(nc.sbuf_tensor("attention_or_ffn", [P, 7488 + 4096 + 6 * CAUSAL + 1024], F32))
        first = ExitStack()
        with first:
            masks = first.enter_context(nc.sbuf_tensor("masks", [P, 4, CAUSAL], F32))
            selected = first.enter_context(nc.sbuf_tensor("selected", [P, CAUSAL], F32))
            scores = first.enter_context(nc.sbuf_tensor("scores", [P, CAUSAL], F32))
            MKV = first.enter_context(nc.sbuf_tensor("MKV", [P, T * 512], F32))
            KI = first.enter_context(nc.sbuf_tensor("KI", [P, T * P], F32))
        second = ExitStack()
        with second:
            causal_2 = second.enter_context(nc.sbuf_tensor("causal_2", [P, CAUSAL], F32))
            bias = second.enter_context(nc.sbuf_tensor("bias", [P, SW_H, CAUSAL], F32))
        ctx.enter_context(nc.sbuf_tensor("first_or_second", [P, 4 * CAUSAL + 2 * CAUSAL + T * 512 + T * P], F32))
        sT_hi = ctx.enter_context(nc.sbuf_tensor("sT_hi", [P, 4, N], F32R))
        sT_lo = ctx.enter_context(nc.sbuf_tensor("sT_lo", [P, 4, N], F32R))

        acc = ctx.enter_context(nc.psum_tensor("acc", [P, 4, 512], F32))
        tps = ctx.enter_context(nc.psum_tensor("tps", [P, 2, 512], F32))
        ops = ctx.enter_context(nc.psum_tensor("ops", [P, 2, 512], F32))

        S = {n: sem(n) for n in (
            "ident_landed", "prologue_landed", "x_landed", "mem_landed", "lambda_terms", "lambda_exp", "angles",
            "trig_done", "rel_ready", "rel_rows_made", "rel_rows_saved", "mem_kv_saved",
            "mem_kv_landed", "bias_landed", "ple_landed", "out_landed", "hi_ready", "lo_ready",
            "unit_used", "acc_taken_dve", "acc_taken_act", "t_ready", "t_hi", "t_taken", "stage",
            "scores_ready", "logits_ready", "max_ready", "probs_ready", "mixed_ready", "pv_ready",
            "out_hi", "recips_ready", "act_normal", "pool_normal",
            "out_taken", "dve_chain", "act_chain", "index_ready", "index_relu", "index_added")}
        unit_landed = [sem(f"unit_landed{i}") for i in range(RAW)]
        gain_landed = [sem(f"gain_landed{i}") for i in range(2)]

        block = ctx.enter_context(nc.Block())

        def rows(src):
            if src == "x":
                return x[:]
            if src == "tmp":
                return tmp[:].rearrange("p (t c) -> p t c", t=T)
            if src == "H":
                return H[:]
            if src == "Y":
                return gain[:, :, 1, :]
            if src == "KI":
                return KI[:].rearrange("p (t c) -> p t c", t=T)
            if src == "MKV":
                return MKV[:].rearrange("p (t c) -> p t c", t=T)
            name, cols, off = src
            buf = {"U": U, "tmp": tmp}[name]
            if name == "tmp":
                off = 0
            return buf[:, off:off + T * cols].rearrange("p (t c) -> p t c", t=T)

        def act_split(name):
            return {"x": (xT_hi, xT_lo, 0), "h": (hT_hi, hT_lo, 0), "s": (sT_hi, sT_lo, 0),
                    "s2": (sT_hi, sT_lo, 2)}[name]

        def act_tile(name, k):
            if name == "mixed":
                name = "s" if k < 4 else "x"
            hi, lo, off = act_split(name)
            return hi[:, off + k], lo[:, off + k]

        def batch_dst(b, buf):
            _, d0, m, width, t = b.dst
            if t is None:
                return buf[0:width, d0:d0 + m, :].rearrange("p k n -> p (k n)")
            return buf[0:width, d0:d0 + m, P * t:P * t + P]

        def batch_src(b):
            _, _, m, width, t = b.dst
            if t is None:
                return tps[0:width, b.b % 2, 0:m * N]
            return tps[0:width, b.b % 2, 0:m * P].rearrange("p (k n) -> p k n", k=m)

        def step_logits(s):
            off = 3 * CAUSAL * (s.s % 2)
            return L[:, off:off + s.maps * s.width].rearrange("p (m c) -> p m c", m=s.maps)

        def tile_cols(s, t):
            if s.width == FULL:
                return slice(256 * t, 256 * t + 256)
            return slice(0, P) if t == 0 else slice(P, CAUSAL)

        def token_col(v):
            return v.rearrange("o (t p) -> p (o t)", p=P)

        PRO = [
            (masks[:], a["c_masks"]),
            (knorm[:, :, 0, :], a["idx_kn_g"].partition_broadcast(P)),
            (knorm[:, :, 1, :], a["idx_kn_b"].partition_broadcast(P)),
            (subln[:], a["da_subln_2"].partition_broadcast(P)),
            (qnorm[:], a["mla_q_norm_2"].partition_broadcast(P)),
            (kvnorm[:], a["mla_kv_norm_2"].partition_broadcast(P)),
            (sinks[:], a["sw_sinks_2"].partition_broadcast(P)),
            (L[:, 0:512], a["da_lambda_2"].rearrange("l f d -> (l f d)").partition_broadcast(P)),
            (L[:, 512:536], a["c_inv"]),
            (L[:, 536:538].bitcast(I32), token_col(a["positions"])),
            (L[:, 538:540].bitcast(I32), token_col(a["positions_2"])),
            (L[0:REL_BUCKETS, 1024:1024 + BIAS_HEADS], a["rel_bias_2"]),
            (L[0:REL_BUCKETS, 1152:1152 + REL_ROW], a["c_onehot"]),
            (L[0:BIAS_HEADS, 1536:1536 + REL_ROW], a["c_relmask"]),
        ]

        @block.sync
        def _(sp):
            def load_gain(g):
                slot = g.j % 2
                if g.j >= 2:
                    sp.wait_ge(S["stage"], gain_list[g.j - 2].stage)
                name, row = g.g
                src = a[name] if row is None else a[name][row]
                sp.dma_start(gain[:, slot, 0, :], src.partition_broadcast(P)).then_inc(gain_landed[slot], 16)
                if g.b[0]:
                    name, row = g.b
                    src = a[name] if row is None else a[name][row]
                    sp.dma_start(gain[:, slot, 1, :], src.partition_broadcast(P)).then_inc(gain_landed[slot], 16)

            sp.dma_start(rows("tmp"), a["mem"][0].rearrange("(t p) d -> p t d", p=P)).then_inc(S["mem_landed"], 16)
            load_gain(p.first_gain)
            for u in p.units:
                if u.u >= RAW:
                    sp.wait_ge(S["lo_ready"], u.u - RAW + 1)
                ch = u.chunk
                src = u.weight[u.k0 * P:(u.k0 + u.nk) * P, ch.col:ch.col + ch.width]
                sp.dma_start(raw[:, u.u % RAW, 0:u.nk, 0:ch.width],
                             src.rearrange("(k p) n -> p k n", p=P)).then_inc(unit_landed[u.u % RAW], 16)
                if u.u == RAW - 1:
                    sp.dma_start(x[:], a["x"][0].rearrange("(t p) d -> p t d", p=P)).then_inc(S["x_landed"], 16)
                if u.gain is not None:
                    load_gain(u.gain)
                if u.late_gain is not None:
                    load_gain(u.late_gain)
            sp.wait_ge(S["stage"], p.n_stage)
            sp.dma_start(out[0].rearrange("(t p) d -> p t d", p=P), x[:]).then_inc(S["out_landed"], 16)
            sp.wait_ge(S["out_landed"], 16)

        @block.gpsimd
        def _(pool):
            def split_unit(n):
                if n >= len(p.units):
                    return
                u = p.units[n]
                ch, slot, r = u.chunk, n % SPLIT, n % RAW
                pool.wait_ge(S["hi_ready"], n + 1)
                if n:
                    pool.wait_ge(S["lo_ready"], n)
                nc.gpsimd.tensor_tensor(w_lo[:, slot, 0:u.nk, 0:ch.width], raw[:, r, 0:u.nk, 0:ch.width],
                                        w_hi[:, slot, 0:u.nk, 0:ch.width].bitcast(F32),
                                        ALU.subtract).then_inc(S["lo_ready"], 1)

            def normalise(s):
                lg = step_logits(s)
                pool.wait_ge(S["recips_ready"], s.normal)
                for t in range(T):
                    part = lg[:, 0, tile_cols(s, t)]
                    by = recips[:, s.s % 2, t:t + 1].to_broadcast(list(part.shape))
                    ins = nc.gpsimd.tensor_tensor(part, part, by, ALU.mult)
                ins.then_inc(S["pool_normal"], 1)

            for n in range(AHEAD):
                split_unit(n)
            for ph in p.phases:
                if ph.kind == "linear":
                    for ch in ph.chunks:
                        for u in ch.units:
                            split_unit(u.u + AHEAD)
                elif ph.kind == "attention":
                    for s in ph.steps:
                        if s.pool_normal:
                            normalise(s)
                        for u in s.fill:
                            split_unit(u.u + AHEAD)

        @block.scalar
        def _(act):
            def split_unit(n):
                if n >= len(p.units):
                    return
                u = p.units[n]
                act.wait_ge(unit_landed[n % RAW], 16 * (n // RAW + 1))
                if n >= SPLIT:
                    act.wait_ge(S["unit_used"], n - SPLIT + 1)
                nc.scalar.copy(w_hi[:, n % SPLIT, 0:u.nk, 0:u.chunk.width],
                               raw[:, n % RAW, 0:u.nk, 0:u.chunk.width]).then_inc(S["hi_ready"], 1)

            def batch_hi(b):
                act.wait_ge(S["t_ready"], b.b + 1)
                hi, _, _ = act_split(b.dst[0])
                nc.scalar.copy(batch_dst(b, hi), batch_src(b)).then_inc(S["t_hi"], 1)

            act.dma_start(ident[:], a["c_ident"]).then_inc(S["ident_landed"], 16)
            with nc.allow_non_contiguous_dma(reason="the positions, one to a partition"):
                for dst, src in PRO:
                    act.dma_start(dst, src).then_inc(S["prologue_landed"], 16)
            started = [False]

            def start_units():
                if not started[0]:
                    started[0] = True
                    for n in range(1, AHEAD):
                        split_unit(n)

            split_unit(0)
            bias_loads = 0

            def take_chunk(ch):
                act.wait_ge(S["unit_used"], ch.last + 1)
                act.wait_ge(S["stage"], ch.stage_before)
                if ch.how == "silu":
                    fn = ACT.Silu
                    if ch.dst[0] == "G":
                        dst = G[:, :, 0:ch.width]
                        if ch.index:
                            act.wait_ge(S["acc_taken_dve"], ch.dve_taken_before)
                    else:
                        src, col = ch.dst
                        dst = rows(src)[:, :, col:col + ch.width]
                else:
                    fn = ACT.Sigmoid
                    _, _, col = ch.dst
                    dst = rows("tmp")[:, :, col:col + ch.width]
                    act.wait_ge(S["acc_taken_dve"], ch.dve_taken_before)
                nc.scalar.activation(dst, acc[:, ch.bank:ch.bank + 2, 0:ch.width], fn).then_inc(S["acc_taken_act"], 1)

            def after_unit(u):
                split_unit(u.u + AHEAD)
                if u.u == u.chunk.last and u.chunk.eng == "act":
                    take_chunk(u.chunk)

            def index_relu(g):
                act.wait_ge(S["index_ready"], g.n + 1)
                if g.n >= 2:
                    act.wait_ge(S["index_added"], g.n - 1)
                nc.scalar.activation(L[:, 512 * (g.n % 2):512 * (g.n % 2) + 512], ops[:, g.n % 2, :],
                                     ACT.Relu).then_inc(S["index_relu"], 1)

            def exponentials(s):
                lg, slot = step_logits(s), s.s % 2
                act.wait_ge(S["max_ready"], s.s + 1)
                if s.flavour == "sinks":
                    nc.scalar.activation(sink_exp[:, slot, :], sink_exp[:, slot, :], ACT.Exp)
                for m in range(1 if s.flavour == "dilated" else s.maps):
                    for t in range(T):
                        part = lg[:, :, tile_cols(s, t)] if s.flavour == "dilated" else lg[:, m, tile_cols(s, t)]
                        c = 2 * m + t
                        ins = nc.scalar.activation(part, part, ACT.Exp, bias=neg_max[:, slot, c:c + 1],
                                                   accum_out=sums[:, slot, c:c + 1])
                ins.then_inc(S["probs_ready"], 1)

            def normalise(s):
                lg, m = step_logits(s), 1 if s.pool_normal else 0
                act.wait_ge(S["recips_ready"], s.normal)
                for t in range(T):
                    part = lg[:, m, tile_cols(s, t)]
                    ins = nc.scalar.activation(part, part, ACT.Copy, scale=recips[:, s.s % 2, 2 * m + t:2 * m + t + 1])
                ins.then_inc(S["act_normal"], 1)

            def output_hi(s):
                act.wait_ge(S["pv_ready"], s.s + 1)
                for half, tile, p0, p1 in s.out:
                    hi, _ = act_tile("mixed", tile)
                    ins = nc.scalar.copy(hi[p0:p1], ops[p0:p1, s.s % 2, N * half:N * half + N])
                ins.then_inc(S["out_hi"], 1)

            for ph in p.phases:
                if ph.kind == "linear":
                    for ch in ph.chunks:
                        for u in ch.units:
                            for b in u.pre:
                                batch_hi(b)
                            for g in u.index:
                                index_relu(g)
                            after_unit(u)
                elif ph.kind == "tables":
                    act.wait_ge(S["lambda_terms"], 1)
                    nc.scalar.activation(small[:, 0, 4:8], small[:, 0, 0:4], ACT.Exp).then_inc(S["lambda_exp"], 1)
                    act.wait_ge(S["angles"], 1)
                    nc.scalar.activation(trig[:].rearrange("p s t f -> p (s t f)"), L[:, 640:736],
                                         ACT.Sin).then_inc(S["trig_done"], 1)
                    act.wait_ge(S["rel_rows_made"], 1)
                    act.dma_start(rel_rows, L[0:BIAS_HEADS, 1152:1152 + REL_ROW].unsqueeze(1)
                                  .to_broadcast([BIAS_HEADS, P, REL_ROW])).then_inc(S["rel_rows_saved"], 16)
                elif ph.kind == "transpose":
                    for b in ph.batches:
                        if b.split:
                            batch_hi(b)
                    start_units()
                elif ph.kind == "save_mem_kv":
                    act.wait_ge(S["acc_taken_dve"], ph.dve_taken)
                    for l in range(DEPTH):
                        act.dma_start(mem_kv[l], U[:, 1024 * l:1024 * l + 1024]).then_inc(S["mem_kv_saved"], 16)
                elif ph.kind == "load_mem_kv":
                    if ph.layer == 0:
                        act.wait_ge(S["mem_kv_saved"], 16 * DEPTH)
                    else:
                        act.wait_ge(S["pv_ready"], ph.steps_before)
                    act.dma_start(MKV[:], mem_kv[ph.layer]).then_inc(S["mem_kv_landed"], 16)
                elif ph.kind == "load_bias":
                    act.wait_ge(S["logits_ready"], ph.steps_before)
                    act.wait_ge(S["pv_ready"], ph.steps_before)
                    if bias_loads == 0:
                        act.wait_ge(S["rel_rows_saved"], 16)
                        act.dma_start(causal_2[:], a["c_masks"][:, 0, :]).then_inc(S["bias_landed"], 16)
                    bias_loads += 1
                    for off, lo, n in ((255, 0, P), (127, P, N)):
                        src = bass.AP(rel_rows.tensor, off + P * REL_ROW * ph.head,
                                      [[REL_ROW - 1, P], [P * REL_ROW, ph.heads], [1, n]])
                        act.dma_start(bias[:, 0:ph.heads, lo:lo + n], src).then_inc(S["bias_landed"], 16)
                elif ph.kind == "load_ple":
                    act.dma_start(rows(("U", 256, 3072)), a["p_2"][ph.layer, 0].rearrange("(t p) d -> p t d", p=P)
                                  ).then_inc(S["ple_landed"], 16)
                elif ph.kind == "attention":
                    exponentials(ph.steps[0])
                    for s in ph.steps:
                        if s.normal:
                            normalise(s)
                        if s.normal and s.i:
                            output_hi(ph.steps[s.i - 1])
                        for u in s.fill:
                            after_unit(u)
                        if s.i + 1 < len(ph.steps):
                            exponentials(ph.steps[s.i + 1])
                    if ph.steps[-1].normal:
                        output_hi(ph.steps[-1])

        @block.tensor
        def _(pe):
            def do_batch(b):
                if b.b >= 2:
                    pe.wait_ge(S["t_taken"], b.b - 1)
                pe.wait_ge(S[b.after[0]], b.after[1])
                for i, (src, t, col, width) in enumerate(b.moves):
                    ins = nc.tensor.transpose(tps[0:width, b.b % 2, P * i:P * i + P],
                                              rows(src)[:, t, col:col + width], ident[:])
                ins.then_inc(S["t_ready"], 1)

            def index_scores(g):
                pe.wait_ge(S["t_taken"], g.t_need)
                pe.wait_ge(S["rel_rows_made"], 1)
                if g.steps_before:
                    pe.wait_ge(S["out_taken"], g.steps_before)
                if g.n >= 2:
                    pe.wait_ge(S["index_relu"], g.n - 1)
                w = P * (g.t + 1)
                for i, h in enumerate(g.heads):
                    base = HD * (h % 2)
                    ins = nc.tensor.matmul(ops[:, g.n % 2, w * i:w * i + w],
                                           QT[base:base + HD, h // 2, P * g.t:P * g.t + P],
                                           KT[base:base + HD, 0, 0:w], start=True, stop=True)
                ins.then_inc(S["index_ready"], 1)

            def do_unit(u):
                ch = u.chunk
                if u.k0 == 0:
                    for name, count in ch.free_when:
                        pe.wait_ge(S[name], count)
                for b in u.pre:
                    do_batch(b)
                for g in u.index:
                    index_scores(g)
                if u.out_need:
                    pe.wait_ge(S["out_taken"], u.out_need)
                else:
                    pe.wait_ge(S["t_taken"], u.t_need)
                pe.wait_ge(S["lo_ready"], u.u + 1)
                slot = u.u % SPLIT
                for k in range(u.nk):
                    hi, lo = act_tile(ch.acts, u.k0 + k)
                    first_k, last_k = u.k0 + k == 0, u.k0 + k == ch.k_tiles - 1
                    for t in range(T):
                        o = acc[:, ch.bank + t, 0:ch.width]
                        tok = slice(P * t, P * t + P)
                        wh, wl = w_hi[:, slot, k, 0:ch.width], w_lo[:, slot, k, 0:ch.width]
                        nc.tensor.matmul(o, hi[:, tok], wh, start=first_k, stop=False)
                        nc.tensor.matmul(o, hi[:, tok], wl, start=False, stop=False)
                        ins = nc.tensor.matmul(o, lo[:, tok], wh, start=False, stop=last_k)
                ins.then_inc(S["unit_used"], 1)

            def do_scores(s):
                for b in s.before:
                    do_batch(b)
                if s.before:
                    pe.wait_ge(S["t_taken"], s.before[-1].b + 1)
                for name, count in s.free_when:
                    pe.wait_ge(S[name], count)
                for m in range(s.maps):
                    (qt, base, k), (kt, kbase, _) = s.q[m], s.k[m]
                    for t in range(T):
                        c = tile_cols(s, t)
                        ins = nc.tensor.matmul(acc[:, s.bank + m, c], QT[base:base + k, qt, P * t:P * t + P],
                                               KT[kbase:kbase + k, kt, 0:c.stop - c.start],
                                               start=True, stop=True)
                ins.then_inc(S["scores_ready"], 1)

            def turn(s):
                lg = step_logits(s)
                if s.mixed:
                    pe.wait_ge(S["mixed_ready"], s.mixed)
                elif not s.normal:
                    pe.wait_ge(S["probs_ready"], s.s + 1)
                for tb in s.tb:
                    if s.normal and tb.j == 0 and s.pool_normal:
                        pe.wait_ge(S["pool_normal"], s.pool_normal)
                    elif s.normal:
                        pe.wait_ge(S["act_normal"], s.normal)
                    pe.wait_ge(S["t_taken"], tb.b - 1)
                    for i in range(tb.blocks):
                        ins = nc.tensor.transpose(tps[:, tb.b % 2, P * i:P * i + P],
                                                  lg[:, tb.j, P * i:P * i + P], ident[:])
                    ins.then_inc(S["t_ready"], 1)

            def do_values(s):
                if s.s >= 2:
                    pe.wait_ge(S["out_taken"], s.s - 1)
                if s.v_taken:
                    pe.wait_ge(S["acc_taken_dve"], s.v_taken)
                if s.normal:
                    pe.wait_ge(S["t_taken"], s.tb[-1].b + 1)
                    for src, col, n, m, half, p0 in s.v:
                        o = ops[p0:p0 + n, s.s % 2, N * half:N * half + N]
                        for kt in range(T):
                            if s.width == FULL:
                                o_part = o.rearrange("e (t q) -> e t q", t=T)
                                blocks = PT[:, m, :].rearrange("p (t k q) -> p t k q", t=T, k=T)[:, :, kt, :]
                            else:
                                o_part, blocks = o[:, P * kt:N], PT[:, m, N * kt:N + P * kt]
                            ins = nc.tensor.matmul(o_part, rows(src)[:, kt, col:col + n], blocks,
                                                   start=kt == 0, stop=kt == T - 1)
                    ins.then_inc(S["pv_ready"], 1)
                    return
                for tb, (src, col) in zip(s.tb, s.v):
                    pe.wait_ge(S["t_taken"], tb.b + 1)
                    for t in range(T):
                        o0 = (tb.j * T + t) * s.dv
                        keys = range(T) if s.width == FULL else range(t + 1)
                        for kt in keys:
                            blk = tile_cols(s, t).start + P * kt
                            ins = nc.tensor.matmul(ops[:, s.s % 2, o0:o0 + s.dv], PT[:, tb.j, blk:blk + P],
                                                   rows(src)[:, kt, col:col + s.dv],
                                                   start=kt == 0, stop=kt == keys[-1])
                ins.then_inc(S["pv_ready"], 1)

            pe.wait_ge(S["ident_landed"], 16)
            for ph in p.phases:
                if ph.kind == "transpose":
                    for b in ph.batches:
                        do_batch(b)
                elif ph.kind == "linear":
                    for ch in ph.chunks:
                        for u in ch.units:
                            do_unit(u)
                elif ph.kind == "tables":
                    pe.wait_ge(S["prologue_landed"], 16 * len(PRO))
                    nc.tensor.matmul(ops[0:BIAS_HEADS, 0, 0:REL_ROW], L[0:REL_BUCKETS, 1024:1024 + BIAS_HEADS],
                                     L[0:REL_BUCKETS, 1152:1152 + REL_ROW], start=True, stop=True
                                     ).then_inc(S["rel_ready"], 1)
                elif ph.kind == "attention":
                    pe.wait_ge(S["t_taken"], ph.t_need)
                    if ph.index_before:
                        pe.wait_ge(S["index_relu"], ph.index_before)
                    do_scores(ph.steps[0])
                    for s in ph.steps:
                        for other in s.ahead:
                            do_scores(other)
                        if s.i:
                            do_values(ph.steps[s.i - 1])
                        for u in s.fill:
                            do_unit(u)
                        turn(s)
                    do_values(ph.steps[-1])

        @block.vector
        def _(dve):
            v = nc.vector
            chain = [0]

            def link(ins):
                chain[0] += 1
                ins.then_inc(S["dve_chain"], 1)
                dve.wait_ge(S["dve_chain"], chain[0])

            def rsqrt(y, var, n):
                a1, a2 = small[:, 8, 0:n], small[:, 9, 0:n]
                v.tensor_scalar(a2, var, -0.5, None, ALU.mult)
                link(v.tensor_scalar(a1.bitcast(I32), var.bitcast(I32), 1, None, ALU.logical_shift_right))
                link(v.tensor_scalar(y.bitcast(I32), a1.bitcast(I32), -1.0, float(0x5F3759DF), ALU.mult, ALU.add))
                for _ in range(3):
                    if n == T:
                        for t in range(T):
                            one = slice(t, t + 1)
                            ins = v.scalar_tensor_tensor(out=a1[:, one], in0=y[:, one], scalar=a2[:, one],
                                                         in1=y[:, one], op0=ALU.mult, op1=ALU.mult)
                        link(ins)
                    else:
                        link(v.tensor_tensor(a1, y, y, ALU.mult))
                        link(v.tensor_tensor(a1, a1, a2, ALU.mult))
                    link(v.scalar_tensor_tensor(out=y, in0=a1, scalar=1.5, in1=y, op0=ALU.add, op1=ALU.mult))

            mean_var, rs = small[:, 1, 0:4], small[:, 2, 0:2]

            def norm_scale(width, eps):
                for t in range(T):
                    ins = v.bn_aggr(mean_var[:, 2 * t:2 * t + 2], stats[:, t, 0:-(-width // 512), :])
                link(ins)
                var = small[:, 3, 0:2]
                link(v.tensor_scalar(var, mean_var[:, 1:4:2], eps, None, ALU.add))
                rsqrt(rs, var, 2)

            def norm_apply(src, dst, g, cols, done=None):
                gg, bb = g
                for t in range(T):
                    ins = v.scalar_tensor_tensor(out=src[:, t, cols], in0=src[:, t, cols],
                                                 scalar=mean_var[:, 2 * t:2 * t + 1], in1=gg[:, cols],
                                                 op0=ALU.subtract, op1=ALU.mult)
                link(ins)
                for t in range(T):
                    ins = v.scalar_tensor_tensor(out=dst[:, t, cols], in0=src[:, t, cols], scalar=rs[:, t:t + 1],
                                                 in1=bb[:, cols], op0=ALU.mult, op1=ALU.add)
                    if done is not None:
                        ins.then_inc(done, 1)
                if done is None:
                    link(ins)

            def rms_scale(src, width):
                ms = small[:, 1, 0:2]
                for t in range(T):
                    ins = v.tensor_tensor_reduce(out=L[:, t * width:(t + 1) * width], in0=src[:, t, :],
                                                 in1=src[:, t, :], scale=1.0, scalar=0.0, op0=ALU.mult, op1=ALU.add,
                                                 accum_out=ms[:, t:t + 1])
                link(ins)
                link(v.tensor_scalar(small[:, 3, 0:2], ms, 1.0 / width, RMS_EPS, ALU.mult, ALU.add))
                rsqrt(rs, small[:, 3, 0:2], 2)

            def rms_apply(src, dst, g, cols, done=None):
                for t in range(T):
                    ins = v.scalar_tensor_tensor(out=dst[:, t, cols], in0=src[:, t, cols], scalar=rs[:, t:t + 1],
                                                 in1=g[:, cols], op0=ALU.mult, op1=ALU.mult)
                    if done is not None:
                        ins.then_inc(done, 1)
                if done is None:
                    link(ins)

            HALF = (slice(0, D // 2), slice(D // 2, D))

            def rms_post(cols, g, done):
                z = rows("tmp")
                rms_apply(z, z, g, cols)
                for t in range(T):
                    v.tensor_tensor(x[:, t, cols], x[:, t, cols], z[:, t, cols], ALU.add).then_inc(done, 1)

            def rope(heads, n, f0, half, out=None):
                x1, x2 = heads[:, :, :, 0:half], heads[:, :, :, half:2 * half]
                size = T * n * half
                cs = trig[:, 1, :, f0:f0 + half].unsqueeze(2).to_broadcast([P, T, n, half])
                sn = trig[:, 0, :, f0:f0 + half].unsqueeze(2).to_broadcast([P, T, n, half])
                tm = [L[:, i * size:(i + 1) * size].rearrange("p (t n f) -> p t n f", t=T, n=n) for i in range(4)]
                v.tensor_tensor(tm[0], x1, cs, ALU.mult)
                v.tensor_tensor(tm[1], x2, sn, ALU.mult)
                v.tensor_tensor(tm[2], x2, cs, ALU.mult)
                link(v.tensor_tensor(tm[3], x1, sn, ALU.mult))
                v.tensor_tensor(x1, tm[0], tm[1], ALU.subtract)
                link(v.tensor_tensor(x2, tm[2], tm[3], ALU.add))

            def tables():
                dve.wait_ge(S["prologue_landed"], 16 * len(PRO))
                lf = L[:, 0:512].rearrange("p (l f d) -> p l f d", l=2, f=4)
                pr = L[:, 768:1024].rearrange("p (l f d) -> p l f d", l=2, f=2)
                link(v.tensor_tensor(pr, lf[:, :, 0:4:2, :], lf[:, :, 1:4:2, :], ALU.mult))
                v.tensor_reduce(small[:, 0, 0:4], pr.rearrange("p l f d -> p (l f) d"), AX.X,
                                ALU.add).then_inc(S["lambda_terms"], 1)
                link(v.tensor_copy(L[:, 540:544], L[:, 536:540].bitcast(I32)))
                ang = L[:, 544:592].rearrange("p (t f) -> p t f", t=T)
                for t in range(T):
                    v.tensor_scalar(ang[:, t, 0:8], L[:, 512:520], L[:, 540 + t:541 + t], None, ALU.mult)
                    ins = v.tensor_scalar(ang[:, t, 8:24], L[:, 520:536], L[:, 542 + t:543 + t], None, ALU.mult)
                link(ins)
                n_turn, r = L[:, 592:640], L[:, 640:736]
                angf = L[:, 544:592]
                for i, quarter in enumerate((0.0, 0.25)):
                    rr = r[:, 48 * i:48 * i + 48]
                    link(v.tensor_scalar(n_turn, angf, 1 / (2 * math.pi), quarter, ALU.mult, ALU.add))
                    link(v.tensor_scalar(n_turn, n_turn, ROUND, None, ALU.add))
                    link(v.tensor_scalar(n_turn, n_turn, ROUND, None, ALU.subtract))
                    link(v.scalar_tensor_tensor(out=rr, in0=n_turn, scalar=-TWO_PI_1, in1=angf, op0=ALU.mult, op1=ALU.add))
                    link(v.scalar_tensor_tensor(out=rr, in0=n_turn, scalar=-TWO_PI_2, in1=rr, op0=ALU.mult, op1=ALU.add))
                    link(v.scalar_tensor_tensor(out=rr, in0=n_turn, scalar=-TWO_PI_3, in1=rr, op0=ALU.mult, op1=ALU.add))
                    if i:
                        link(v.tensor_scalar(rr, rr, math.pi / 2, None, ALU.add))
                v.tensor_scalar(r, r, PI_INSIDE, -PI_INSIDE, ALU.min, ALU.max).then_inc(S["angles"], 1)
                link(v.tensor_scalar(neg_sinks[:], sinks[:], -1.0, None, ALU.mult))
                dve.wait_ge(S["rel_ready"], 1)
                v.tensor_tensor(L[0:BIAS_HEADS, 1152:1152 + REL_ROW], ops[0:BIAS_HEADS, 0, 0:REL_ROW],
                                L[0:BIAS_HEADS, 1536:1536 + REL_ROW], ALU.add).then_inc(S["rel_rows_made"], 1)
                dve.wait_ge(S["lambda_exp"], 1)
                for l in range(DEPTH_2):
                    lam_init = 0.8 - 0.6 * math.exp(-0.3 * l)
                    link(v.tensor_tensor(small[:, 0, 8 + l:9 + l], small[:, 0, 5 + 2 * l:6 + 2 * l],
                                         small[:, 0, 4 + 2 * l:5 + 2 * l], ALU.subtract))
                    link(v.tensor_scalar(neg_lam[:, l:l + 1], small[:, 0, 8 + l:9 + l], lam_init, None, ALU.subtract))
                dve.wait_ge(S["trig_done"], 1)
                dve.wait_ge(S["rel_rows_saved"], 16)

            gain_count = [0, 0]

            def gains(g):
                slot = g.j % 2
                gain_count[slot] += 32 if g.b[0] else 16
                dve.wait_ge(gain_landed[slot], gain_count[slot])
                return gain[:, slot, 0, :], gain[:, slot, 1, :]

            def take_batch(b):
                ps = batch_src(b)
                if b.split:
                    hi, lo, _ = act_split(b.dst[0])
                    dve.wait_ge(S["t_hi"], b.hi)
                    ins = v.tensor_tensor(batch_dst(b, lo), ps, batch_dst(b, hi).bitcast(F32), ALU.subtract)
                else:
                    dve.wait_ge(S["t_ready"], b.b + 1)
                    ins = v.tensor_copy(batch_dst(b, {"QT": QT, "KT": KT}[b.dst[0]]), ps)
                ins.then_inc(S["t_taken"], 1)

            def take_chunk(ch):
                ps = acc[:, ch.bank:ch.bank + 2, 0:ch.width]
                dve.wait_ge(S["unit_used"], ch.last + 1)
                dve.wait_ge(S["stage"], ch.stage_before)
                if ch.how == "copy":
                    if not saved[0]:
                        saved[0] = True
                        dve.wait_ge(S["mem_kv_saved"], 16 * DEPTH)
                    src, col = ch.dst
                    ins = v.tensor_copy(rows(src)[:, :, col:col + ch.width], ps)
                elif ch.how == "mem_kv":
                    l = ch.dst
                    ins = v.tensor_copy(rows(("U", 512, 1024 * l)), ps)
                elif ch.how == "residual":
                    c = slice(ch.dst, ch.dst + ch.width)
                    y = rows("tmp")
                    for t in range(T):
                        ins = v.scalar_tensor_tensor(out=y[:, t, c], in0=x[:, t, c], scalar=ALPHA, in1=ps[:, t, :],
                                                     op0=ALU.mult, op1=ALU.add)
                    link(ins)
                    for t in range(T):
                        ins = v.bn_stats(stats[:, t, ch.dst // 512, :], y[:, t, c])
                elif ch.how == "up":
                    dve.wait_ge(S["acc_taken_act"], ch.act_taken)
                    ins = v.tensor_tensor(H[:, :, 0:ch.width], G[:, :, 0:ch.width], ps, ALU.mult)
                elif ch.how in ("branch_first", "branch"):
                    dve.wait_ge(S["acc_taken_act"], ch.act_taken)
                    c = slice(ch.dst, ch.dst + ch.width)
                    y, gate = rows("Y")[:, :, c], rows("tmp")[:, :, c]
                    if ch.how == "branch_first":
                        ins = v.tensor_tensor(y, gate, ps, ALU.mult)
                    else:
                        link(v.tensor_tensor(gate, gate, ps, ALU.mult))
                        ins = v.tensor_tensor(y, y, gate, ALU.add)
                ins.then_inc(S["acc_taken_dve"], 1)

            norm_now = [None]
            saved = [False]

            def index_add(g):
                wi = rows(g.src)[:, :, 2816:2816 + IDXH]
                w = P * (g.t + 1)
                dst = scores[:, 0:P] if g.t == 0 else scores[:, P:CAUSAL]
                dve.wait_ge(S["index_relu"], g.n + 1)
                for i, h in enumerate(g.heads):
                    at = 512 * (g.n % 2) + w * i
                    relu, weight = L[:, at:at + w], wi[:, g.t, h:h + 1]
                    if h == 0:
                        ins = v.tensor_scalar(dst, relu, weight, None, ALU.mult)
                    else:
                        ins = v.scalar_tensor_tensor(out=dst, in0=relu, scalar=weight, in1=dst,
                                                     op0=ALU.mult, op1=ALU.add)
                    if h != g.heads[-1]:
                        link(ins)
                ins.then_inc(S["index_added"], 1)
                dve.wait_ge(S["index_added"], g.n + 1)

            def top_k(rounds, done):
                best = small[:, 4:6, 0:8]
                if rounds[0] == 0:
                    link(v.tensor_tensor(scores[:], scores[:], masks[:, 0, :], ALU.add))
                for _ in range(*rounds):
                    for t, c in ((0, slice(0, P)), (1, slice(P, CAUSAL))):
                        ins = v.max(best[:, t, :], scores[:, c])
                    link(ins)
                    for t, c in ((0, slice(0, P)), (1, slice(P, CAUSAL))):
                        ins = v.match_replace(scores[:, c], best[:, t, :], scores[:, c], SENTINEL)
                    link(ins)
                if rounds[1] < TOPK // 8:
                    v.memset(small[:, 7, 0:1], 0.0).then_inc(done, 1)
                    return
                link(v.tensor_scalar(selected[:], scores[:], SENTINEL, NEG, ALU.not_equal, ALU.mult))
                v.tensor_tensor(selected[:], selected[:], masks[:, 0, :], ALU.add).then_inc(done, 1)

            def do_stage(ph):
                done = S["stage"]
                if ph.n > ph.incs:
                    dve.wait_ge(done, ph.n - ph.incs)
                fn = ph.fn
                if fn == "mem_norm":
                    dve.wait_ge(S["mem_landed"], 16)
                    m = rows("tmp")
                    for t in range(T):
                        for c in range(2):
                            ins = v.bn_stats(stats[:, t, c, :], m[:, t, 512 * c:512 * c + 512])
                    link(ins)
                    norm_scale(D, LN_EPS)
                    norm_now[0] = (m, m, gains(ph.gain))
                    norm_apply(*norm_now[0], HALF[0], done)
                elif fn == "layer_norm":
                    dve.wait_ge(S["acc_taken_dve"], ph.dve_taken)
                    norm_scale(D, LN_EPS)
                    norm_now[0] = (rows("tmp"), x[:], gains(ph.gain))
                    norm_apply(*norm_now[0], HALF[0], done)
                elif fn == "norm_rest":
                    norm_apply(*norm_now[0], HALF[1], done)
                elif fn == "rope_index":
                    dve.wait_ge(S["acc_taken_dve"], ph.dve_taken)
                    r = rows(ph.src)
                    ki = r[:, :, 2824:2888]
                    for t in range(T):
                        ins = v.bn_stats(stats[:, t, 0, :], ki[:, t, :])
                    link(ins)
                    norm_scale(HD, LN_EPS)
                    norm_apply(ki, ki, (knorm[:, ph.layer, 0, :], knorm[:, ph.layer, 1, :]), slice(0, HD))
                    rope(ki.unsqueeze(2), 1, 0, 8)
                    twice = rows("KI").rearrange("p t (m d) -> p t m d", m=2)
                    v.tensor_copy(twice, ki.unsqueeze(2).to_broadcast([P, T, 2, HD]))
                    rope(r[:, :, 2304:2816].rearrange("p t (n d) -> p t n d", d=HD), IDXH, 0, 8)
                    wi = r[:, :, 2816:2816 + IDXH]
                    v.tensor_scalar(wi, wi, (IDXH * HD) ** -0.5, None, ALU.mult).then_inc(done, 1)
                elif fn == "rope_heads":
                    dve.wait_ge(S["acc_taken_dve"], ph.dve_taken)
                    rope(rows(ph.src)[:, :, 0:2 * MIX].rearrange("p t (n d) -> p t n d", d=HD), 2 * HEADS, 0, 8)
                    v.memset(small[:, 7, 0:1], 0.0).then_inc(done, 1)
                elif fn == "top_k":
                    top_k(ph.src, done)
                elif fn == "rms_pre":
                    dve.wait_ge(S["acc_taken_dve"], ph.dve_taken)
                    rms_scale(x[:], D)
                    norm_now[0] = gains(ph.gain)[0]
                    rms_apply(x[:], rows("tmp"), norm_now[0], HALF[0], done)
                elif fn == "rms_pre_rest":
                    rms_apply(x[:], rows("tmp"), norm_now[0], HALF[1], done)
                elif fn == "rms_post":
                    dve.wait_ge(S["acc_taken_dve"], ph.dve_taken)
                    rms_scale(rows("tmp"), D)
                    norm_now[0] = gains(ph.gain)[0]
                    rms_post(HALF[0], norm_now[0], done)
                elif fn == "rms_post_rest":
                    rms_post(HALF[1], norm_now[0], done)
                elif fn == "ple_add":
                    dve.wait_ge(S["acc_taken_act"], ph.act_need)
                    dve.wait_ge(S["acc_taken_dve"], ph.dve_taken)
                    c = slice(ph.dst[0], ph.dst[0] + ph.dst[1])
                    gate = rows("tmp")[:, :, c]
                    link(v.tensor_tensor(gate, gate, rows(ph.src)[:, :, c], ALU.mult))
                    v.tensor_tensor(x[:, :, c], x[:, :, c], gate, ALU.add).then_inc(done, 1)
                elif fn == "sub_norm":
                    dve.wait_ge(S["out_taken"], ph.steps_before)
                    o = rows(ph.src)[:, :, 0:512]
                    lam_init = 0.8 - 0.6 * math.exp(-0.3 * ph.layer)
                    sq = L[:, 0:1024].rearrange("p (t c) -> p t c", t=T)
                    link(v.tensor_tensor(sq, o, o, ALU.mult))
                    link(v.tensor_reduce(small[:, 1, 0:8], sq.rearrange("p t (h e) -> p (t h) e", e=P), AX.X, ALU.add))
                    link(v.tensor_scalar(small[:, 3, 0:8], small[:, 1, 0:8], 1.0 / P, RMS_EPS, ALU.mult, ALU.add))
                    rsqrt(small[:, 2, 0:8], small[:, 3, 0:8], 8)
                    link(v.tensor_scalar(small[:, 2, 0:8], small[:, 2, 0:8], 1.0 - lam_init, None, ALU.mult))
                    heads = o.rearrange("p t (h e) -> p t h e", e=P)
                    rs = small[:, 2, 0:8].rearrange("p (t h) -> p t h", t=T).unsqueeze(3).to_broadcast([P, T, DA_H, P])
                    link(v.tensor_tensor(heads, heads, rs, ALU.mult))
                    gg = subln[:, ph.layer, :].unsqueeze(1).unsqueeze(1).to_broadcast([P, T, DA_H, P])
                    link(v.tensor_tensor(heads, heads, gg, ALU.mult))
                    dve.wait_ge(S["acc_taken_act"], ph.act_taken)
                    v.tensor_tensor(o, o, rows(ph.src)[:, :, 1536:2048], ALU.mult).then_inc(done, 1)
                elif fn == "gate_mixed":
                    dve.wait_ge(S["out_taken"], ph.steps_before)
                    dve.wait_ge(S["acc_taken_act"], ph.act_taken)
                    o = rows(ph.src)[:, :, 0:512]
                    src, col = ph.z
                    v.tensor_tensor(o, o, rows(src)[:, :, col:col + 512], ALU.mult).then_inc(done, 1)
                elif fn == "latent_norm":
                    dve.wait_ge(S["acc_taken_dve"], ph.dve_taken)
                    r = rows(ph.src)
                    for cols, g in ((slice(0, 256), qnorm), (slice(256, 384), kvnorm)):
                        part, width = r[:, :, cols], cols.stop - cols.start
                        rms_scale(part, width)
                        rms_apply(part, part, g[:, ph.layer, :], slice(0, width))
                    rope(r[:, :, 384:416].unsqueeze(2), 1, 8, 16)
                    v.memset(small[:, 7, 0:1], 0.0).then_inc(done, 1)
                elif fn == "latent_rope_q":
                    dve.wait_ge(S["acc_taken_dve"], ph.dve_taken)
                    heads = rows(ph.src).rearrange("p t (n d) -> p t n d", d=MLA_K)
                    rope(heads[:, :, :, HD:MLA_K], MLA_H, 8, 16)
                    v.memset(small[:, 7, 0:1], 0.0).then_inc(done, 1)
                elif fn == "latent_keys":
                    dve.wait_ge(S["t_ready"], ph.t_need)
                    heads = rows(ph.dst).rearrange("p t (n d) -> p t n d", d=MLA_K)
                    kv = rows(ph.src).rearrange("p t (n d) -> p t n d", d=P)
                    for t in range(T):
                        v.tensor_copy(heads[:, t, :, 0:HD], kv[:, t, :, 0:HD])
                        kr = rows(ph.low)[:, t, 384:416].unsqueeze(1).to_broadcast([P, MLA_H, 32])
                        ins = v.tensor_copy(heads[:, t, :, HD:MLA_K], kr)
                    ins.then_inc(done, 1)
                elif fn == "twice_keys":
                    dve.wait_ge(S["acc_taken_dve"], ph.dve_taken)
                    k2 = rows(ph.dst).rearrange("p t (h m d) -> p t h m d", h=2, m=2)
                    for t in range(T):
                        k1 = rows(ph.src)[:, t, 512:640].rearrange("p (h d) -> p h d", h=2)
                        ins = v.tensor_copy(k2[:, t], k1.unsqueeze(2).to_broadcast([P, 2, 2, HD]))
                    ins.then_inc(done, 1)
                else:
                    raise ValueError(fn)

            def attention(ph):
                def mask_of(s):
                    if s.flavour == "dilated":
                        return masks[:, 1:4, :]
                    if s.flavour == "sinks":
                        return bias[:, s.bias_row:s.bias_row + 2, :]
                    if s.mask == "bias":
                        return bias[:, s.bias_row:s.bias_row + 1, :].to_broadcast([P, 2, CAUSAL])
                    if s.mask == "selected":
                        return selected[:].unsqueeze(1).to_broadcast([P, 2, CAUSAL])
                    m = masks[:, 0, :] if ph.block == 1 else causal_2[:]
                    return m.unsqueeze(1).to_broadcast([P, 2, CAUSAL])

                if ph.steps[0].mask == "bias":
                    dve.wait_ge(S["bias_landed"], ph.bias_need)
                if ph.steps[0].mask == "selected":
                    dve.wait_ge(S["stage"], ph.stage_need)

                def logits(s):
                    lg, slot = step_logits(s), s.s % 2
                    dve.wait_ge(S["scores_ready"], s.s + 1)
                    ps = acc[:, s.bank:s.bank + s.maps, 0:s.width]
                    if s.width == FULL:
                        ins = v.tensor_scalar(lg, ps, s.scale, None, ALU.mult)
                    else:
                        ins = v.scalar_tensor_tensor(out=lg, in0=ps, scalar=s.scale, in1=mask_of(s),
                                                     op0=ALU.mult, op1=ALU.add)
                    ins.then_inc(S["logits_ready"], 1)

                def maxima(s):
                    lg, slot = step_logits(s), s.s % 2
                    dve.wait_ge(S["logits_ready"], s.s + 1)
                    nm = neg_max[:, slot, :]
                    for t in range(T):
                        part = lg[:, :, tile_cols(s, t)]
                        if s.flavour == "dilated":
                            ins = v.tensor_reduce(nm[:, t:t + 1], part, AX.XY, ALU.max, negate=True)
                        else:
                            ins = v.tensor_reduce(nm[:, t:t + 3:2], part, AX.X, ALU.max, negate=True)
                    if s.flavour == "sinks":
                        link(ins)
                        nm2 = nm.rearrange("p (m t) -> p m t", m=2)
                        h = slice(2 * s.i, 2 * s.i + 2)
                        link(v.tensor_tensor(nm2, nm2, neg_sinks[:, ph.layer, h].unsqueeze(2).to_broadcast([P, 2, T]),
                                             ALU.min))
                        ins = v.tensor_tensor(sink_exp[:, slot, :].rearrange("p (m t) -> p m t", m=2), nm2,
                                              sinks[:, ph.layer, h].unsqueeze(2).to_broadcast([P, 2, T]), ALU.add)
                    ins.then_inc(S["max_ready"], 1)

                def combine(s):
                    lg, slot = step_logits(s), s.s % 2
                    dve.wait_ge(S["probs_ready"], s.s + 1)
                    if s.s >= 2:
                        dve.wait_ge(S["out_taken"], s.s - 1)
                    rc, sm = recips[:, slot, :], sums[:, slot, :]
                    if s.normal:
                        if s.flavour == "dilated":
                            link(v.tensor_tensor(lg[:, 0, :], lg[:, 0, :], lg[:, 1, :], ALU.add))
                            v.tensor_tensor(lg[:, 0, :], lg[:, 0, :], lg[:, 2, :], ALU.add)
                            v.reciprocal(rc[:, 0:2], sm[:, 0:2]).then_inc(S["recips_ready"], 1)
                        else:
                            v.reciprocal(rc, sm).then_inc(S["recips_ready"], 1)
                        return
                    if s.flavour == "sinks":
                        link(v.tensor_tensor(sm, sm, sink_exp[:, slot, :], ALU.add))
                    link(v.reciprocal(rc, sm))
                    if s.flavour == "differential":
                        link(v.tensor_scalar(rc[:, 2:4], rc[:, 2:4], neg_lam[:, ph.layer:ph.layer + 1], None, ALU.mult))
                        for t in range(T):
                            c = tile_cols(s, t)
                            ins = v.tensor_scalar(lg[:, 1, c], lg[:, 1, c], rc[:, 2 + t:3 + t], None, ALU.mult)
                        link(ins)
                        for t in range(T):
                            c = tile_cols(s, t)
                            ins = v.scalar_tensor_tensor(out=lg[:, 0, c], in0=lg[:, 0, c], scalar=rc[:, t:t + 1],
                                                         in1=lg[:, 1, c], op0=ALU.mult, op1=ALU.add)
                        ins.then_inc(S["mixed_ready"], 1)

                def take_turns(s):
                    for tb in s.tb:
                        dve.wait_ge(S["t_ready"], tb.b + 1)
                        v.tensor_copy(PT[:, tb.j, 0:tb.blocks * P],
                                      tps[:, tb.b % 2, 0:tb.blocks * P]).then_inc(S["t_taken"], 1)

                def outputs(s):
                    slot, rc = s.s % 2, recips[:, s.s % 2, :]
                    if s.normal:
                        dve.wait_ge(S["out_hi"], s.normal)
                        for half, tile, p0, p1 in s.out:
                            hi, lo = act_tile("mixed", tile)
                            ins = v.tensor_tensor(lo[p0:p1], ops[p0:p1, slot, N * half:N * half + N],
                                                  hi[p0:p1].bitcast(F32), ALU.subtract)
                        ins.then_inc(S["out_taken"], 1)
                        return
                    dve.wait_ge(S["pv_ready"], s.s + 1)
                    dst = rows(s.heads_out)[:, :, s.out:s.out + (s.dv if s.mixed else P)]
                    if s.flavour == "differential":
                        ins = v.tensor_copy(dst, ops[:, slot, 0:T * P].rearrange("p (t e) -> p t e", t=T))
                    else:
                        o = ops[:, slot, 0:4 * HD].rearrange("p (m t e) -> p m t e", m=2, t=T)
                        r4 = rc.rearrange("p (m t) -> p m t", m=2).unsqueeze(3).to_broadcast([P, 2, T, HD])
                        ins = v.tensor_tensor(dst.rearrange("p t (m e) -> p m t e", m=2), o, r4, ALU.mult)
                    ins.then_inc(S["out_taken"], 1)

                logits(ph.steps[0])
                maxima(ph.steps[0])
                for s in ph.steps:
                    for other in s.ahead:
                        for b in other.before:
                            take_batch(b)
                    combine(s)
                    if s.i + 1 < len(ph.steps):
                        logits(ph.steps[s.i + 1])
                        maxima(ph.steps[s.i + 1])
                    if s.i:
                        outputs(ph.steps[s.i - 1])
                    for u in s.fill:
                        if u.u == u.chunk.last and u.chunk.eng == "dve":
                            take_chunk(u.chunk)
                    take_turns(s)
                outputs(ph.steps[-1])

            for ph in p.phases:
                if ph.kind == "stage":
                    do_stage(ph)
                elif ph.kind == "transpose":
                    for b in ph.batches:
                        take_batch(b)
                elif ph.kind == "linear":
                    for ch in ph.chunks:
                        for u in ch.units:
                            for b in u.pre:
                                take_batch(b)
                            for g in u.index:
                                index_add(g)
                        if ch.eng == "dve":
                            take_chunk(ch)
                elif ph.kind == "tables":
                    tables()
                elif ph.kind == "attention":
                    attention(ph)


_CONSTS = ("c_ident", "c_masks", "c_inv", "c_onehot", "c_relmask")


def kernel(**inputs):
    import concourse.bacc as bacc
    from concourse.bass_utils import run_bass_kernel_spmd

    nc = bacc.Bacc("TRN2", target_bir_lowering=False, num_devices=1)
    arrays, aps = {}, {}
    given = {k: np.ascontiguousarray(v) for k, v in inputs.items()}
    for name, arr in {**given, **shape_constants()}.items():
        arrays[f"in_{name}"] = arr
        aps[name] = nc.dram_tensor(f"in_{name}", arr.shape, mybir.dt.from_np(arr.dtype), kind="ExternalInput").ap()
    out = nc.dram_tensor("out", (1, N, D), F32, kind="ExternalOutput").ap()
    build(nc, aps, out)
    r = run_bass_kernel_spmd(nc, [arrays], core_ids=[0])
    return r.results[0]["out"]
```
